# Optimizing a Trainium2 kernel written in Bass

```python
import jax, jax.numpy as jnp
from jax import lax
import numpy as np

D_MODEL = 1024
BATCH = 1
SEQ = 128
DEPTH = 1
DEC_BATCH = 1
DEC_SEQ = 1024
PAST_LEN = 256

GRID_W = 64
N_RET_HEADS = 4
RET_DK = 256
RET_DV = 256
D_RET = N_RET_HEADS * RET_DV
D_QK = N_RET_HEADS * RET_DK
D_CONV = 1024
CONV_WIDTH = 31
D_FF = 2816
FFN_CONV_WIDTH = 3
CHUNK = 128
ROPE_BASE = 10000.0
EPS = 1e-6
GN_EPS = 1e-5
IN_COLS = 2 * D_QK + 2 * D_RET + 2 * D_CONV + 2 * D_MODEL

kernel_name = 'retention_conformer_convffn_dit_step'

def rms_norm(x, w):
    xf = x.astype(jnp.float32)
    y = xf * lax.rsqrt(jnp.mean(xf * xf, axis=-1, keepdims=True) + EPS)
    return (y * w.astype(jnp.float32)).astype(x.dtype)

def layer_norm(x, w, b):
    xf = x.astype(jnp.float32)
    mu = jnp.mean(xf, axis=-1, keepdims=True)
    var = jnp.mean(jnp.square(xf - mu), axis=-1, keepdims=True)
    y = (xf - mu) * lax.rsqrt(var + GN_EPS)
    return (y * w.astype(jnp.float32) + b.astype(jnp.float32)).astype(x.dtype)

def head_group_norm(o, w):
    mu = jnp.mean(o, axis=-1, keepdims=True)
    var = jnp.mean(jnp.square(o - mu), axis=-1, keepdims=True)
    y = (o - mu) * lax.rsqrt(var + GN_EPS)
    b, t = o.shape[0], o.shape[1]
    return y.reshape(b, t, D_RET) * w.astype(jnp.float32)

def depthwise_conv(x, w, bias):
    width, ch = w.shape
    y = lax.conv_general_dilated(
        x, w[:, None, :].astype(x.dtype), window_strides=(1,),
        padding=[(width // 2, width // 2)],
        dimension_numbers=('NWC', 'WIO', 'NWC'), feature_group_count=ch)
    return y + bias.astype(x.dtype)

def adaln(cond, w, b):
    return jax.nn.silu(cond.astype(jnp.float32)) @ w.astype(jnp.float32) + b.astype(jnp.float32)

def axial_rope(x, rows):
    d = x.shape[-1]
    nf = d // 4
    r = jnp.repeat(jnp.arange(rows), GRID_W).astype(jnp.float32)
    col = jnp.tile(jnp.arange(GRID_W), rows).astype(jnp.float32)
    inv = ROPE_BASE ** (-jnp.arange(nf, dtype=jnp.float32) / nf)

    def rot(xh, pos):
        ang = pos[:, None] * inv[None, :]
        cos = jnp.cos(ang)[None, :, None, :]
        sin = jnp.sin(ang)[None, :, None, :]
        x1, x2 = xh[..., :nf], xh[..., nf:]
        return jnp.concatenate([x1 * cos - x2 * sin, x2 * cos + x1 * sin], axis=-1)

    xf = x.astype(jnp.float32)
    out = jnp.concatenate([rot(xf[..., :2 * nf], r), rot(xf[..., 2 * nf:], col)], axis=-1)
    return out.astype(x.dtype)

def retention_dir(q, k, v, log_gamma, s0):
    b, t, h, dk = q.shape
    dv = v.shape[-1]
    n = t // CHUNK
    qc = q.astype(jnp.float32).reshape(b, n, CHUNK, h, dk)
    kc = k.astype(jnp.float32).reshape(b, n, CHUNK, h, dk)
    vc = v.astype(jnp.float32).reshape(b, n, CHUNK, h, dv)
    idx = jnp.arange(CHUNK, dtype=jnp.float32)
    rel = idx[:, None] - idx[None, :]
    decay_in = jnp.where(rel[None] >= 0,
                         jnp.exp(jnp.maximum(rel, 0.0)[None] * log_gamma[:, None, None]), 0.0)
    scores = jnp.einsum('bnqhd,bnkhd->bnhqk', qc, kc) * decay_in[None, None]
    inner = jnp.einsum('bnhqk,bnkhe->bnqhe', scores, vc)
    q_dec = jnp.exp((idx + 1.0)[:, None] * log_gamma[None, :])
    k_dec = jnp.exp((CHUNK - 1.0 - idx)[:, None] * log_gamma[None, :])
    chunk_dec = jnp.exp(CHUNK * log_gamma)

    def step(s, xs):
        qi, ki, vi = xs
        cross = jnp.einsum('bqhd,bhde->bqhe', qi * q_dec[None, :, :, None], s)
        s = s * chunk_dec[None, :, None, None] + jnp.einsum(
            'bkhd,bkhe->bhde', ki * k_dec[None, :, :, None], vi)
        return s, cross

    s_final, cross = lax.scan(step, s0.astype(jnp.float32),
                              (jnp.moveaxis(qc, 1, 0), jnp.moveaxis(kc, 1, 0), jnp.moveaxis(vc, 1, 0)))
    out = inner + jnp.moveaxis(cross, 0, 1)
    return out.reshape(b, t, h, dv), s_final

def bidirectional_retention(q, k, v, lg_f, lg_b, s_f0, s_b0):
    o_f, s_f = retention_dir(q, k, v, lg_f, s_f0)
    o_b, s_b = retention_dir(q[:, ::-1], k[:, ::-1], v[:, ::-1], lg_b, s_b0)
    return o_f + o_b[:, ::-1], s_f, s_b

def trunk_layer(x, mod, rows, s_f0, s_b0, n1_pre, n1_post, n2_pre, n2_post, w_in, dec_f, dec_b,
                gn_w, ret_w_out, cdw_w, cdw_b, cln_w, cln_b, conv_w_out, w_mix_out,
                ffn_w_up, fdw_w, fdw_b, ffn_w_down):
    b, t, _ = x.shape
    mod = mod.astype(x.dtype)
    sh1, sc1, g1, sh2, sc2, g2 = jnp.split(mod, 6, axis=-1)
    h = rms_norm(x, n1_pre) * (1 + sc1) + sh1
    proj = h @ w_in
    cuts = [D_QK, 2 * D_QK, 2 * D_QK + D_RET, 2 * D_QK + 2 * D_RET,
            2 * D_QK + 2 * D_RET + D_CONV, 2 * D_QK + 2 * D_RET + 2 * D_CONV,
            2 * D_QK + 2 * D_RET + 2 * D_CONV + D_MODEL]
    q, k, v, g_ret, u_a, u_b, gate_ret, gate_conv = jnp.split(proj, cuts, axis=-1)
    q = q.reshape(b, t, N_RET_HEADS, RET_DK)
    k = k.reshape(b, t, N_RET_HEADS, RET_DK)
    v = v.reshape(b, t, N_RET_HEADS, RET_DV)
    if rows is not None:
        q = axial_rope(q, rows)
        k = axial_rope(k, rows)
    q = q * (RET_DK ** -0.5)
    lg_f = jax.nn.log_sigmoid(dec_f.astype(jnp.float32))
    lg_b = jax.nn.log_sigmoid(dec_b.astype(jnp.float32))
    o, s_f, s_b = bidirectional_retention(q, k, v, lg_f, lg_b, s_f0, s_b0)
    o = head_group_norm(o, gn_w).astype(x.dtype)
    ret_out = (jax.nn.silu(g_ret) * o) @ ret_w_out
    u = u_a * jax.nn.sigmoid(u_b)
    u = depthwise_conv(u, cdw_w, cdw_b)
    u = jax.nn.silu(layer_norm(u, cln_w, cln_b))
    conv_out = u @ conv_w_out
    mixed = jax.nn.sigmoid(gate_ret) * ret_out + jax.nn.sigmoid(gate_conv) * conv_out
    x = x + g1 * rms_norm(mixed @ w_mix_out, n1_post)
    h2 = rms_norm(x, n2_pre) * (1 + sc2) + sh2
    up = depthwise_conv(h2 @ ffn_w_up, fdw_w, fdw_b)
    a, gl = jnp.split(up, 2, axis=-1)
    x = x + g2 * rms_norm((jax.nn.silu(a) * gl) @ ffn_w_down, n2_post)
    return x, s_f, s_b

def setup_inputs(seed: int = 0) -> dict:
    key = jax.random.key(seed)
    ks = jax.random.split(key, 32)

    def nrm(k, shape, scale):
        return jax.random.normal(k, shape, jnp.float32) * scale

    gamma = 1.0 - 2.0 ** (-5.0 - np.arange(N_RET_HEADS))
    base_logit = jnp.asarray(np.log(gamma) - np.log1p(-gamma), dtype=jnp.float32)
    st_shape = (DEC_BATCH, DEPTH, N_RET_HEADS, RET_DK, RET_DV)
    return {
        'x_prompt': nrm(ks[0], (BATCH, SEQ, D_MODEL), 1.0),
        'x_sample': nrm(ks[1], (DEC_BATCH, DEC_SEQ, D_MODEL), 1.0),
        'state_ret_fwd': nrm(ks[2], st_shape, 0.5),
        'state_ret_bwd': nrm(ks[3], st_shape, 0.5),
        'c': nrm(ks[4], (DEC_BATCH, D_MODEL), 1.0),
        'c_ctx': nrm(ks[5], (D_MODEL,), 1.0),
        'norm1_pre': 1.0 + nrm(ks[6], (DEPTH, D_MODEL), 0.1),
        'norm1_post': 1.0 + nrm(ks[7], (DEPTH, D_MODEL), 0.1),
        'norm2_pre': 1.0 + nrm(ks[8], (DEPTH, D_MODEL), 0.1),
        'norm2_post': 1.0 + nrm(ks[9], (DEPTH, D_MODEL), 0.1),
        'ada_w': nrm(ks[10], (DEPTH, D_MODEL, 6 * D_MODEL), D_MODEL ** -0.5),
        'ada_b': nrm(ks[11], (DEPTH, 6 * D_MODEL), 0.02),
        'w_in': nrm(ks[12], (DEPTH, D_MODEL, IN_COLS), D_MODEL ** -0.5),
        'ret_decay_fwd': base_logit[None] + nrm(ks[13], (DEPTH, N_RET_HEADS), 0.1),
        'ret_decay_bwd': base_logit[None] + nrm(ks[14], (DEPTH, N_RET_HEADS), 0.1),
        'ret_gn_w': 1.0 + nrm(ks[15], (DEPTH, D_RET), 0.1),
        'ret_w_out': nrm(ks[16], (DEPTH, D_RET, D_MODEL), D_RET ** -0.5),
        'conv_dw_w': nrm(ks[17], (DEPTH, CONV_WIDTH, D_CONV), CONV_WIDTH ** -0.5),
        'conv_dw_b': nrm(ks[18], (DEPTH, D_CONV), 0.02),
        'conv_ln_w': 1.0 + nrm(ks[19], (DEPTH, D_CONV), 0.1),
        'conv_ln_b': nrm(ks[20], (DEPTH, D_CONV), 0.02),
        'conv_w_out': nrm(ks[21], (DEPTH, D_CONV, D_MODEL), D_CONV ** -0.5),
        'w_mix_out': nrm(ks[22], (DEPTH, D_MODEL, D_MODEL), D_MODEL ** -0.5),
        'ffn_w_up': nrm(ks[23], (DEPTH, D_MODEL, 2 * D_FF), D_MODEL ** -0.5),
        'ffn_dw_w': nrm(ks[24], (DEPTH, FFN_CONV_WIDTH, 2 * D_FF), FFN_CONV_WIDTH ** -0.5),
        'ffn_dw_b': nrm(ks[25], (DEPTH, 2 * D_FF), 0.02),
        'ffn_w_down': nrm(ks[26], (DEPTH, D_FF, D_MODEL), D_FF ** -0.5),
    }

def reference(x_prompt, x_sample, state_ret_fwd, state_ret_bwd, c, c_ctx,
              norm1_pre, norm1_post, norm2_pre, norm2_post, ada_w, ada_b, w_in,
              ret_decay_fwd, ret_decay_bwd, ret_gn_w, ret_w_out,
              conv_dw_w, conv_dw_b, conv_ln_w, conv_ln_b, conv_w_out, w_mix_out,
              ffn_w_up, ffn_dw_w, ffn_dw_b, ffn_w_down):
    rows = x_sample.shape[1] // GRID_W
    xp, xs = x_prompt, x_sample
    zero_state = jnp.zeros((x_prompt.shape[0], N_RET_HEADS, RET_DK, RET_DV), jnp.float32)
    new_f, new_b = [], []
    for l in range(DEPTH):
        lw = (norm1_pre[l], norm1_post[l], norm2_pre[l], norm2_post[l], w_in[l],
              ret_decay_fwd[l], ret_decay_bwd[l], ret_gn_w[l], ret_w_out[l],
              conv_dw_w[l], conv_dw_b[l], conv_ln_w[l], conv_ln_b[l], conv_w_out[l],
              w_mix_out[l], ffn_w_up[l], ffn_dw_w[l], ffn_dw_b[l], ffn_w_down[l])
        mod_ctx = adaln(c_ctx[None], ada_w[l], ada_b[l])[:, None, :]
        mod_lat = adaln(c, ada_w[l], ada_b[l])[:, None, :]
        xp, s_f, s_b = trunk_layer(xp, mod_ctx, None, zero_state, zero_state, *lw)
        new_f.append(s_f)
        new_b.append(s_b)
        xs, _, _ = trunk_layer(xs, mod_lat, rows, state_ret_fwd[:, l], state_ret_bwd[:, l], *lw)
    new_state_ret_fwd = jnp.stack(new_f, axis=1).astype(x_prompt.dtype)
    new_state_ret_bwd = jnp.stack(new_b, axis=1).astype(x_prompt.dtype)
    return (xp, xs, new_state_ret_fwd, new_state_ret_bwd)


_drawn_inputs = setup_inputs


def setup_inputs(seed=0):
    import zlib

    import numpy as np

    out = dict(_drawn_inputs(seed))
    spreads = {}
    factors = {'state_ret_fwd': 27.526,
     'state_ret_bwd': 31.468,
     'conv_dw_b': 6.225,
     'conv_ln_b': 8.0,
     'ffn_dw_b': 5.188}
    for name, (base, spread) in spreads.items():
        noise = np.random.default_rng([zlib.crc32(name.encode()), seed]).standard_normal(out[name].shape)
        drawn = base * np.exp(spread * noise) if base else spread * noise
        out[name] = __import__('jax').numpy.asarray(drawn.astype(out[name].dtype))
    for name, factor in factors.items():
        out[name] = (out[name] * factor).astype(out[name].dtype)
    return out
```

```python
from contextlib import ExitStack

import numpy as np
import concourse.bass as bass
from concourse import mybir

P = 128
D = 1024
KT = D // P
LAT, CTX = 1024, 128
T = LAT + CTX
NT = T // P
NL = LAT // P
TG = 384
NTG = T // TG
HEADS, DK, DV = 4, 256, 256
CW = 31
HALO = CW // 2
FF = 2816
FKT = FF // P
EPS, GN_EPS = 1e-6, 1e-5
GRID_W = 64
CHW = 1024
U_OUT = LAT + HALO + CTX
U_IN = U_OUT + 2 * HALO
F_OUT = LAT + 1 + CTX
F_IN = F_OUT + 2
NPOS = 4

F32, F32R = mybir.dt.float32, mybir.dt.float32r
ALU = mybir.AluOpType
ACT = mybir.ActivationFunctionType
AX = mybir.AxisListType

V_C, V_CC, V_N1PRE, V_N2PRE, V_LNW, V_LNB, V_CDB, V_N1POST, V_N2POST, V_ADAB = 0, 8, 16, 24, 32, 40, 48, 56, 64, 72
SH1, SC1, G1, SH2, SC2, G2 = range(6)


def shape_tables():
    nf = DK // 4
    inv = (10000.0 ** (-np.arange(nf, dtype=np.float32) / nf)).astype(np.float32)
    tok = np.arange(LAT)
    rope = np.zeros((NL, P, 2, 2, 2, nf), np.float32)
    for half, pos in enumerate((tok // GRID_W, tok % GRID_W)):
        ang = (pos[:, None].astype(np.float32) * inv[None, :]).astype(np.float32)
        c, s = np.cos(ang).reshape(NL, P, nf), np.sin(ang).reshape(NL, P, nf)
        rope[:, :, 0, half, 0], rope[:, :, 0, half, 1] = c, c
        rope[:, :, 1, half, 0], rope[:, :, 1, half, 1] = -s, s
    i = np.arange(P, dtype=np.float32)
    pos = np.stack([i + 1, P - i, P - 1 - i, i], 1)
    rel = i[None, :] - i[:, None]
    scale = DK ** -0.5
    dist = np.stack([np.maximum(rel, 0), np.maximum(-rel, 0), (rel >= 0) * scale, (rel <= 0) * scale], 1)
    table = np.concatenate([pos, dist.reshape(P, 4 * P)], 1).astype(np.float32)
    return rope.reshape(NL, P, 4 * P), np.ascontiguousarray(table)


def build(nc, a, out_xp, out_xs, out_sf, out_sb):
    ctx = ExitStack()
    uniq = [0]

    def sb(name, shape, dt=F32, stack=None):
        return (stack or ctx).enter_context(nc.sbuf_tensor(name, shape, dt))

    def sem(name):
        return ctx.enter_context(nc.semaphore(name))

    with ctx:
        conv_d = nc.dram_tensor("conv_d", [KT, P, T], F32, kind="Internal").ap()
        gate_d = nc.dram_tensor("gate_d", [2, KT, P, T], F32, kind="Internal").ap()
        qkvg_d = nc.dram_tensor("qkvg_d", [HEADS, NT, P, 1024], F32, kind="Internal").ap()
        rT_d = nc.dram_tensor("rT_d", [KT, P, T], F32, kind="Internal").ap()
        x2_d = nc.dram_tensor("x2_d", [NT, P, D], F32, kind="Internal").ap()
        h2T_d = nc.dram_tensor("h2T_d", [KT, P, T], F32, kind="Internal").ap()
        gain_d = nc.dram_tensor("gain_d", [32, P], F32, kind="Internal").ap()

        W_hi = sb("W_hi", [P, 6, CHW], F32R)
        W_lo = sb("W_lo", [P, 6, CHW], F32R)
        W_raw = sb("W_raw", [P, 3, CHW])
        V0 = sb("V0", [P, P])
        VF = sb("VF", [P, 4 * FKT * 2])
        mod = sb("mod", [P, 48, 2])
        ident = sb("ident", [P, P])
        mean_w = sb("mean_w", [P, P])

        s_L = ExitStack()
        A_hi = sb("A_hi", [P, KT, T], F32R, s_L)
        A_lo = sb("A_lo", [P, KT, T], F32R, s_L)
        W2_hi = sb("W2_hi", [P, 2, CHW], F32R, s_L)
        W2_lo = sb("W2_lo", [P, 2, CHW], F32R, s_L)
        W2_raw = sb("W2_raw", [P, 1, CHW], F32, s_L)
        VC = sb("VC", [P, CW * KT], F32, s_L)
        s_PU = ExitStack()
        ada_w = sb("ada_w", [P, 2, KT, P], F32, s_PU)
        cs = sb("cs", [P, KT, 2], F32, s_PU)
        s_P = ExitStack()
        x_all = sb("x_all", [P, NT, D], F32, s_P)
        rows = sb("rows", [P, 5, P], F32, s_P)
        hf = sb("hf", [P, T], F32, s_P)
        ssq = sb("ssq", [P, NT], F32, s_P)
        rst = sb("rst", [P, NT], F32, s_P)
        hscale = sb("hscale", [P, KT, 2], F32, s_P)
        s_P.close()
        s_U = ExitStack()
        u_in = sb("u_in", [P, 2, U_IN], F32, s_U)
        sig = sb("sig", [P, T], F32, s_U)
        u_a = sb("u_a", [P, T], F32, s_U)
        gates = sb("gates", [P, 2, T], F32, s_U)
        conv_y = sb("conv_y", [P, 2, U_OUT], F32, s_U)
        s_U.close()
        s_PU.close()
        s_Q = ExitStack()
        rope = sb("rope", [P, NL, 2, 256], F32, s_Q)
        gn_row = sb("gn_row", [P, D], F32, s_Q)
        gn_head = sb("gn_head", [P, 256], F32, s_Q)
        qk_st = sb("qk_st", [P, 3, 512], F32, s_Q)
        vg_st = sb("vg_st", [P, 3, 512], F32, s_Q)
        rope_c = sb("rope_c", [P, 512], F32, s_Q)
        rope_s = sb("rope_s", [P, 512], F32, s_Q)
        gm1 = sb("gm1", [P, 32], F32, s_Q)
        gmr = sb("gmr", [32, P], F32, s_Q)
        s_Q.close()
        s_L.close()
        s_R = ExitStack()
        qkvg = sb("qkvg", [P, NT, 4, 256], F32, s_R)
        S = sb("S", [P, NL, 2, 512], F32, s_R)
        k_hi = sb("k_hi", [P, 2, 256], F32R, s_R)
        k_lo = sb("k_lo", [P, 2, 256], F32R, s_R)
        vs = sb("vs", [P, 2, 512], F32, s_R)
        vs_hi = sb("vs_hi", [P, 2, 512], F32R, s_R)
        vs_lo = sb("vs_lo", [P, 2, 512], F32R, s_R)
        st_out = sb("st_out", [P, 2, 2, 256], F32, s_R)
        T_hi = sb("T_hi", [P, 2, 512], F32R, s_R)
        T_lo = sb("T_lo", [P, 2, 512], F32R, s_R)
        S_hi = sb("S_hi", [P, 2, 1024], F32R, s_R)
        S_lo = sb("S_lo", [P, 2, 1024], F32R, s_R)
        v_hi = sb("v_hi", [P, 2, 256], F32R, s_R)
        v_lo = sb("v_lo", [P, 2, 256], F32R, s_R)
        sm = sb("sm", [P, 2, P], F32, s_R)
        sm_hi = sb("sm_hi", [P, 2, P], F32R, s_R)
        sm_lo = sb("sm_lo", [P, 2, P], F32R, s_R)
        o_a = sb("o_a", [P, 2, 256], F32, s_R)
        o_b = sb("o_b", [P, 2, 256], F32, s_R)
        o_o = sb("o_o", [P, 2, 256], F32, s_R)
        o_y = sb("o_y", [P, 2, 256], F32, s_R)
        o_r = sb("o_r", [P, 2, 256], F32, s_R)
        bn6 = sb("bn6", [P, 2, 6], F32, s_R)
        bn2 = sb("bn2", [P, 2, 2], F32, s_R)
        gstd = sb("gstd", [P, 2, 4], F32, s_R)
        rT_st = sb("rT_st", [P, 2, 2, P], F32, s_R)
        tab = sb("tab", [P, NPOS + 4 * P], F32, s_R)
        dec = sb("dec", [P, 2 * HEADS], F32, s_R)
        lg = sb("lg", [P, 2 * HEADS], F32, s_R)
        lgt = sb("lgt", [P, 6, 2 * HEADS], F32, s_R)
        dk_a = sb("dk_a", [P, HEADS, 6], F32, s_R)
        dk_c = sb("dk_c", [P, HEADS, 6], F32, s_R)
        hd = sb("hd", [P, 8], F32, s_R)
        dkt = sb("dkt", [P, HEADS, 8], F32, s_R)
        mask = sb("mask", [P, P], F32, s_R)
        mtmp = sb("mtmp", [P, 4, P], F32, s_R)
        s_R.close()
        s_M = ExitStack()
        r_hi = sb("r_hi", [P, KT, TG], F32R, s_M)
        r_lo = sb("r_lo", [P, KT, TG], F32R, s_M)
        c_hi = sb("c_hi", [P, KT, TG], F32R, s_M)
        c_lo = sb("c_lo", [P, KT, TG], F32R, s_M)
        m_hi = sb("m_hi", [P, KT, TG], F32R, s_M)
        m_lo = sb("m_lo", [P, KT, TG], F32R, s_M)
        rc_st = sb("rc_st", [P, KT, TG], F32, s_M)
        m_part = sb("m_part", [P, KT, TG], F32, s_M)
        gate_t = sb("gate_t", [P, 4, TG], F32, s_M)
        ln_a = sb("ln_a", [P, TG], F32, s_M)
        ln_sq = sb("ln_sq", [P, 2, TG], F32, s_M)
        ln_acc = sb("ln_acc", [P, TG], F32, s_M)
        g1_row = sb("g1_row", [P, 2, D], F32, s_M)
        mo = sb("mo", [P, 3, D], F32, s_M)
        h2o = sb("h2o", [P, KT, P], F32, s_M)
        xt = sb("xt", [P, 2, D], F32, s_M)
        sq_junk = sb("sq_junk", [P, D], F32, s_M)
        mst = sb("mst", [P, 2, 8], F32, s_M)
        h2s = sb("h2s", [P, KT, 2], F32, s_M)
        s_M.close()
        s_F = ExitStack()
        B_hi = sb("B_hi", [P, KT, T], F32R, s_F)
        B_lo = sb("B_lo", [P, KT, T], F32R, s_F)
        y_acc = sb("y_acc", [P, NT, D], F32, s_F)
        f_in = sb("f_in", [P, 2, F_IN], F32, s_F)
        f_cv = sb("f_cv", [P, 2, F_OUT], F32, s_F)
        g_hi = sb("g_hi", [P, 2, T], F32R, s_F)
        g_lo = sb("g_lo", [P, 2, T], F32R, s_F)
        s_F.close()
        s_E = ExitStack()
        x2t = sb("x2t", [P, NT, D], F32, s_E)
        g2_row = sb("g2_row", [P, 2, D], F32, s_E)
        ej = sb("ej", [P, D], F32, s_E)
        est = sb("est", [P, NT, 4], F32, s_E)
        s_E.close()

        ps = ctx.enter_context(nc.psum_tensor("ps", [P, 8, 512], F32))

        def wslot(n, ring):
            s = n % ring
            return (W_hi[:, s, :], W_lo[:, s, :]) if s < 6 else (W2_hi[:, s - 6, :], W2_lo[:, s - 6, :])

        def wraw(n, ring):
            s = n % ring
            return W_raw[:, s, :] if s < 3 else W2_raw[:, 0, :]

        w_in = a["w_in"][0]
        ada = a["ada_w"][0].rearrange("(k p) n -> p k n", p=P)
        w_in_p = w_in.rearrange("(k p) n -> p k n", p=P)
        w_in_s = w_in.rearrange("(k p) (s c) -> p k s c", p=P, s=8)
        Fv = lambda x: x.bitcast(F32)

        class Semaphores:
            pass
        q = Semaphores()
        q.gnh_ok = sem("gnh_ok")
        q.kv_hi = sem("kv_hi")
        q.kv_lo = sem("kv_lo")
        q.Tv_hi = sem("Tv_hi")
        q.mem_free = sem("mem_free")
        q.dve_own = sem("dve_own")
        q.w_hi = sem("w_hi")
        q.w_lo = sem("w_lo")
        q.vec_in = sem("vec_in")
        q.vecT = sem("vecT")
        q.vec_ok = sem("vec_ok")
        q.x_in0 = sem("x_in0")
        q.ident_ok = sem("ident_ok")
        q.cs_ok = sem("cs_ok")
        q.ada_in0 = sem("ada_in0")
        q.ada_in1 = sem("ada_in1")
        q.ada_used = sem("ada_used")
        q.mod_ok = sem("mod_ok")
        q.ssq_ok = sem("ssq_ok")
        q.rstd_a = sem("rstd_a")
        q.rstd_b = sem("rstd_b")
        q.xn_ok = sem("xn_ok")
        q.hT_ps = sem("hT_ps")
        q.hT_f = sem("hT_f")
        q.hT_lo = sem("hT_lo")
        q.u_ps = sem("u_ps")
        q.u_evac = sem("u_evac")
        q.u_ok = sem("u_ok")
        q.pads_ok = sem("pads_ok")
        q.conv_step = sem("conv_step")
        q.conv_st0 = sem("conv_st0")
        q.conv_st1 = sem("conv_st1")
        q.gate_st0 = sem("gate_st0")
        q.gate_st1 = sem("gate_st1")
        q.adaU_ok = sem("adaU_ok")
        q.q_ps = sem("q_ps")
        q.qk_evac = sem("qk_evac")
        q.vg_evac = sem("vg_evac")
        q.rope_in = sem("rope_in")
        q.rope_ok = sem("rope_ok")
        q.qk_st0 = sem("qk_st0")
        q.qk_st1 = sem("qk_st1")
        q.qk_st2 = sem("qk_st2")
        q.vg_ok = sem("vg_ok")
        q.vg_st0 = sem("vg_st0")
        q.vg_st1 = sem("vg_st1")
        q.vg_st2 = sem("vg_st2")
        q.gain_t = sem("gain_t")
        q.gain_c = sem("gain_c")
        q.gain_st = sem("gain_st")
        q.tab_in = sem("tab_in")
        q.dk_arg = sem("dk_arg")
        q.dk_exp = sem("dk_exp")
        q.hd_ok = sem("hd_ok")
        q.mexp = sem("mexp")
        q.mask_ok = sem("mask_ok")
        q.s0_in = sem("s0_in")
        q.vs_ok = sem("vs_ok")
        q.P_ps = sem("P_ps")
        q.P_evac = sem("P_evac")
        q.st_f_st = sem("st_f_st")
        q.Sscan = sem("Sscan")
        q.T_ps = sem("T_ps")
        q.T_lo_ok = sem("T_lo_ok")
        q.S_hi_ok = sem("S_hi_ok")
        q.S_lo_ok = sem("S_lo_ok")
        q.v_lo_ok = sem("v_lo_ok")
        q.sc_ps = sem("sc_ps")
        q.sm_ok = sem("sm_ok")
        q.sm_hi_ok = sem("sm_hi_ok")
        q.sm_lo_ok = sem("sm_lo_ok")
        q.in_ps = sem("in_ps")
        q.cr_ps = sem("cr_ps")
        q.oa_ok = sem("oa_ok")
        q.ob_ok = sem("ob_ok")
        q.o_ok = sem("o_ok")
        q.gn_s = sem("gn_s")
        q.gn_v = sem("gn_v")
        q.gn_q = sem("gn_q")
        q.gn_r = sem("gn_r")
        q.y_ok = sem("y_ok")
        q.r_ok = sem("r_ok")
        q.rT_ps = sem("rT_ps")
        q.rT_ok = sem("rT_ok")
        q.rT_s0 = sem("rT_s0")
        q.rT_s1 = sem("rT_s1")
        q.g1_in = sem("g1_in")
        q.rc_in = sem("rc_in")
        q.r_hi_ok = sem("r_hi_ok")
        q.r_lo_ok = sem("r_lo_ok")
        q.ln_s = sem("ln_s")
        q.ln_mp = sem("ln_mp")
        q.ln_d = sem("ln_d")
        q.ln_sqk = sem("ln_sqk")
        q.ln_acck = sem("ln_acck")
        q.ln_vp = sem("ln_vp")
        q.ln_v = sem("ln_v")
        q.ln_r1 = sem("ln_r1")
        q.ln_z = sem("ln_z")
        q.ln_silu = sem("ln_silu")
        q.c_hi_ok = sem("c_hi_ok")
        q.c_lo_ok = sem("c_lo_ok")
        q.gt_in0 = sem("gt_in0")
        q.gt_in1 = sem("gt_in1")
        q.mr_ps = sem("mr_ps")
        q.mr_evac = sem("mr_evac")
        q.m_hi_ok = sem("m_hi_ok")
        q.m_lo_ok = sem("m_lo_ok")
        q.mo_ps = sem("mo_ps")
        q.mo_ok = sem("mo_ok")
        q.mst_s = sem("mst_s")
        q.mst_v = sem("mst_v")
        q.mst_q = sem("mst_q")
        q.x2_ok = sem("x2_ok")
        q.xn2_ok = sem("xn2_ok")
        q.h2_ps = sem("h2_ps")
        q.h2_f = sem("h2_f")
        q.h2_st = sem("h2_st")
        q.h2s_ok = sem("h2s_ok")
        q.B_hi_ok = sem("B_hi_ok")
        q.B_lo_ok = sem("B_lo_ok")
        q.fpad = sem("fpad")
        q.fa_ps = sem("fa_ps")
        q.fg_ps = sem("fg_ps")
        q.fa_ev = sem("fa_ev")
        q.fg_ev = sem("fg_ev")
        q.fa_c0 = sem("fa_c0")
        q.fg_c0 = sem("fg_c0")
        q.fa_c = sem("fa_c")
        q.fg_c = sem("fg_c")
        q.fsilu = sem("fsilu")
        q.fprod = sem("fprod")
        q.gact_hi = sem("gact_hi")
        q.gact_lo = sem("gact_lo")
        q.fd_ps = sem("fd_ps")
        q.y_add = sem("y_add")
        q.x2_in = sem("x2_in")
        q.e_s = sem("e_s")
        q.e_v = sem("e_v")
        q.e_q = sem("e_q")
        q.e_o = sem("e_o")
        q.out_st = sem("out_st")
        wl_in = [sem(f"wl_in{i}") for i in range(4)]
        wr_in = [sem(f"wr_in{i}") for i in range(3)]
        tile_in = [sem(f"tile_in{i}") for i in range(3)]
        x_in = q.x_in0
        ada_in = [q.ada_in0, q.ada_in1]
        conv_st = [q.conv_st0, q.conv_st1]
        gate_st = [q.gate_st0, q.gate_st1]
        qk_st_s = [q.qk_st0, q.qk_st1, q.qk_st2]
        vg_st_s = [q.vg_st0, q.vg_st1, q.vg_st2]
        rT_s = [q.rT_s0, q.rT_s1]
        gt_in = [q.gt_in0, q.gt_in1]
        xt_in = [sem("xt_in0"), sem("xt_in1")]
        xt_st = [sem("xt_st0"), sem("xt_st1")]

        U_COLS = [(5, 0), (4, 0), (5, 1), (4, 1), (6, 0), (7, 0), (6, 1), (7, 1)]
        M_CHUNKS = 24
        N_L = 64
        N_LM = N_L + NTG * M_CHUNKS

        block = ctx.enter_context(nc.Block())

        @block.sync
        def _(sp):
            r = 0
            for name in ("c", "c_ctx", "norm1_pre", "norm2_pre", "conv_ln_w", "conv_ln_b", "conv_dw_b",
                         "norm1_post", "norm2_post", "ada_b"):
                v = a[name]
                v = (v if len(v.shape) == 1 else v[0]).rearrange("(k p) -> k p", p=P)
                n = v.shape[0]
                if name == "ada_b":
                    assert r == V_ADAB
                sp.dma_start(rows[r:r + n, 0, :], v).then_inc(q.vec_in, 16)
                r += n
            fw = a["ffn_dw_w"][0].rearrange("w (j p) -> (w j) p", p=P)
            fb = a["ffn_dw_b"][0].rearrange("(j p) -> j p", p=P)
            cw = a["conv_dw_w"][0].rearrange("w (k p) -> (w k) p", p=P)
            sp.dma_start(rows[0:88, 1, :], fw[0:88, :]).then_inc(q.vec_in, 16)
            sp.dma_start(rows[0:44, 2, :], fw[88:132, :]).then_inc(q.vec_in, 16)
            sp.dma_start(rows[44:88, 2, :], fb).then_inc(q.vec_in, 16)
            sp.dma_start(rows[0:124, 3, :], cw[0:124, :]).then_inc(q.vec_in, 16)
            sp.dma_start(rows[0:124, 4, :], cw[124:248, :]).then_inc(q.vec_in, 16)
            for m in range(2):
                sp.dma_start(ada_w[:, m, :, :], ada[:, :, m * P:(m + 1) * P]).then_inc(ada_in[m], 16)
            xs = a["x_sample"][0].rearrange("(t p) d -> p t d", p=P)
            sp.dma_start(x_all[:, 0:NL, :], xs).then_inc(x_in, 16)
            sp.dma_start(x_all[:, NL, :], a["x_prompt"][0]).then_inc(x_in, 16)
            for m in range(2, 16):
                sp.wait_ge(q.ada_used, m - 1)
                sp.dma_start(ada_w[:, m % 2, :, :], ada[:, :, m * P:(m + 1) * P]).then_inc(ada_in[m % 2], 16)

            def u_chunk(i, e):
                s, t = U_COLS[e]
                if not (isinstance(i, int) and i == 0 and e < 4):
                    sp.wait_ge(q.w_lo, i * 8 + e - 3)
                sp.dma_start(wraw(e, 4).rearrange("p (k n) -> p k n", k=KT),
                             w_in_p[:, :, bass.ds(i * 256 + (s * 1024 + t * P), P)]).then_inc(wl_in[e % 4], 16)

            for e in range(8):
                u_chunk(0, e)
            with sp.Fori(1, 4) as i:
                for e in range(8):
                    u_chunk(i, e)
            with sp.Fori(0, HEADS) as h:
                for e in range(8):
                    g, j = e // 4, e % 4
                    sp.wait_ge(q.w_lo, h * 8 + (32 + e - 3))
                    for s in range(2):
                        sp.dma_start(wraw(e, 4).rearrange("p (k s n) -> p k s n", k=2, s=2)[:, :, s, :],
                                     w_in_s[:, 2 * j:2 * j + 2, 2 * g + s, bass.ds(h * 256, 256)]).then_inc(wl_in[e % 4], 16)
            def row_of(c):
                return gain_d[c * KT:(c + 1) * KT, :].rearrange("k p -> (k p)").partition_broadcast(P)
            sp.wait_ge(q.gain_c, 1)
            sp.dma_start(gain_d, gmr[:, :]).then_inc(q.gain_st, 16)

            sp.wait_ge(q.qk_evac, NT * HEADS)
            sp.wait_ge(q.vg_evac, NT * HEADS)
            for s_ in qk_st_s + vg_st_s:
                sp.wait_ge(s_, 16 * 3 * HEADS)
            wr, wc, wx = (a[n][0].rearrange("(k p) n -> p k n", p=P) for n in ("ret_w_out", "conv_w_out", "w_mix_out"))
            def m_chunk(n):
                if n == 0:
                    sp.wait_ge(q.w_lo, 64)
                if n >= 3:
                    sp.wait_ge(q.w_lo, N_L + n - 2)
                c = n % M_CHUNKS
                dst = wraw(n, 3)
                if c < 16:
                    w, m = (wr, c) if c < 8 else (wc, c - 8)
                    sp.dma_start(dst.rearrange("p (k n) -> p k n", k=KT), w[:, :, m * P:(m + 1) * P]).then_inc(wr_in[n % 3], 16)
                else:
                    half, j = (c - 16) // 4, (c - 16) % 4
                    sp.dma_start(dst.rearrange("p (k n) -> p k n", k=2),
                                 wx[:, 2 * j:2 * j + 2, half * 512:(half + 1) * 512]).then_inc(wr_in[n % 3], 16)
            for n in range(3):
                m_chunk(n)
            sp.wait_ge(q.gain_st, 16)
            sp.dma_start(tab[:, :], a["shape_table"]).then_inc(q.tab_in, 16)
            for n, name in enumerate(("ret_decay_fwd", "ret_decay_bwd")):
                sp.dma_start(dec[:, n * HEADS:(n + 1) * HEADS], a[name].partition_broadcast(P)).then_inc(q.tab_in, 16)
            def r_loads(h, first):
                for d, (name, slot) in enumerate((("state_ret_fwd", 0), ("state_ret_bwd", NL - 1))):
                    if not first:
                        sp.wait_ge(q.S_lo_ok, h * NL)
                    st = a[name][0, 0].rearrange("h (k p) e -> h p k e", p=P)
                    src = st[0] if first else st[bass.ds(h, 1)].rearrange("o p k e -> (o p) k e")
                    sp.dma_start(S[:, slot, :, d * 256:(d + 1) * 256], src).then_inc(q.s0_in, 16)
                for t in range(0, NT, 3):
                    if not first:
                        sp.wait_ge(q.r_ok, h * NT + (t + 3 - NT))
                    src = qkvg_d[bass.ds(h, 1), t:t + 3].rearrange("o t p n -> p (o t) n")
                    sp.dma_start(qkvg[:, t:t + 3, :, :].rearrange("p t a b -> p t (a b)"), src).then_inc(tile_in[t // 3], 16)

            r_loads(0, True)
            for n in range(3, 6):
                m_chunk(n)
            with sp.Fori(1, HEADS) as h:
                r_loads(h, False)
            sp.wait_ge(q.r_ok, HEADS * NT)
            sp.wait_ge(q.rT_ok, HEADS * NT)
            sp.wait_ge(q.st_f_st, 32 * HEADS)
            for s_, n in ((rT_s[0], 5), (rT_s[1], 4)):
                sp.wait_ge(s_, 16 * n * HEADS)
            sp.sem_inc(q.mem_free, 1)
            for c in range(2):
                sp.dma_start(g1_row[:, c, :], row_of(c)).then_inc(q.g1_in, 16)
            for n in range(6, 3 * M_CHUNKS):
                m_chunk(n)

            wu = a["ffn_w_up"][0].rearrange("(k p) n -> p k n", p=P)
            wd = a["ffn_w_down"][0].rearrange("(k p) n -> p k n", p=P)
            def f_chunks(i, first=False):
                for e in range(6):
                    p, kind = e // 3, e % 3
                    if first and e == 3:
                        sp.wait_ge(q.h2_st, 16 * NT)
                        for s_, n in ((xt_st[0], 5), (xt_st[1], 4)):
                            sp.wait_ge(s_, 16 * n)
                        sp.sem_inc(q.mem_free, 1)
                    if first and e < 3:
                        sp.wait_ge(q.w_lo, N_L + 3 * M_CHUNKS)
                    else:
                        sp.wait_ge(q.w_lo, N_LM + i * 6 + e - 2)
                    if kind < 2:
                        sp.dma_start(wraw(e, 3).rearrange("p (k n) -> p k n", k=KT),
                                     wu[:, :, bass.ds(i * 256 + (p * P + kind * FF), P)]).then_inc(wr_in[e % 3], 16)
                    else:
                        sp.dma_start(wraw(e, 3), wd[:, bass.ds(i * 2 + p, 1), :].rearrange("p o n -> p (o n)")).then_inc(wr_in[e % 3], 16)
            f_chunks(0, True)
            with sp.Fori(1, FKT // 2) as i:
                f_chunks(i)
            sp.wait_ge(q.fg_ps, FKT)
            for t in range(NT):
                sp.dma_start(x2t[:, t, :], x2_d[t]).then_inc(q.x2_in, 16)
            for c in range(2):
                sp.dma_start(g2_row[:, c, :], row_of(2 + c)).then_inc(q.x2_in, 16)
            for t in range(NT):
                sp.wait_ge(q.e_o, t + 1)
                dst = out_xs[0, t * P:(t + 1) * P, :] if t < NL else out_xp[0]
                sp.dma_start(dst, x2t[:, t, :]).then_inc(q.out_st, 16)
            sp.wait_ge(q.out_st, 16 * NT)
            sp.wait_ge(q.st_f_st, 32 * HEADS)

        @block.tensor
        def _(pe):
            def mm(out, l, r, start, stop):
                return pe.matmul(out, l, r, start=start, stop=stop)

            def fm3(out, wh, wl, ah, al, toks):
                wh, wl = (x.rearrange("p (k n) -> p k n", k=KT) for x in (wh, wl))
                for k in range(KT):
                    mm(out, wh[:, k, :], ah[:, k, toks], k == 0, False)
                    mm(out, wh[:, k, :], al[:, k, toks], False, False)
                    last = mm(out, wl[:, k, :], ah[:, k, toks], False, k == KT - 1)
                return last

            pe.wait_ge(q.ident_ok, 3)
            pe.wait_ge(q.vec_in, 16 * 15)
            pe.transpose(ps[:, 7, 0:120], rows[0:120, 0, :], ident[0:120, 0:120]).then_inc(q.vecT, 1)
            pe.transpose(ps[:, 5, 0:88], rows[0:88, 1, :], ident[0:88, 0:88]).then_inc(q.vecT, 1)
            pe.transpose(ps[:, 5, 128:216], rows[0:88, 2, :], ident[0:88, 0:88]).then_inc(q.vecT, 1)
            pe.transpose(ps[:, 4, 0:124], rows[0:124, 3, :], ident[0:124, 0:124]).then_inc(q.vecT, 1)
            pe.transpose(ps[:, 4, 128:252], rows[0:124, 4, :], ident[0:124, 0:124]).then_inc(q.vecT, 1)
            pe.wait_ge(q.cs_ok, 1)
            def ada_unit(slot, col):
                for k in range(KT):
                    last = mm(ps[:, 6, col:col + 2], ada_w[:, slot, k, :], cs[:, k, :], k == 0, k == KT - 1)
                last.then_inc(q.ada_used, 1)
                return last
            for m in range(16):
                pe.wait_ge(ada_in[m % 2], 16 * (m // 2 + 1))
                ada_unit(m % 2, 2 * m)
            for k in range(KT):
                if k == 0:
                    pe.wait_ge(q.xn_ok, NT)
                    pe.wait_ge(q.vec_ok, 5)
                if k >= 2:
                    pe.wait_ge(q.hT_f, k - 1)
                for t in range(NT):
                    last = pe.transpose(ps[:, 3 * (k % 2) + t // 4, (t % 4) * P:(t % 4 + 1) * P],
                                        x_all[:, t, k * P:(k + 1) * P], ident[:, :])
                last.then_inc(q.hT_ps, 1)

            pe.wait_ge(q.hT_f, KT)
            pe.wait_ge(q.mod_ok, 1)
            def u_step(i, e):
                wh, wl = wslot(e, 8)
                pe.wait_ge(q.w_lo, i * 8 + e + 1)
                if not (isinstance(i, int) and e < 2):
                    pe.wait_ge(q.u_evac, i * 8 + e - 1)
                for g in range(NTG):
                    if isinstance(i, int) and e == 0 and g == 0:
                        pe.wait_ge(q.hT_lo, KT)
                    last = fm3(ps[:, 3 * (e % 2) + g, 0:TG], wh, wl, A_hi, A_lo, slice(g * TG, (g + 1) * TG))
                last.then_inc(q.u_ps, 1)
                if e == 0 and not isinstance(i, int):
                    pe.wait_ge(q.adaU_ok, i)
                pe.wait_ge(ada_in[e % 2], i * 64 + (16 * (9 + e // 2)))
                ada_unit(e % 2, 2 * e)
            for e in range(8):
                u_step(0, e)
            with pe.Fori(1, 4) as i:
                for e in range(8):
                    u_step(i, e)

            pe.wait_ge(q.u_evac, 32)
            def q_step(h, first):
                for n in range(18):
                    g, t = n // 9, n % 9
                    if n < 6 and not first:
                        pe.wait_ge(q.vg_evac, h * NT + (n - 5))
                    elif 6 <= n < 15:
                        pe.wait_ge(q.qk_evac, h * NT + (n - 5))
                    elif n >= 15:
                        pe.wait_ge(q.vg_evac, h * NT + (n - 14))
                    for k in range(KT):
                        j = 4 * g + k // 2
                        wh, wl = (x.rearrange("p (k n) -> p k n", k=2)[:, k % 2, :] for x in wslot(j, 8))
                        if t == 0 and k % 2 == 0:
                            pe.wait_ge(q.w_lo, h * 8 + (32 + j + 1))
                        tok = slice(t * P, (t + 1) * P)
                        o = ps[:, n % 6, :]
                        mm(o, A_hi[:, k, tok], wh, k == 0, False)
                        mm(o, A_hi[:, k, tok], wl, False, False)
                        last = mm(o, A_lo[:, k, tok], wh, False, k == KT - 1)
                    last.then_inc(q.q_ps, 1)
            q_step(0, True)
            pe.wait_ge(q.mod_ok, 4)
            pe.transpose(ps[0:32, 7, 0:P], gm1[:, :], ident[:, :]).then_inc(q.gain_t, 1)
            with pe.Fori(1, HEADS) as h:
                q_step(h, False)

            pe.wait_ge(q.qk_evac, NT * HEADS)
            pe.wait_ge(q.vg_evac, NT * HEADS)
            def r_head(h, first):
                for c in range(NT):
                    b = 2 * (c % 2)
                    p = c % 2
                    pe.wait_ge(q.kv_lo, h * 2 * NT + (2 * c + 2))
                    if c == 0 and not first:
                        pe.wait_ge(q.rT_ok, h * NT)
                        pe.wait_ge(q.o_ok, h * NT)
                        pe.wait_ge(q.ob_ok, h * NL)
                    if not (first and c < 2):
                        pe.wait_ge(q.P_evac, h * NT + c - 1)
                    for k in range(2):
                        o = ps[:, b + k, :]
                        kh, kl = k_hi[:, p, k * P:(k + 1) * P], k_lo[:, p, k * P:(k + 1) * P]
                        mm(o, kh, vs_hi[:, p, :], True, False)
                        mm(o, kh, vs_lo[:, p, :], False, False)
                        last = mm(o, kl, vs_hi[:, p, :], False, True)
                    last.then_inc(q.P_ps, 1)

                def turn(c):
                    if c % 3 == 0:
                        pe.wait_ge(tile_in[c // 3], h * 16 + 16)
                    if not (first and c < 2):
                        pe.wait_ge(q.T_lo_ok, h * NT + c - 1)
                    for n in range(4):
                        last = pe.transpose(ps[:, 4 + c % 2, n * P:(n + 1) * P],
                                            qkvg[:, c, n // 2, (n % 2) * P:(n % 2 + 1) * P], ident[:, :])
                    last.then_inc(q.T_ps, 1)

                def back(c):
                    pe.wait_ge(q.r_ok, h * NT + c + 1)
                    if not (first and c == 0):
                        pe.wait_ge(q.rT_ok, h * NT + c)
                    for k in range(2):
                        last = pe.transpose(ps[:, 2, k * P:(k + 1) * P], o_r[:, c % 2, k * P:(k + 1) * P], ident[:, :])
                    last.then_inc(q.rT_ps, 1)

                turn(0)
                for c in range(NT):
                    p = c % 2
                    qT = [[x[:, p, k * P:(k + 1) * P] for k in range(2)] for x in (T_hi, T_lo)]
                    kT = [[x[:, p, (2 + k) * P:(3 + k) * P] for k in range(2)] for x in (T_hi, T_lo)]
                    pe.wait_ge(q.T_lo_ok, h * NT + c + 1)
                    if not (first and c == 0):
                        pe.wait_ge(q.sm_ok, h * NT + c)
                    for k in range(2):
                        o = ps[:, 6, 0:P]
                        mm(o, kT[0][k], qT[0][k], k == 0, False)
                        mm(o, kT[0][k], qT[1][k], False, False)
                        last = mm(o, kT[1][k], qT[0][k], False, k == 1)
                    last.then_inc(q.sc_ps, 1)
                    if c + 1 < NT:
                        turn(c + 1)
                    if c < NL:
                        pe.wait_ge(q.S_lo_ok, h * NL + c + 1)
                        if c >= 2:
                            pe.wait_ge(q.ob_ok, h * NL + c - 1)
                        elif c == 0:
                            pe.wait_ge(q.P_evac, h * NT + NT)
                        for k in range(2):
                            o = ps[:, c % 2, :]
                            sh, sl = S_hi[:, p, k * 512:(k + 1) * 512], S_lo[:, p, k * 512:(k + 1) * 512]
                            mm(o, qT[0][k], sh, k == 0, False)
                            mm(o, qT[0][k], sl, False, False)
                            last = mm(o, qT[1][k], sh, False, k == 1)
                        last.then_inc(q.cr_ps, 1)
                    if c >= 2:
                        back(c - 2)
                    pe.wait_ge(q.sm_lo_ok, h * NT + c + 1)
                    pe.wait_ge(q.v_lo_ok, h * NT + c + 1)
                    if c >= 2:
                        pe.wait_ge(q.o_ok, h * NT + c - 1)
                    o = ps[:, 7 if p else 3, 0:256]
                    mm(o, sm_hi[:, p, :], v_hi[:, p, :], True, False)
                    mm(o, sm_hi[:, p, :], v_lo[:, p, :], False, False)
                    mm(o, sm_lo[:, p, :], v_hi[:, p, :], False, True).then_inc(q.in_ps, 1)
                back(NT - 2)
                back(NT - 1)
            r_head(0, True)
            with pe.Fori(1, HEADS) as h:
                r_head(h, False)

            pe.wait_ge(q.rT_ok, HEADS * NT)
            pe.wait_ge(q.o_ok, HEADS * NT)
            def tile(g, which, m):
                hi, lo = ((r_hi, r_lo), (c_hi, c_lo))[which]
                n = g * M_CHUNKS + which * 8 + m
                e = g * 16 + which * 8 + m
                pe.wait_ge(q.w_lo, N_L + n + 1)
                if e >= 2:
                    pe.wait_ge(q.mr_evac, e - 1)
                wh, wl = wslot(n, 6)
                fm3(ps[:, e % 2, 0:TG], wh, wl, hi, lo, slice(0, TG)).then_inc(q.mr_ps, 1)
            def ln_mean(g):
                pe.wait_ge(q.ln_s, g + 1)
                if g:
                    pe.wait_ge(q.ln_v, g)
                if g > 1:
                    pe.wait_ge(q.h2_f, 6 * (g - 1))
                mm(ps[:, 6, 0:TG], mean_w[:, :], ln_a[:, :], True, True).then_inc(q.ln_mp, 1)
            def ln_var(g):
                pe.wait_ge(q.ln_acck, KT * (g + 1))
                pe.wait_ge(q.ln_d, g + 1)
                if g:
                    pe.wait_ge(q.h2_f, 6 * (g - 1) + 4)
                mm(ps[:, 6, 0:TG], mean_w[:, :], ln_acc[:, :], True, True).then_inc(q.ln_vp, 1)
            def h2_turns(g, t):
                n = 3 * g + t
                for half in range(2):
                    pe.wait_ge(q.xn2_ok, n + 1)
                    if n:
                        pe.wait_ge(q.h2_f, 2 * n)
                    for k in range(4):
                        kk = 4 * half + k
                        last = pe.transpose(ps[:, 7 - half, k * P:(k + 1) * P], mo[:, t, kk * P:(kk + 1) * P], ident[:, :])
                    last.then_inc(q.h2_ps, 1)
            for g in range(NTG):
                pe.wait_ge(q.r_lo_ok, KT * (g + 1))
                for m in range(KT):
                    tile(g, 0, m)
                    if m == 0:
                        ln_mean(g)
                    if m == 3:
                        ln_var(g)
                    if g and m in (1, 2, 5):
                        pe.wait_ge(q.ln_d if m < 5 else q.ln_v, g + 1)
                        h2_turns(g - 1, (1, 2, 5).index(m))
                pe.wait_ge(q.c_lo_ok, KT * (g + 1))
                for m in range(KT):
                    tile(g, 1, m)
                for half in range(2):
                    for t in range(3):
                        n = 6 * g + 3 * half + t
                        if n >= 4:
                            pe.wait_ge(q.mo_ok, n - 3)
                        o = ps[:, 2 + n % 4, :]
                        for k in range(KT):
                            cn = g * M_CHUNKS + 16 + half * 4 + k // 2
                            if t == 0:
                                pe.wait_ge(q.w_lo, N_L + cn + 1)
                            if half == 0 and t == 0:
                                pe.wait_ge(q.m_lo_ok, KT * g + k + 1)
                            wh, wl = (x.rearrange("p (k n) -> p k n", k=2)[:, k % 2, :] for x in wslot(cn, 6))
                            tok = slice(t * P, (t + 1) * P)
                            mm(o, m_hi[:, k, tok], wh, k == 0, False)
                            mm(o, m_hi[:, k, tok], wl, False, False)
                            last = mm(o, m_lo[:, k, tok], wh, False, k == KT - 1)
                        last.then_inc(q.mo_ps, 1)
            pe.wait_ge(q.ln_v, NTG)
            for t in range(3):
                h2_turns(NTG - 1, t)

            pe.wait_ge(q.h2_f, 2 * NT)
            pe.wait_ge(q.mo_ok, 6 * NTG)
            def up(i, p, first=False):
                for kind in range(2):
                    e = 3 * p + kind
                    pe.wait_ge(q.w_lo, N_LM + i * 6 + e + 1)
                    if not first:
                        pe.wait_ge((q.fa_ev, q.fg_ev)[kind], i * 2 + p)
                    wh, wl = wslot(e, 6)
                    for g in range(NTG):
                        if first and kind == 0 and g == 0:
                            pe.wait_ge(q.B_lo_ok, KT)
                        last = fm3(ps[:, 3 * kind + g, 0:TG], wh, wl, B_hi, B_lo, slice(g * TG, (g + 1) * TG))
                    last.then_inc((q.fa_ps, q.fg_ps)[kind], 1)
            def down(i, p, first=False):
                e = 3 * p + 2
                wh, wl = wslot(e, 6)
                pe.wait_ge(q.w_lo, N_LM + i * 6 + e + 1)
                pe.wait_ge(q.gact_lo, i * 2 + p + 1)
                for n in range(2 * NT):
                    t, half = n // 2, n % 2
                    if not (first and n < 2):
                        pe.wait_ge(q.y_add, i * 4 * NT + (p * 2 * NT + n - 1))
                    o = ps[:, 6 + half, :]
                    tok, col = slice(t * P, (t + 1) * P), slice(half * 512, (half + 1) * 512)
                    mm(o, g_hi[:, p, tok], wh[:, col], True, False)
                    mm(o, g_hi[:, p, tok], wl[:, col], False, False)
                    last = mm(o, g_lo[:, p, tok], wh[:, col], False, True)
                    last.then_inc(q.fd_ps, 1)
            up(0, 0, True)
            up(0, 1)
            down(0, 0, True)
            with pe.Fori(1, FKT // 2) as i:
                up(i, 0)
                down(i - 1, 1)
                up(i, 1)
                down(i, 0)
            down(FKT // 2 - 1, 1)

        @block.scalar
        def _(act):
            def copy(dst, src):
                return act.activation(dst, src, ACT.Copy)

            act.wait_ge(q.vec_ok, 1)
            act.activation(cs[:, :, :].rearrange("p k c -> p c k"),
                           V0[:, 0:16].rearrange("p (c k) -> p c k", c=2), ACT.Silu).then_inc(q.cs_ok, 1)
            for t in range(NT):
                act.wait_ge(x_in, 32)
                if t:
                    act.wait_ge(q.ssq_ok, t)
                act.activation(hf[:, 0:D], x_all[:, t, :], ACT.Square, accum_out=ssq[:, t:t + 1]).then_inc(q.ssq_ok, 1)
            act.wait_ge(q.rstd_a, 1)
            act.activation(ssq[:, :], rst[:, :], ACT.Sqrt).then_inc(q.rstd_b, 1)
            act.wait_ge(q.mod_ok, 2)
            for k in range(KT):
                act.wait_ge(q.hT_ps, k + 1)
                if k:
                    act.wait_ge(q.hT_lo, k)
                b = 3 * (k % 2)
                act.activation(hf[:, 0:LAT].rearrange("p (b n) -> p b n", b=2), ps[:, b:b + 2, :], ACT.Identity,
                               bias=mod[:, SH1 * KT + k, 0:1], scale=hscale[:, k, 0:1])
                act.activation(hf[:, LAT:T], ps[:, b + 2, 0:P], ACT.Identity,
                               bias=mod[:, SH1 * KT + k, 1:2], scale=hscale[:, k, 1:2]).then_inc(q.hT_f, 1)

            def split_w(n, per, used=None):
                act.wait_ge(wl_in[n % 4], per)
                if used is not None:
                    act.wait_ge(*used)
                copy(wslot(n, 8)[0], wraw(n, 4)).then_inc(q.w_hi, 1)

            for n in range(4):
                split_w(n, 16)

            def ada_load(i, e):
                act.wait_ge(q.ada_used, i * 8 + e + 15)
                act.dma_start(ada_w[:, e % 2, :, :], ada[:, :, bass.ds(i * 1024 + (16 + e) * P, P)]).then_inc(ada_in[e % 2], 16)
            def u_step(i, e):
                s, t = U_COLS[e]
                act.wait_ge(q.u_ps, i * 8 + e + 1)
                src = ps[:, 3 * (e % 2):3 * (e % 2) + 3, 0:TG]
                v3 = lambda x: x.rearrange("p (b n) -> p b n", b=3)
                first = isinstance(i, int)
                if s == 5:
                    if not (first and t == 0):
                        act.wait_ge(q.u_ok, i * 2 + t)
                    act.activation(v3(sig[:, :]), src, ACT.Sigmoid).then_inc(q.u_evac, 1)
                elif s == 4:
                    act.activation(v3(u_a[:, :]), src, ACT.Copy).then_inc(q.u_evac, 1)
                else:
                    if not (first and t == 0):
                        act.wait_ge(gate_st[s - 6], i * 32 + 16 * t)
                    act.activation(v3(gates[:, s - 6, :]), src, ACT.Sigmoid).then_inc(q.u_evac, 1)
                    act.wait_ge(q.u_evac, i * 8 + e + 1)
                    act.dma_start(gate_d[s - 6, bass.ds(i * 2 + t, 1)].rearrange("o p n -> (o p) n"), gates[:, s - 6, :]).then_inc(gate_st[s - 6], 16)
                if e + 2 < 8:
                    ada_load(i, e + 2)
                else:
                    if not (isinstance(i, int) and i == 3):
                        ada_load(i + 1, e - 6)
                n = e + 4
                if first and i == 0 and n < 8:
                    used = None
                else:
                    used = (q.u_ps, i * 8 + n - 7)
                per = (i * 32) + 16 * (n // 4 + 1)
                if isinstance(i, int) and i == 3 and n >= 8:
                    per = 16 * (8 + 0) + 32
                split_w(n, per, used)
                if e == 7:
                    act.wait_ge(q.ada_used, i * 8 + 24)
                    copy(mod[:, bass.ds(i * 8 + 16, 8), :].rearrange("p k c -> p (k c)"), ps[:, 6, 0:16]).then_inc(q.adaU_ok, 1)
            for n in range(2):
                ada_load(0, n)
            for e in range(8):
                u_step(0, e)
            with act.Fori(1, 3) as i:
                for e in range(8):
                    u_step(i, e)
            for e in range(8):
                u_step(3, e)

            act.wait_ge(q.conv_step, CW * KT)
            for s_ in conv_st + gate_st:
                act.wait_ge(s_, 16 * KT)
            act.dma_start(rope[:, :, :, :], a["rope_table"].rearrange("t p (c n) -> p t c n", c=2)).then_inc(q.rope_in, 16)
            act.dma_start(gn_row[:, :], a["ret_gn_w"][0].partition_broadcast(P)).then_inc(q.rope_in, 16)
            def w_q(h, n, first):
                per = h * 64 + (16 * 8 + 32 * (n // 4 + 1))
                used = (q.u_ps, 32) if (first and n < 8) else (q.q_ps, h * 18 + ((n - 4) // 4) * 9)
                split_w(n, per, used)
            def q_step(h, first, last):
                for t in range(NT):
                    if t < 4:
                        w_q(h, 4 + t, first)
                    act.wait_ge(q.rope_ok, h * NT + t + 1)
                    act.dma_start(qkvg_d[bass.ds(h, 1), t, :, 0:512].rearrange("o p n -> (o p) n"),
                                  qk_st[:, t % 3, :]).then_inc(qk_st_s[t % 3], 16)
                def vg_store(t):
                    act.wait_ge(q.vg_ok, h * NT + t + 1)
                    act.dma_start(qkvg_d[bass.ds(h, 1), t, :, 512:1024].rearrange("o p n -> (o p) n"),
                                  vg_st[:, t % 3, :]).then_inc(vg_st_s[t % 3], 16)
                for t in range(NT):
                    if t < 4 and not last:
                        w_q(h, 8 + t, False)
                    act.wait_ge(q.q_ps, h * 18 + (10 + t))
                    if not (first and t < 3):
                        act.wait_ge(vg_st_s[t % 3], h * 48 + 16 * (t // 3))
                    src = ps[:, (9 + t) % 6, :]
                    copy(vg_st[:, t % 3, 0:256], src[:, 0:256])
                    act.activation(vg_st[:, t % 3, 256:512], src[:, 256:512], ACT.Silu).then_inc(q.vg_evac, 1)
                    if t:
                        vg_store(t - 1)
                vg_store(NT - 1)
            q_step(0, True, False)
            with act.Fori(1, HEADS - 1) as h:
                q_step(h, False, False)
            act.wait_ge(q.gain_t, 1)
            copy(gmr[:, :], ps[0:32, 7, 0:P]).then_inc(q.gain_c, 1)
            q_step(HEADS - 1, False, True)

            act.wait_ge(q.dk_arg, 1)
            act.activation(lgt[:, 1, :], lgt[:, 0, :], ACT.Exp, scale=-1.0).then_inc(q.dk_exp, 1)
            act.wait_ge(q.dk_arg, 7)
            act.activation(dk_c[:, :, :], dk_a[:, :, :], ACT.Exp).then_inc(q.dk_exp, 1)

            def split_m(n):
                if n < 6:
                    act.wait_ge(q.q_ps, 18 * HEADS)
                else:
                    c = (n - 6) % M_CHUNKS
                    g = (n - 6) // M_CHUNKS
                    if c < 16:
                        act.wait_ge(q.mr_ps, g * 16 + c + 1)
                    else:
                        act.wait_ge(q.mo_ps, 6 * g + 3 * ((c - 16) // 4 + 1))
                act.wait_ge(wr_in[n % 3], 16 * (n // 3 + 1))
                copy(wslot(n, 6)[0], wraw(n, 3)).then_inc(q.w_hi, 1)

            def r_head(h, first):
                act.wait_ge(q.hd_ok, h + 1)
                if not first:
                    act.wait_ge(q.mask_ok, h * 2)
                for d in range(2):
                    ins = act.activation(mtmp[:, d, :], tab[:, NPOS + d * P:NPOS + (d + 1) * P], ACT.Exp,
                                         scale=hd[:, 6 + d:7 + d])
                ins.then_inc(q.mexp, 1)
                for c in range(NT):
                    p = c % 2
                    act.wait_ge(tile_in[c // 3], h * 16 + 16)
                    if not (first and c < 2):
                        act.wait_ge(q.P_ps, h * NT + c - 1)
                    copy(k_hi[:, p, :], qkvg[:, c, 1, :]).then_inc(q.kv_hi, 1)
                    act.wait_ge(q.vs_ok, h * NT + c + 1)
                    copy(vs_hi[:, p, :], vs[:, p, :]).then_inc(q.kv_hi, 1)
                    if c >= 1:
                        state_evac(h, c - 1, first)
                state_evac(h, NT - 1, first)
                def prep(c):
                    p = c % 2
                    act.wait_ge(q.T_ps, h * NT + c + 1)
                    if not (first and c < 2):
                        act.wait_ge(q.in_ps, h * NT + c - 1)
                    copy(T_hi[:, p, :], ps[:, 4 + p, :]).then_inc(q.Tv_hi, 1)
                    copy(v_hi[:, p, :], qkvg[:, c, 2, :]).then_inc(q.Tv_hi, 1)
                    if c < NL:
                        act.wait_ge(q.Sscan, h * 14 + (14 - c))
                        copy(S_hi[:, p, :].rearrange("p (k n) -> p k n", k=2), S[:, c, :, :]).then_inc(q.S_hi_ok, 1)
                prep(0)
                for c in range(NT):
                    p = c % 2
                    act.wait_ge(q.sm_ok, h * NT + c + 1)
                    copy(sm_hi[:, p, :], sm[:, p, :]).then_inc(q.sm_hi_ok, 1)
                    if c + 1 < NT:
                        prep(c + 1)
                    if c < NL:
                        act.wait_ge(q.cr_ps, h * NL + c + 1)
                        if c >= 2:
                            act.wait_ge(q.ob_ok, h * NL + c - 1)
                        act.activation(o_a[:, p, :], ps[:, p, 0:256], ACT.Copy, scale=hd[:, 0:1]).then_inc(q.oa_ok, 1)
                    if c >= 1:
                        out_part(h, c - 1, first)
                out_part(h, NT - 1, first)

            def state_evac(h, c, first):
                b = 2 * (c % 2)
                act.wait_ge(q.P_ps, h * NT + c + 1)
                if c < NL:
                    src = ps[:, b:b + 2, :]
                    ins = None
                    if c == 0:
                        act.wait_ge(q.s0_in, h * 32 + 32)
                    if c < NL - 1:
                        ins = copy(S[:, c + 1, :, 0:256], src[:, :, 0:256])
                    if c > 0:
                        ins = copy(S[:, c - 1, :, 256:512], src[:, :, 256:512])
                    ins.then_inc(q.P_evac, 1)
                else:
                    if not first:
                        act.wait_ge(q.st_f_st, h * 32)
                    copy(st_out[:, :, :, :], ps[:, b:b + 2, :].rearrange("p k (d e) -> p d k e", d=2)).then_inc(q.P_evac, 1)
                    act.wait_ge(q.P_evac, h * NT + NT)
                    for d, dst in enumerate((out_sf, out_sb)):
                        act.dma_start(dst[0, 0, bass.ds(h, 1)].rearrange("o (k p) e -> p (o k) e", p=P),
                                      st_out[:, d, :, :]).then_inc(q.st_f_st, 16)

            def out_part(h, c, first):
                p = c % 2
                act.wait_ge(q.gn_v, h * NT + c + 1)
                act.activation(gstd[:, p, 1:2], gstd[:, p, 0:1], ACT.Sqrt).then_inc(q.gn_q, 1)
                if c >= 1:
                    rT_out(h, c - 1, first)
                if c == NT - 1:
                    rT_out(h, c, first)

            def rT_out(h, c, first):
                p = c % 2
                act.wait_ge(q.rT_ps, h * NT + c + 1)
                if not (first and c < 2):
                    act.wait_ge(rT_s[p], rt_count(h, c))
                copy(rT_st[:, p, :, :].rearrange("p k n -> p (k n)"), ps[:, 2, 0:256]).then_inc(q.rT_ok, 1)
                act.wait_ge(q.rT_ok, h * NT + c + 1)
                act.dma_start(rT_d[bass.ds(h * 2, 2), :, c * P:(c + 1) * P].rearrange("k p n -> p k n"),
                              rT_st[:, p, :, :]).then_inc(rT_s[p], 16)

            def rt_count(h, c):
                per = 5 if c % 2 == 0 else 4
                return h * (16 * per) + 16 * (c // 2)
            for n in range(6):
                split_m(n)
            r_head(0, True)
            with act.Fori(1, HEADS) as h:
                r_head(h, False)

            act.wait_ge(q.mem_free, 1)

            def rc_load(g, which):
                if which:
                    act.wait_ge(q.r_lo_ok, KT * (g + 1))
                elif g:
                    act.wait_ge(q.c_lo_ok, KT * g)
                src = (rT_d, conv_d)[which][:, :, g * TG:(g + 1) * TG]
                act.dma_start(rc_st[:, :, :], src.rearrange("k p n -> p k n")).then_inc(q.rc_in, 16)
            def gate_load(e):
                if e >= 16 * NTG or e % 2:
                    return
                g, w, m = e // 16, (e // 8) % 2, e % 8
                if e >= 4:
                    act.wait_ge(q.mr_evac, e - 2)
                act.dma_start(gate_t[:, e % 4:e % 4 + 2, :],
                              gate_d[w, m:m + 2, :, g * TG:(g + 1) * TG].rearrange("m p n -> p m n")).then_inc(gt_in[(e // 2) % 2], 16)
            def r_hi_part(g):
                act.wait_ge(q.rc_in, 16 * (2 * g + 1))
                if g:
                    act.wait_ge(q.mr_ps, 16 * (g - 1) + 8)
                for k in range(KT):
                    copy(r_hi[:, k, :], rc_st[:, k, :]).then_inc(q.r_hi_ok, 1)
            def squares(g):
                act.wait_ge(q.ln_d, g + 1)
                for k in range(KT):
                    n = g * KT + k
                    if n >= 2:
                        act.wait_ge(q.ln_acck, n - 1)
                    act.activation(ln_sq[:, n % 2, :], rc_st[:, k, :], ACT.Square).then_inc(q.ln_sqk, 1)
            def c_hi_part(g):
                act.wait_ge(q.ln_z, g + 1)
                for k in range(KT):
                    act.activation(rc_st[:, k, :], rc_st[:, k, :], ACT.Silu, bias=V0[:, V_LNB + k:V_LNB + k + 1],
                                   scale=V0[:, V_LNW + k:V_LNW + k + 1]).then_inc(q.ln_silu, 1)
                if g:
                    act.wait_ge(q.mr_ps, 16 * g)
                for k in range(KT):
                    act.wait_ge(q.ln_silu, g * KT + k + 1)
                    copy(c_hi[:, k, :], rc_st[:, k, :]).then_inc(q.c_hi_ok, 1)
            def m_tail(g, t):
                n = 3 * g + t
                s = n % 2
                if n >= 2:
                    act.wait_ge(xt_st[s], 16 * (n // 2))
                    act.wait_ge(q.xn2_ok, n - 1)
                act.dma_start(xt[:, s, :], a["x_sample"][0, n * P:(n + 1) * P, :] if n < NL else a["x_prompt"][0]).then_inc(xt_in[s], 16)
                act.wait_ge(q.mo_ok, 6 * g + 4 + t)
                if n:
                    act.wait_ge(q.mst_s, 2 * n)
                act.activation(sq_junk[:, :], mo[:, t, :], ACT.Square, accum_out=mst[:, s, 0:1]).then_inc(q.mst_s, 1)
                act.wait_ge(q.mst_v, 2 * n + 1)
                act.activation(mst[:, s, 2:3], mst[:, s, 1:2], ACT.Sqrt).then_inc(q.mst_q, 1)
                act.wait_ge(q.x2_ok, n + 1)
                act.dma_start(x2_d[n], xt[:, s, :]).then_inc(xt_st[s], 16)
                act.wait_ge(q.mst_s, 2 * n + 1)
                act.activation(sq_junk[:, :], xt[:, s, :], ACT.Square, accum_out=mst[:, s, 4:5]).then_inc(q.mst_s, 1)
                act.wait_ge(q.mst_v, 2 * n + 2)
                act.activation(mst[:, s, 6:7], mst[:, s, 5:6], ACT.Sqrt).then_inc(q.mst_q, 1)
            def h2_out(g, t):
                n = 3 * g + t
                cond = 0 if n < NL else 1
                act.wait_ge(q.h2s_ok, 1)
                if n:
                    act.wait_ge(q.h2_st, 16 * n)
                for half in range(2):
                    act.wait_ge(q.h2_ps, 2 * n + half + 1)
                    for k in range(4):
                        kk = 4 * half + k
                        ins = act.activation(h2o[:, kk, :], ps[:, 7 - half, k * P:(k + 1) * P], ACT.Identity,
                                             bias=mod[:, SH2 * KT + kk, cond:cond + 1], scale=h2s[:, kk, cond:cond + 1])
                    ins.then_inc(q.h2_f, 1)
                act.wait_ge(q.h2_f, 2 * n + 2)
                act.dma_start(h2T_d[:, :, n * P:(n + 1) * P].rearrange("k p n -> p k n"), h2o[:, :, :]).then_inc(q.h2_st, 16)

            split_to = [6]
            def more_w(upto):
                while split_to[0] < min(upto, 3 * M_CHUNKS):
                    split_m(split_to[0])
                    split_to[0] += 1
            rc_load(0, 0)
            for e in range(4):
                gate_load(e)
            r_hi_part(0)
            rc_load(0, 1)
            for g in range(NTG):
                for m in range(KT):
                    e = g * 16 + m
                    act.wait_ge(q.mr_evac, e + 1)
                    gate_load(e + 3)
                    more_w(g * M_CHUNKS + m + 7)
                    if m == 1:
                        squares(g)
                    if m == 4:
                        act.wait_ge(q.ln_v, g + 1)
                        act.activation(ln_a[:, :], ln_acc[:, :], ACT.Sqrt).then_inc(q.ln_r1, 1)
                    if m == 5:
                        c_hi_part(g)
                    if g and m in (1, 2, 5):
                        h2_out(g - 1, (1, 2, 5).index(m))
                for m in range(KT):
                    e = g * 16 + 8 + m
                    act.wait_ge(q.mr_evac, e + 1)
                    if g and m == 0:
                        act.wait_ge(q.mo_ps, 6 * g)
                    copy(m_hi[:, m, :], m_part[:, m, :]).then_inc(q.m_hi_ok, 1)
                    gate_load(e + 3)
                    more_w(g * M_CHUNKS + 8 + m + 7)
                    if m == 1 and g + 1 < NTG:
                        rc_load(g + 1, 0)
                    if m == 4 and g + 1 < NTG:
                        r_hi_part(g + 1)
                if g + 1 < NTG:
                    rc_load(g + 1, 1)
                for n in range(6):
                    half, t = n // 3, n % 3
                    act.wait_ge(q.mo_ps, 6 * g + n + 1)
                    if g:
                        act.wait_ge(q.h2_ps, 6 * g)
                    copy(mo[:, t, half * 512:(half + 1) * 512], ps[:, 2 + (6 * g + n) % 4, :]).then_inc(q.mo_ok, 1)
                    if n == 2:
                        more_w(g * M_CHUNKS + 26)
                more_w(g * M_CHUNKS + 30)
                for t in range(3):
                    m_tail(g, t)
            for t in range(3):
                h2_out(NTG - 1, t)

            act.wait_ge(q.mem_free, 2)
            for k in range(KT + 1):
                if k < KT:
                    if k >= 2:
                        act.wait_ge(q.B_lo_ok, k - 1)
                    act.dma_start(f_cv[:, k % 2, 0:T], h2T_d[k]).then_inc(xt_in[k % 2], 16)
                if k:
                    act.wait_ge(xt_in[(k - 1) % 2], 16 * ((5, 4)[(k - 1) % 2] + (k - 1) // 2 + 1))
                    copy(B_hi[:, k - 1, :], f_cv[:, (k - 1) % 2, 0:T]).then_inc(q.B_hi_ok, 1)

            def split_f(i, p, kind):
                if not (isinstance(i, int) and i == 0):
                    if kind < 2:
                        act.wait_ge((q.fa_ps, q.fg_ps)[kind], i * 2 + p - 1)
                    else:
                        act.wait_ge(q.fd_ps, i * 4 * NT + (p - 1) * 2 * NT)
                else:
                    act.wait_ge(q.mo_ps, 6 * NTG)
                act.wait_ge(wr_in[kind], i * 32 + 16 * (NTG * M_CHUNKS // 3 + p + 1))
                copy(wslot(3 * p + kind, 6)[0], wraw(kind, 3)).then_inc(q.w_hi, 1)
            def f_step(i, p, d_next, up_next):
                first = isinstance(i, int) and i == 0 and p == 0
                for kind in range(2):
                    ev, c0, cv = ((q.fa_ev, q.fa_c0, q.fa_c), (q.fg_ev, q.fg_c0, q.fg_c))[kind]
                    act.wait_ge((q.fa_ps, q.fg_ps)[kind], i * 2 + p + 1)
                    if not first:
                        act.wait_ge(cv, i * 4 + 2 * p)
                    b = 3 * kind
                    copy(f_in[:, kind, 1:1 + 2 * TG].rearrange("p (b n) -> p b n", b=2), ps[:, b:b + 2, 0:TG])
                    copy(f_in[:, kind, 1 + 2 * TG:1 + LAT], ps[:, b + 2, 0:LAT - 2 * TG])
                    copy(f_in[:, kind, 2 + LAT:2 + T], ps[:, b + 2, LAT - 2 * TG:TG]).then_inc(ev, 1)
                    act.wait_ge(ev, i * 2 + p + 1)
                    if not first:
                        act.wait_ge((q.gact_lo, q.fprod)[kind], i * 2 + p)
                    act.activation(f_cv[:, kind, :], f_in[:, kind, 1:1 + F_OUT], ACT.Identity,
                                   bias=VF[:, bass.ds(i * 2 + (6 * FKT + kind * FKT + p), 1)],
                                   scale=VF[:, bass.ds(i * 2 + (2 * FKT + kind * FKT + p), 1)]).then_inc(c0, 1)
                    if kind == 0:
                        act.wait_ge(q.fa_c, i * 4 + (2 * p + 2))
                        act.activation(f_cv[:, 0, :], f_cv[:, 0, :], ACT.Silu).then_inc(q.fsilu, 1)
                act.wait_ge(q.fprod, i * 2 + p + 1)
                if not (isinstance(i, int) and i == 0):
                    act.wait_ge(q.fd_ps, i * 4 * NT + (p - 1) * 2 * NT)
                for d0, s0, n_ in ((0, 0, LAT), (LAT, LAT + 1, CTX)):
                    ins = copy(g_hi[:, p, d0:d0 + n_], f_cv[:, 0, s0:s0 + n_])
                ins.then_inc(q.gact_hi, 1)
                if d_next:
                    split_f(i + (p + 1) // 2, (p + 1) % 2, 2)
                if up_next:
                    split_f(i + 1, p, 0)
                    split_f(i + 1, p, 1)
            for p in range(2):
                for kind in range(3):
                    split_f(0, p, kind)
            act.wait_ge(q.fpad, 1)
            act.wait_ge(q.B_lo_ok, KT)
            f_step(0, 0, False, True)
            f_step(0, 1, True, True)
            with act.Fori(1, FKT // 2 - 1) as i:
                f_step(i, 0, True, True)
                f_step(i, 1, True, True)
            f_step(FKT // 2 - 1, 0, True, False)
            f_step(FKT // 2 - 1, 1, False, False)

            act.wait_ge(q.fg_ps, FKT)
            act.wait_ge(q.fd_ps, 2 * NT * (FKT - 1))
            for t in range(NT):
                act.wait_ge(q.y_add, 2 * NT * (FKT - 1) + 2 * t + 2)
                if t:
                    act.wait_ge(q.e_s, t)
                act.activation(ej[:, :], y_acc[:, t, :], ACT.Square, accum_out=est[:, t, 0:1]).then_inc(q.e_s, 1)
                if t:
                    act.wait_ge(q.e_v, t)
                    act.activation(est[:, t - 1, 2:3], est[:, t - 1, 1:2], ACT.Sqrt).then_inc(q.e_q, 1)
            act.wait_ge(q.e_v, NT)
            act.activation(est[:, NT - 1, 2:3], est[:, NT - 1, 1:2], ACT.Sqrt).then_inc(q.e_q, 1)

        @block.gpsimd
        def _(pool):
            def sub(dst, x, hi):
                return pool.tensor_tensor(dst, x, Fv(hi), ALU.subtract)

            pool.memset(ident[:, :], 0.0).then_inc(q.ident_ok, 1)
            pool.memset(mean_w[:, :], 1.0 / D).then_inc(q.ident_ok, 1)
            pool.wait_ge(q.ident_ok, 2)
            pool.affine_select(out=ident[:, :], in_=ident[:, :], compare_op=ALU.not_equal, fill=1.0, base=0,
                               pattern=[[-1, P]], channel_multiplier=1).then_inc(q.ident_ok, 1)

            def lo_w(n, ring, rawring, count):
                pool.wait_ge(q.w_hi, count)
                h_, l_ = wslot(n, ring)
                sub(l_, wraw(n, rawring), h_).then_inc(q.w_lo, 1)

            for n in range(4):
                lo_w(n, 8, 4, n + 1)
            pool.wait_ge(q.hT_lo, KT)
            pool.memset(u_in[:, :, :], 0.0).then_inc(q.pads_ok, 1)
            pool.wait_ge(q.pads_ok, 1)
            def conv_store(i, t):
                for c0, y0, n in ((0, 0, LAT), (LAT, LAT + HALO, CTX)):
                    pool.dma_start(conv_d[bass.ds(i * 2 + t, 1), :, c0:c0 + n].rearrange("o p n -> (o p) n"),
                                   conv_y[:, t, y0:y0 + n]).then_inc(conv_st[t], 16)
            def u_step(i, e):
                s, t = U_COLS[e]
                if s == 4:
                    pool.wait_ge(q.u_evac, i * 8 + e + 1)
                    if not (isinstance(i, int) and i == 0):
                        pool.wait_ge(q.conv_step, i * 2 * CW + (t - 1) * CW)
                    pool.tensor_tensor(u_in[:, t, HALO:HALO + LAT], u_a[:, 0:LAT], sig[:, 0:LAT], ALU.mult)
                    pool.tensor_tensor(u_in[:, t, 2 * HALO + LAT:2 * HALO + T], u_a[:, LAT:T], sig[:, LAT:T],
                                       ALU.mult).then_inc(q.u_ok, 1)
                    if not (isinstance(i, int) and i == 0):
                        conv_store(i - 1, t)
                lo_w(e + 4, 8, 4, i * 8 + (e + 5))
            for e in range(8):
                u_step(0, e)
            with pool.Fori(1, 4) as i:
                for e in range(8):
                    u_step(i, e)
            for t in range(2):
                pool.wait_ge(q.conv_step, CW * (KT - 1 + t))
                conv_store(3, t)
            pool.wait_ge(q.rope_in, 32)
            def q_step(h, first, last):
                if not first:
                    pool.wait_ge(q.vg_ok, h * NT)
                for t in range(4):
                    lo_w(4 + t, 8, 4, h * 8 + (32 + 4 + t + 1))
                    if t == 0:
                        pool.tensor_copy(gn_head[:, :], gn_row[:, bass.ds(h * 256, 256)]).then_inc(q.gnh_ok, 1)
                pool.wait_ge(q.gnh_ok, h + 1)
                for t in range(NT):
                    if t < 4 and not last:
                        lo_w(8 + t, 8, 4, h * 8 + (32 + 8 + t + 1))
                    pool.wait_ge(q.vg_evac, h * NT + (t + 1))
                    g_ = vg_st[:, t % 3, 256:512]
                    pool.tensor_tensor(g_, g_, gn_head[:, :], ALU.mult).then_inc(q.vg_ok, 1)
            q_step(0, True, False)
            with pool.Fori(1, HEADS - 1) as h:
                q_step(h, False, False)
            q_step(HEADS - 1, False, True)

            for n in range(6):
                lo_w(n, 6, 3, N_L + n + 1)
            def r_head(h, first):
                for c in range(NT):
                    p = c % 2
                    pool.wait_ge(q.kv_hi, h * 2 * NT + (2 * c + 1))
                    sub(k_lo[:, p, :], qkvg[:, c, 1, :], k_hi[:, p, :]).then_inc(q.kv_lo, 1)
                    pool.wait_ge(q.kv_hi, h * 2 * NT + (2 * c + 2))
                    sub(vs_lo[:, p, :], vs[:, p, :], vs_hi[:, p, :]).then_inc(q.kv_lo, 1)
                def prep(c):
                    p = c % 2
                    pool.wait_ge(q.Tv_hi, h * 2 * NT + (2 * c + 2))
                    sub(v_lo[:, p, :], qkvg[:, c, 2, :], v_hi[:, p, :]).then_inc(q.v_lo_ok, 1)
                    if c < NL:
                        pool.wait_ge(q.S_hi_ok, h * NL + c + 1)
                        sub(S_lo[:, p, :].rearrange("p (k n) -> p k n", k=2), S[:, c, :, :],
                            S_hi[:, p, :].rearrange("p (k n) -> p k n", k=2)).then_inc(q.S_lo_ok, 1)
                def gated(c):
                    pool.wait_ge(q.y_ok, h * NT + c + 1)
                    if not (first and c < 2):
                        pool.wait_ge(q.rT_ps, h * NT + c - 1)
                    pool.tensor_tensor(o_r[:, c % 2, :], o_y[:, c % 2, :], qkvg[:, c, 3, :], ALU.mult).then_inc(q.r_ok, 1)
                prep(0)
                for c in range(NT):
                    pool.wait_ge(q.sm_hi_ok, h * NT + c + 1)
                    sub(sm_lo[:, c % 2, :], sm[:, c % 2, :], sm_hi[:, c % 2, :]).then_inc(q.sm_lo_ok, 1)
                    if c + 1 < NT:
                        prep(c + 1)
                    if c >= 1:
                        gated(c - 1)
                gated(NT - 1)
            r_head(0, True)
            with pool.Fori(1, HEADS) as h:
                r_head(h, False)

            split_to = [6]
            def more_w(upto):
                while split_to[0] < min(upto, 3 * M_CHUNKS):
                    n = split_to[0]
                    lo_w(n, 6, 3, N_L + n + 1)
                    split_to[0] += 1
            for g in range(NTG):
                for m in range(KT):
                    more_w(g * M_CHUNKS + m + 7)
                    if m == 1:
                        for k in range(KT):
                            n = g * KT + k
                            pool.wait_ge(q.ln_sqk, n + 1)
                            if k:
                                pool.wait_ge(q.ln_acck, n)
                                pool.tensor_tensor(ln_acc[:, :], ln_acc[:, :], ln_sq[:, n % 2, :], ALU.add).then_inc(q.ln_acck, 1)
                            else:
                                pool.tensor_copy(ln_acc[:, :], ln_sq[:, n % 2, :]).then_inc(q.ln_acck, 1)
                for m in range(KT):
                    pool.wait_ge(q.m_hi_ok, g * KT + m + 1)
                    sub(m_lo[:, m, :], m_part[:, m, :], m_hi[:, m, :]).then_inc(q.m_lo_ok, 1)
                    more_w(g * M_CHUNKS + 8 + m + 7)
                more_w(g * M_CHUNKS + 30)

            pool.wait_ge(q.mem_free, 2)
            pool.memset(f_in[:, :, :], 0.0).then_inc(q.fpad, 1)
            for t in range(NT):
                ins = pool.memset(y_acc[:, t, :], 0.0)
            ins.then_inc(q.fpad, 1)
            for n in range(6):
                lo_w(n, 6, 3, N_LM + n + 1)
            def f_step(i, p, d_next, up_next):
                pool.wait_ge(q.fg_c, i * 4 + (2 * p + 2))
                pool.wait_ge(q.fsilu, i * 2 + p + 1)
                pool.tensor_tensor(f_cv[:, 0, :], f_cv[:, 0, :], f_cv[:, 1, :], ALU.mult).then_inc(q.fprod, 1)
                pool.wait_ge(q.gact_hi, i * 2 + p + 1)
                for d0, s0, n_ in ((0, 0, LAT), (LAT, LAT + 1, CTX)):
                    ins = sub(g_lo[:, p, d0:d0 + n_], f_cv[:, 0, s0:s0 + n_], g_hi[:, p, d0:d0 + n_])
                ins.then_inc(q.gact_lo, 1)
                if d_next:
                    lo_w(3 * p + 5, 6, 3, N_LM + i * 6 + (3 * p + 6))
                if up_next:
                    lo_w(3 * p + 6, 6, 3, N_LM + i * 6 + (3 * p + 7))
                    lo_w(3 * p + 7, 6, 3, N_LM + i * 6 + (3 * p + 8))
            f_step(0, 0, False, True)
            f_step(0, 1, True, True)
            with pool.Fori(1, FKT // 2 - 1) as i:
                f_step(i, 0, True, True)
                f_step(i, 1, True, True)
            f_step(FKT // 2 - 1, 0, True, False)
            f_step(FKT // 2 - 1, 1, False, False)

        @block.vector
        def _(dve):
            steps = [0]
            def then(ins):
                steps[0] += 1
                ins.then_inc(q.dve_own, 1)
                dve.wait_ge(q.dve_own, steps[0])

            for n, (dst, src) in enumerate(((V0[:, 0:120], ps[:, 7, 0:120]), (VF[:, 0:88], ps[:, 5, 0:88]),
                                            (VF[:, 88:176], ps[:, 5, 128:216]), (VC[:, 0:124], ps[:, 4, 0:124]),
                                            (VC[:, 124:248], ps[:, 4, 128:252]))):
                dve.wait_ge(q.vecT, 5)
                dve.tensor_copy(dst, src).then_inc(q.vec_ok, 1)
            dve.wait_ge(q.ssq_ok, NT)
            dve.tensor_scalar(rst[:, :], ssq[:, :], 1.0 / D, EPS, ALU.mult, ALU.add).then_inc(q.rstd_a, 1)
            dve.wait_ge(q.rstd_b, 1)
            then(dve.reciprocal(rst[:, :], ssq[:, :]))
            for t in range(NT):
                dve.tensor_scalar(x_all[:, t, :], x_all[:, t, :], rst[:, t:t + 1], None, ALU.mult).then_inc(q.xn_ok, 1)
            def col2(c, n):
                return V0[:, c:c + n].unsqueeze(2).broadcast_to([P, n, 2])
            dve.wait_ge(q.ada_used, 16)
            dve.wait_ge(q.vec_ok, 1)
            dve.tensor_tensor(mod[:, 0:16, :], ps[:, 6, 0:32].rearrange("p (k c) -> p k c", c=2), col2(V_ADAB, 16),
                              ALU.add).then_inc(q.mod_ok, 1)
            dve.wait_ge(q.mod_ok, 1)
            dve.scalar_tensor_tensor(out=hscale[:, :, :], in0=mod[:, SC1 * KT:SC1 * KT + KT, :], scalar=1.0,
                                     in1=col2(V_N1PRE, KT), op0=ALU.add, op1=ALU.mult).then_inc(q.mod_ok, 1)
            for k in range(KT):
                dve.wait_ge(q.hT_f, k + 1)
                then(dve.tensor_copy(A_hi[:, k, :], hf[:, :]))
                dve.tensor_tensor(A_lo[:, k, :], hf[:, :], Fv(A_hi[:, k, :]), ALU.subtract).then_inc(q.hT_lo, 1)

            def conv(i, t):
                first = isinstance(i, int)
                dve.wait_ge(q.u_ok, i * 2 + t + 1)
                if not first:
                    dve.wait_ge(conv_st[t], i * 32)
                y = conv_y[:, t, :]
                for w in range(CW):
                    tap = VC[:, bass.ds(i * 2 + (w * KT + t), 1)]
                    x = u_in[:, t, w:w + U_OUT]
                    if w == 0:
                        dve.tensor_scalar(y, x, tap, V0[:, bass.ds(i * 2 + (V_CDB + t), 1)], ALU.mult, ALU.add).then_inc(q.conv_step, 1)
                    else:
                        dve.wait_ge(q.conv_step, i * 2 * CW + (t * CW + w))
                        dve.scalar_tensor_tensor(out=y, in0=x, scalar=tap, in1=y, op0=ALU.mult, op1=ALU.add).then_inc(q.conv_step, 1)
            for t in range(2):
                conv(0, t)
            with dve.Fori(1, 4) as i:
                for t in range(2):
                    conv(i, t)

            dve.wait_ge(q.rope_in, 32)
            dve.wait_ge(q.adaU_ok, 4)
            dve.tensor_tensor(mod[:, 16:48, :], mod[:, 16:48, :], col2(V_ADAB + 16, 32), ALU.add).then_inc(q.mod_ok, 1)
            dve.wait_ge(q.mod_ok, 3)
            for n, (g_, v) in enumerate(((G1, V_N1POST), (G2, V_N2POST))):
                for c in range(2):
                    ins = dve.tensor_tensor(gm1[:, (2 * n + c) * KT:(2 * n + c + 1) * KT], mod[:, g_ * KT:(g_ + 1) * KT, c],
                                            V0[:, v:v + KT], ALU.mult)
            ins.then_inc(q.mod_ok, 1)
            def q_step(h, first):
                for t in range(NT):
                    src = ps[:, t % 6, :]
                    dst = qk_st[:, t % 3, :]
                    dve.wait_ge(q.q_ps, h * 18 + (t + 1))
                    if not (first and t == 0):
                        dve.wait_ge(q.rope_ok, h * NT + t)
                    if t < NL:
                        q2 = lambda x: x.rearrange("p (s n) -> p s n", s=2)
                        dve.tensor_tensor(q2(rope_c[:, :]), q2(src), rope[:, t, 0, :].unsqueeze(1).broadcast_to([P, 2, 256]), ALU.mult)
                        parts = lambda x: x.rearrange("p (s h a f) -> p s h a f", s=2, h=2, a=2)
                        sn = rope[:, t, 1, :].rearrange("p (h a f) -> p h a f", h=2, a=2)
                        for a_ in range(2):
                            for s_ in range(2):
                                ins = dve.tensor_tensor(parts(rope_s[:, :])[:, s_, :, a_, :], parts(src)[:, s_, :, 1 - a_, :],
                                                        sn[:, :, a_, :], ALU.mult)
                        ins.then_inc(q.qk_evac, 1)
                        dve.wait_ge(q.qk_evac, h * NT + (t + 1))
                        if not (first and t < 3):
                            dve.wait_ge(qk_st_s[t % 3], h * 48 + 16 * (t // 3))
                        dve.tensor_tensor(dst, rope_c[:, :], rope_s[:, :], ALU.add).then_inc(q.rope_ok, 1)
                    else:
                        dve.tensor_copy(rope_c[:, :], src).then_inc(q.qk_evac, 1)
                        dve.wait_ge(q.qk_evac, h * NT + (t + 1))
                        if not (first and t < 3):
                            dve.wait_ge(qk_st_s[t % 3], h * 48 + 16 * (t // 3))
                        dve.tensor_copy(dst, rope_c[:, :]).then_inc(q.rope_ok, 1)
            q_step(0, True)
            with dve.Fori(1, HEADS) as h:
                q_step(h, False)

            dve.wait_ge(q.tab_in, 48)
            dve.scalar_tensor_tensor(out=lgt[:, 0, :], in0=dec[:, :], scalar=-1.0, in1=dec[:, :],
                                     op0=ALU.mult, op1=ALU.max).then_inc(q.dk_arg, 1)
            dve.wait_ge(q.dk_exp, 1)
            e_, d_, z_, zz, p_ = (lgt[:, n, :] for n in range(1, 6))
            then(dve.tensor_scalar(d_, e_, 2.0, None, ALU.add))
            then(dve.reciprocal(z_, d_))
            then(dve.tensor_tensor(z_, z_, e_, ALU.mult))
            then(dve.tensor_tensor(zz, z_, z_, ALU.mult))
            then(dve.tensor_scalar(p_, zz, 1.0 / 15, None, ALU.mult))
            for m in (13, 11, 9, 7, 5, 3):
                then(dve.scalar_tensor_tensor(out=p_, in0=p_, scalar=1.0 / m, in1=zz, op0=ALU.add, op1=ALU.mult))
            then(dve.scalar_tensor_tensor(out=p_, in0=p_, scalar=1.0, in1=z_, op0=ALU.add, op1=ALU.mult))
            then(dve.tensor_scalar(p_, p_, 2.0, None, ALU.mult))
            then(dve.scalar_tensor_tensor(out=lg[:, :], in0=dec[:, :], scalar=0.0, in1=p_, op0=ALU.min, op1=ALU.subtract))
            for n in range(4):
                dve.tensor_scalar(dk_a[:, :, n], lg[:, (n % 2) * HEADS:(n % 2 + 1) * HEADS], tab[:, n:n + 1], None,
                                  ALU.mult).then_inc(q.dk_arg, 1)
            for n in range(2):
                dve.tensor_scalar(dk_a[:, :, 4 + n], lg[:, n * HEADS:(n + 1) * HEADS], float(P), None,
                                  ALU.mult).then_inc(q.dk_arg, 1)
            dve.wait_ge(q.dk_exp, 2)
            then(dve.tensor_scalar(dkt[:, :, 0:2], dk_c[:, :, 0:2], DK ** -0.5, None, ALU.mult))
            then(dve.tensor_copy(dkt[:, :, 2:6], dk_c[:, :, 2:6]))
            then(dve.tensor_copy(dkt[:, :, 6:8], lg[:, :].rearrange("p (d h) -> p h d", d=2)))

            def r_head(h, first):
                if not first:
                    dve.wait_ge(q.oa_ok, h * NL)
                dve.tensor_copy(hd[:, :], dkt[:, bass.ds(h, 1), :].rearrange("p o n -> p (o n)")).then_inc(q.hd_ok, 1)
                dve.wait_ge(q.mexp, h + 1)
                for d in range(2):
                    ins = dve.tensor_tensor(mtmp[:, 2 + d, :], mtmp[:, d, :], tab[:, NPOS + (2 + d) * P:NPOS + (3 + d) * P], ALU.mult)
                ins.then_inc(q.mask_ok, 1)
                dve.wait_ge(q.mask_ok, h * 2 + 1)
                dve.tensor_tensor(mask[:, :], mtmp[:, 2, :], mtmp[:, 3, :], ALU.add).then_inc(q.mask_ok, 1)
                dve.wait_ge(q.mask_ok, h * 2 + 2)

                def fwd(c):
                    dve.wait_ge(q.P_evac, h * NT + c + 1)
                    dve.wait_ge(q.Sscan, h * 14 + c) if c or not first else None
                    dve.scalar_tensor_tensor(out=S[:, c + 1, :, 0:256], in0=S[:, c, :, 0:256], scalar=hd[:, 4:5],
                                             in1=S[:, c + 1, :, 0:256], op0=ALU.mult, op1=ALU.add).then_inc(q.Sscan, 1)
                dve.wait_ge(q.s0_in, h * 32 + 32)
                for c in range(NT):
                    p = c % 2
                    dve.wait_ge(tile_in[c // 3], h * 16 + 16)
                    if not (first and c < 2):
                        dve.wait_ge(q.kv_lo, h * 2 * NT + (2 * c - 2))
                    dve.tensor_scalar(vs[:, p, 0:256], qkvg[:, c, 2, :], hd[:, 2:3], None, ALU.mult)
                    dve.tensor_scalar(vs[:, p, 256:512], qkvg[:, c, 2, :], hd[:, 3:4], None, ALU.mult).then_inc(q.vs_ok, 1)
                    if c >= 2:
                        fwd(c - 2) if c - 2 < NL - 1 else None
                dve.wait_ge(q.P_evac, h * NT + NL)
                for c in range(NL - 2, -1, -1):
                    dve.wait_ge(q.Sscan, h * 14 + (13 - c))
                    dve.scalar_tensor_tensor(out=S[:, c, :, 256:512], in0=S[:, c + 1, :, 256:512], scalar=hd[:, 5:6],
                                             in1=S[:, c, :, 256:512], op0=ALU.mult, op1=ALU.add).then_inc(q.Sscan, 1)

                def t_lo(c):
                    p = c % 2
                    dve.wait_ge(q.Tv_hi, h * 2 * NT + (2 * c + 1))
                    dve.tensor_tensor(T_lo[:, p, :], ps[:, 4 + p, :], Fv(T_hi[:, p, :]), ALU.subtract).then_inc(q.T_lo_ok, 1)
                def finish(c):
                    p = c % 2
                    dve.wait_ge(q.gn_q, h * NT + c + 1)
                    dve.reciprocal(gstd[:, p, 2:3], gstd[:, p, 1:2]).then_inc(q.gn_r, 1)
                    dve.wait_ge(q.gn_r, h * NT + c + 1)
                    if not (first and c < 2):
                        dve.wait_ge(q.r_ok, h * NT + c - 1)
                    dve.tensor_scalar(o_y[:, p, :], o_o[:, p, :], bn2[:, p, 0:1], gstd[:, p, 2:3], ALU.subtract, ALU.mult).then_inc(q.y_ok, 1)
                t_lo(0)
                for c in range(NT):
                    p = c % 2
                    dve.wait_ge(q.sc_ps, h * NT + c + 1)
                    if not (first and c < 2):
                        dve.wait_ge(q.sm_lo_ok, h * NT + c - 1)
                    dve.tensor_tensor(sm[:, p, :], ps[:, 6, 0:P], mask[:, :], ALU.mult).then_inc(q.sm_ok, 1)
                    if c + 1 < NT:
                        t_lo(c + 1)
                    if c < NL:
                        dve.wait_ge(q.oa_ok, h * NL + c + 1)
                        dve.scalar_tensor_tensor(out=o_b[:, p, :], in0=ps[:, p, 256:512], scalar=hd[:, 1:2],
                                                 in1=o_a[:, p, :], op0=ALU.mult, op1=ALU.add).then_inc(q.ob_ok, 1)
                    if c >= 1:
                        finish(c - 1)
                    dve.wait_ge(q.in_ps, h * NT + c + 1)
                    o_ = ps[:, 7 if p else 3, 0:256]
                    if c < NL:
                        dve.wait_ge(q.ob_ok, h * NL + c + 1)
                        dve.tensor_tensor(o_o[:, p, :], o_, o_b[:, p, :], ALU.add).then_inc(q.o_ok, 1)
                    else:
                        dve.tensor_copy(o_o[:, p, :], o_).then_inc(q.o_ok, 1)
                    dve.wait_ge(q.o_ok, h * NT + c + 1)
                    dve.bn_stats(bn6[:, p, :], o_o[:, p, :]).then_inc(q.gn_s, 1)
                    dve.wait_ge(q.gn_s, h * 2 * NT + 2 * c + 1)
                    dve.memset(gstd[:, p, 3:4], 0.0)
                    dve.bn_aggr(bn2[:, p, :], bn6[:, p, :]).then_inc(q.gn_s, 1)
                    dve.wait_ge(q.gn_s, h * 2 * NT + 2 * c + 2)
                    dve.tensor_scalar(gstd[:, p, 0:1], bn2[:, p, 1:2], GN_EPS, None, ALU.add).then_inc(q.gn_v, 1)
                finish(NT - 1)
            r_head(0, True)
            with dve.Fori(1, HEADS) as h:
                r_head(h, False)

            dve.wait_ge(q.mem_free, 1)
            dve.scalar_tensor_tensor(out=h2s[:, :, :], in0=mod[:, SC2 * KT:SC2 * KT + KT, :], scalar=1.0,
                                     in1=col2(V_N2PRE, KT), op0=ALU.add, op1=ALU.mult).then_inc(q.h2s_ok, 1)
            def r_lo_part(g):
                for k in range(KT):
                    dve.wait_ge(q.r_hi_ok, g * KT + k + 1)
                    dve.tensor_tensor(r_lo[:, k, :], rc_st[:, k, :], Fv(r_hi[:, k, :]), ALU.subtract).then_inc(q.r_lo_ok, 1)
            def over_k(x):
                return x.unsqueeze(1).broadcast_to([P, KT, TG])
            def m_tail(g, t):
                n = 3 * g + t
                s = n % 2
                cond = 0 if n < NL else 1
                dve.wait_ge(q.mst_s, 2 * n + 1)
                dve.tensor_scalar(mst[:, s, 1:2], mst[:, s, 0:1], 1.0 / D, EPS, ALU.mult, ALU.add).then_inc(q.mst_v, 1)
                dve.wait_ge(q.mst_q, 2 * n + 1)
                then(dve.reciprocal(mst[:, s, 3:4], mst[:, s, 2:3]))
                if n == 0:
                    dve.wait_ge(q.g1_in, 32)
                then(dve.scalar_tensor_tensor(out=mo[:, t, :], in0=mo[:, t, :], scalar=mst[:, s, 3:4], in1=g1_row[:, cond, :],
                                              op0=ALU.mult, op1=ALU.mult))
                dve.wait_ge(xt_in[s], 16 * (n // 2 + 1))
                dve.tensor_tensor(xt[:, s, :], xt[:, s, :], mo[:, t, :], ALU.add).then_inc(q.x2_ok, 1)
                dve.wait_ge(q.mst_s, 2 * n + 2)
                dve.tensor_scalar(mst[:, s, 5:6], mst[:, s, 4:5], 1.0 / D, EPS, ALU.mult, ALU.add).then_inc(q.mst_v, 1)
                dve.wait_ge(q.mst_q, 2 * n + 2)
                then(dve.reciprocal(mst[:, s, 7:8], mst[:, s, 6:7]))
                dve.tensor_scalar(mo[:, t, :], xt[:, s, :], mst[:, s, 7:8], None, ALU.mult).then_inc(q.xn2_ok, 1)
            r_lo_part(0)
            for g in range(NTG):
                dve.wait_ge(q.rc_in, 16 * (2 * g + 2))
                dve.tensor_reduce(ln_a[:, :], rc_st[:, :, :].rearrange("p k t -> p t k"), AX.X, ALU.add).then_inc(q.ln_s, 1)
                if g:
                    for t in range(3):
                        m_tail(g - 1, t)
                for m in range(KT):
                    e = 16 * g + m
                    dve.wait_ge(q.mr_ps, e + 1)
                    dve.wait_ge(gt_in[(e // 2) % 2], 16 * (e // 4 + 1))
                    if g:
                        dve.wait_ge(q.m_lo_ok, KT * (g - 1) + m + 1)
                    dve.tensor_tensor(m_part[:, m, :], ps[:, e % 2, 0:TG], gate_t[:, e % 4, :], ALU.mult).then_inc(q.mr_evac, 1)
                    if m == 0:
                        dve.wait_ge(q.ln_mp, g + 1)
                        dve.tensor_tensor(rc_st[:, :, :], rc_st[:, :, :], over_k(ps[:, 6, 0:TG]), ALU.subtract).then_inc(q.ln_d, 1)
                    if m == 3:
                        dve.wait_ge(q.ln_vp, g + 1)
                        dve.tensor_scalar(ln_acc[:, :], ps[:, 6, 0:TG], GN_EPS, None, ALU.add).then_inc(q.ln_v, 1)
                    if m == 4:
                        dve.wait_ge(q.ln_r1, g + 1)
                        then(dve.reciprocal(ln_acc[:, :], ln_a[:, :]))
                        dve.tensor_tensor(rc_st[:, :, :], rc_st[:, :, :], over_k(ln_acc[:, :]), ALU.mult).then_inc(q.ln_z, 1)
                    if m == 6:
                        for k in range(KT):
                            dve.wait_ge(q.c_hi_ok, g * KT + k + 1)
                            dve.tensor_tensor(c_lo[:, k, :], rc_st[:, k, :], Fv(c_hi[:, k, :]), ALU.subtract).then_inc(q.c_lo_ok, 1)
                for m in range(KT):
                    e = 16 * g + 8 + m
                    dve.wait_ge(q.mr_ps, e + 1)
                    dve.wait_ge(gt_in[(e // 2) % 2], 16 * (e // 4 + 1))
                    then(dve.tensor_tensor(gate_t[:, e % 4, :], ps[:, e % 2, 0:TG], gate_t[:, e % 4, :], ALU.mult))
                    dve.tensor_tensor(m_part[:, m, :], m_part[:, m, :], gate_t[:, e % 4, :], ALU.add).then_inc(q.mr_evac, 1)
                    if m == 5 and g + 1 < NTG:
                        r_lo_part(g + 1)
            for t in range(3):
                m_tail(NTG - 1, t)

            for k in range(KT):
                dve.wait_ge(q.B_hi_ok, k + 1)
                dve.tensor_tensor(B_lo[:, k, :], f_cv[:, k % 2, 0:T], Fv(B_hi[:, k, :]), ALU.subtract).then_inc(q.B_lo_ok, 1)
            dve.wait_ge(q.fpad, 2)
            def taps(i, p, kind):
                c0, cv = ((q.fa_c0, q.fa_c), (q.fg_c0, q.fg_c))[kind]
                dve.wait_ge(c0, i * 2 + p + 1)
                for n, w in enumerate((0, 2)):
                    if n:
                        dve.wait_ge(cv, i * 4 + (2 * p + 1))
                    dve.scalar_tensor_tensor(out=f_cv[:, kind, :], in0=f_in[:, kind, w:w + F_OUT],
                                             scalar=VF[:, bass.ds(i * 2 + (w * 2 * FKT + kind * FKT + p), 1)],
                                             in1=f_cv[:, kind, :], op0=ALU.mult, op1=ALU.add).then_inc(cv, 1)
            def add_down(i, p):
                for n in range(2 * NT):
                    t, half = n // 2, n % 2
                    dve.wait_ge(q.fd_ps, i * 4 * NT + (p * 2 * NT + n + 1))
                    y = y_acc[:, t, half * 512:(half + 1) * 512]
                    dve.tensor_tensor(y, ps[:, 6 + half, :], y, ALU.add).then_inc(q.y_add, 1)
            taps(0, 0, 0)
            taps(0, 0, 1)
            taps(0, 1, 0)
            add_down(0, 0)
            taps(0, 1, 1)
            with dve.Fori(1, FKT // 2) as i:
                taps(i, 0, 0)
                add_down(i - 1, 1)
                taps(i, 0, 1)
                taps(i, 1, 0)
                add_down(i, 0)
                taps(i, 1, 1)
            add_down(FKT // 2 - 1, 1)

            def e_apply(t):
                cond = 0 if t < NL else 1
                dve.wait_ge(q.e_q, t + 1)
                then(dve.reciprocal(est[:, t, 3:4], est[:, t, 2:3]))
                then(dve.scalar_tensor_tensor(out=y_acc[:, t, :], in0=y_acc[:, t, :], scalar=est[:, t, 3:4], in1=g2_row[:, cond, :],
                                              op0=ALU.mult, op1=ALU.mult))
                dve.tensor_tensor(x2t[:, t, :], x2t[:, t, :], y_acc[:, t, :], ALU.add).then_inc(q.e_o, 1)
            dve.wait_ge(q.x2_in, 16 * (NT + 2))
            for t in range(NT):
                dve.wait_ge(q.e_s, t + 1)
                dve.tensor_scalar(est[:, t, 1:2], est[:, t, 0:1], 1.0 / D, EPS, ALU.mult, ALU.add).then_inc(q.e_v, 1)
                if t:
                    e_apply(t - 1)
            e_apply(NT - 1)


_INS = ["x_prompt", "x_sample", "state_ret_fwd", "state_ret_bwd", "c", "c_ctx", "norm1_pre", "norm1_post", "norm2_pre",
        "norm2_post", "ada_w", "ada_b", "w_in", "ret_decay_fwd", "ret_decay_bwd", "ret_gn_w", "ret_w_out", "conv_dw_w",
        "conv_dw_b", "conv_ln_w", "conv_ln_b", "conv_w_out", "w_mix_out", "ffn_w_up", "ffn_dw_w", "ffn_dw_b", "ffn_w_down"]
_OUTS = [(1, CTX, D), (1, LAT, D), (1, 1, HEADS, DK, DV), (1, 1, HEADS, DK, DV)]


def kernel(**inputs):
    import concourse.bacc as bacc
    from concourse.bass_utils import run_bass_kernel_spmd

    nc = bacc.Bacc("TRN2", target_bir_lowering=False, num_devices=1)
    arrays, aps = {}, {}
    rope_table, shape_table = shape_tables()
    for name, v in [(n, inputs[n]) for n in _INS] + [("rope_table", rope_table), ("shape_table", shape_table)]:
        v = np.ascontiguousarray(v)
        arrays[f"in_{name}"] = v
        aps[name] = nc.dram_tensor(f"in_{name}", v.shape, mybir.dt.from_np(v.dtype), kind="ExternalInput").ap()
    outs = [nc.dram_tensor(f"out_{i}", s, F32, kind="ExternalOutput").ap() for i, s in enumerate(_OUTS)]
    build(nc, aps, *outs)
    r = run_bass_kernel_spmd(nc, [arrays], core_ids=[0])
    return tuple(r.results[0][f"out_{i}"] for i in range(len(_OUTS)))
```

```python
from contextlib import ExitStack

import numpy as np
import concourse.bass as bass
from concourse import mybir

P = 128
D = 1024
KT = D // P
LAT, CTX = 1024, 128
T = LAT + CTX
NT = T // P
NL = LAT // P
TG = 384
NTG = T // TG
HEADS, DK, DV = 4, 256, 256
CW = 31
HALO = CW // 2
FF = 2816
FKT = FF // P
EPS, GN_EPS = 1e-6, 1e-5
GRID_W = 64
CHW = 1024
U_OUT = LAT + HALO + CTX
U_IN = U_OUT + 2 * HALO
F_OUT = LAT + 1 + CTX
F_IN = F_OUT + 2
NPOS = 4

F32, F32R = mybir.dt.float32, mybir.dt.float32r
ALU = mybir.AluOpType
ACT = mybir.ActivationFunctionType
AX = mybir.AxisListType

V_C, V_CC, V_N1PRE, V_N2PRE, V_LNW, V_LNB, V_CDB, V_N1POST, V_N2POST, V_ADAB = 0, 8, 16, 24, 32, 40, 48, 56, 64, 72
SH1, SC1, G1, SH2, SC2, G2 = range(6)


def shape_tables():
    nf = DK // 4
    inv = (10000.0 ** (-np.arange(nf, dtype=np.float32) / nf)).astype(np.float32)
    tok = np.arange(LAT)
    rope = np.zeros((NL, P, 2, 2, 2, nf), np.float32)
    for half, pos in enumerate((tok // GRID_W, tok % GRID_W)):
        ang = (pos[:, None].astype(np.float32) * inv[None, :]).astype(np.float32)
        c, s = np.cos(ang).reshape(NL, P, nf), np.sin(ang).reshape(NL, P, nf)
        rope[:, :, 0, half, 0], rope[:, :, 0, half, 1] = c, c
        rope[:, :, 1, half, 0], rope[:, :, 1, half, 1] = -s, s
    i = np.arange(P, dtype=np.float32)
    pos = np.stack([i + 1, P - i, P - 1 - i, i], 1)
    rel = i[None, :] - i[:, None]
    scale = DK ** -0.5
    dist = np.stack([np.maximum(rel, 0), np.maximum(-rel, 0), (rel >= 0) * scale, (rel <= 0) * scale], 1)
    table = np.concatenate([pos, dist.reshape(P, 4 * P)], 1).astype(np.float32)
    return rope.reshape(NL, P, 4 * P), np.ascontiguousarray(table)


def build(nc, a, out_xp, out_xs, out_sf, out_sb):
    ctx = ExitStack()
    uniq = [0]

    def sb(name, shape, dt=F32, stack=None):
        return (stack or ctx).enter_context(nc.sbuf_tensor(name, shape, dt))

    def sem(name):
        return ctx.enter_context(nc.semaphore(name))

    with ctx:
        conv_d = nc.dram_tensor("conv_d", [KT, P, T], F32, kind="Internal").ap()
        gate_d = nc.dram_tensor("gate_d", [2, KT, P, T], F32, kind="Internal").ap()
        qkvg_d = nc.dram_tensor("qkvg_d", [HEADS, NT, P, 1024], F32, kind="Internal").ap()
        rT_d = nc.dram_tensor("rT_d", [KT, P, T], F32, kind="Internal").ap()
        x2_d = nc.dram_tensor("x2_d", [NT, P, D], F32, kind="Internal").ap()
        h2T_d = nc.dram_tensor("h2T_d", [KT, P, T], F32, kind="Internal").ap()
        gain_d = nc.dram_tensor("gain_d", [32, P], F32, kind="Internal").ap()

        W_hi = sb("W_hi", [P, 6, CHW], F32R)
        W_lo = sb("W_lo", [P, 6, CHW], F32R)
        W_raw = sb("W_raw", [P, 3, CHW])
        V0 = sb("V0", [P, P])
        VF = sb("VF", [P, 4 * FKT * 2])
        mod = sb("mod", [P, 48, 2])
        ident = sb("ident", [P, P])
        mean_w = sb("mean_w", [P, P])

        s_L = ExitStack()
        A_hi = sb("A_hi", [P, KT, T], F32R, s_L)
        A_lo = sb("A_lo", [P, KT, T], F32R, s_L)
        W2_hi = sb("W2_hi", [P, 2, CHW], F32R, s_L)
        W2_lo = sb("W2_lo", [P, 2, CHW], F32R, s_L)
        W2_raw = sb("W2_raw", [P, 1, CHW], F32, s_L)
        VC = sb("VC", [P, CW * KT], F32, s_L)
        s_PU = ExitStack()
        ada_w = sb("ada_w", [P, 2, KT, P], F32, s_PU)
        cs = sb("cs", [P, KT, 2], F32, s_PU)
        s_P = ExitStack()
        x_all = sb("x_all", [P, NT, D], F32, s_P)
        rows = sb("rows", [P, 5, P], F32, s_P)
        hf = sb("hf", [P, T], F32, s_P)
        ssq = sb("ssq", [P, NT], F32, s_P)
        rst = sb("rst", [P, NT], F32, s_P)
        hscale = sb("hscale", [P, KT, 2], F32, s_P)
        s_P.close()
        s_U = ExitStack()
        u_in = sb("u_in", [P, 2, U_IN], F32, s_U)
        sig = sb("sig", [P, T], F32, s_U)
        u_a = sb("u_a", [P, T], F32, s_U)
        gates = sb("gates", [P, 2, T], F32, s_U)
        conv_y = sb("conv_y", [P, 2, U_OUT], F32, s_U)
        s_U.close()
        s_PU.close()
        s_Q = ExitStack()
        rope = sb("rope", [P, NL, 2, 256], F32, s_Q)
        gn_row = sb("gn_row", [P, D], F32, s_Q)
        gn_head = sb("gn_head", [P, 256], F32, s_Q)
        qk_st = sb("qk_st", [P, 3, 512], F32, s_Q)
        vg_st = sb("vg_st", [P, 3, 512], F32, s_Q)
        rope_c = sb("rope_c", [P, 512], F32, s_Q)
        rope_s = sb("rope_s", [P, 512], F32, s_Q)
        gm1 = sb("gm1", [P, 32], F32, s_Q)
        gmr = sb("gmr", [32, P], F32, s_Q)
        s_Q.close()
        s_L.close()
        s_R = ExitStack()
        qkvg = sb("qkvg", [P, NT, 4, 256], F32, s_R)
        S = sb("S", [P, NL, 2, 512], F32, s_R)
        k_hi = sb("k_hi", [P, 2, 256], F32R, s_R)
        k_lo = sb("k_lo", [P, 2, 256], F32R, s_R)
        vs = sb("vs", [P, 2, 512], F32, s_R)
        vs_hi = sb("vs_hi", [P, 2, 512], F32R, s_R)
        vs_lo = sb("vs_lo", [P, 2, 512], F32R, s_R)
        st_out = sb("st_out", [P, 2, 2, 256], F32, s_R)
        T_hi = sb("T_hi", [P, 2, 512], F32R, s_R)
        T_lo = sb("T_lo", [P, 2, 512], F32R, s_R)
        S_hi = sb("S_hi", [P, 2, 1024], F32R, s_R)
        S_lo = sb("S_lo", [P, 2, 1024], F32R, s_R)
        v_hi = sb("v_hi", [P, 2, 256], F32R, s_R)
        v_lo = sb("v_lo", [P, 2, 256], F32R, s_R)
        sm = sb("sm", [P, 2, P], F32, s_R)
        sm_hi = sb("sm_hi", [P, 2, P], F32R, s_R)
        sm_lo = sb("sm_lo", [P, 2, P], F32R, s_R)
        o_a = sb("o_a", [P, 2, 256], F32, s_R)
        o_b = sb("o_b", [P, 2, 256], F32, s_R)
        o_o = sb("o_o", [P, 2, 256], F32, s_R)
        o_y = sb("o_y", [P, 2, 256], F32, s_R)
        o_r = sb("o_r", [P, 2, 256], F32, s_R)
        bn6 = sb("bn6", [P, 2, 6], F32, s_R)
        bn2 = sb("bn2", [P, 2, 2], F32, s_R)
        gstd = sb("gstd", [P, 2, 4], F32, s_R)
        rT_st = sb("rT_st", [P, 2, 2, P], F32, s_R)
        tab = sb("tab", [P, NPOS + 4 * P], F32, s_R)
        dec = sb("dec", [P, 2 * HEADS], F32, s_R)
        lg = sb("lg", [P, 2 * HEADS], F32, s_R)
        lgt = sb("lgt", [P, 6, 2 * HEADS], F32, s_R)
        dk_a = sb("dk_a", [P, HEADS, 6], F32, s_R)
        dk_c = sb("dk_c", [P, HEADS, 6], F32, s_R)
        hd = sb("hd", [P, 8], F32, s_R)
        dkt = sb("dkt", [P, HEADS, 8], F32, s_R)
        mask = sb("mask", [P, P], F32, s_R)
        mtmp = sb("mtmp", [P, 4, P], F32, s_R)
        s_R.close()
        s_M = ExitStack()
        r_hi = sb("r_hi", [P, KT, TG], F32R, s_M)
        r_lo = sb("r_lo", [P, KT, TG], F32R, s_M)
        c_hi = sb("c_hi", [P, KT, TG], F32R, s_M)
        c_lo = sb("c_lo", [P, KT, TG], F32R, s_M)
        s_C = ExitStack()
        conv0 = sb("conv0", [P, KT, TG], F32, s_C)
        s_C.close()
        m_hi = sb("m_hi", [P, KT, TG], F32R, s_M)
        m_lo = sb("m_lo", [P, KT, TG], F32R, s_M)
        rc_st = sb("rc_st", [P, KT, TG], F32, s_M)
        m_part = sb("m_part", [P, KT, TG], F32, s_M)
        gate_t = sb("gate_t", [P, 4, TG], F32, s_M)
        ln_a = sb("ln_a", [P, TG], F32, s_M)
        ln_sq = sb("ln_sq", [P, 2, TG], F32, s_M)
        ln_acc = sb("ln_acc", [P, TG], F32, s_M)
        g1_row = sb("g1_row", [P, D], F32, s_M)
        mo = sb("mo", [P, 3, D], F32, s_M)
        h2o = sb("h2o", [P, KT, P], F32, s_M)
        xt = sb("xt", [P, 3, D], F32, s_M)
        sq_junk = sb("sq_junk", [P, D], F32, s_M)
        mst = sb("mst", [P, 3, 8], F32, s_M)
        h2s = sb("h2s", [P, KT, 2], F32, s_M)
        s_M.close()
        s_F = ExitStack()
        B_hi = sb("B_hi", [P, KT, T], F32R, s_F)
        B_lo = sb("B_lo", [P, KT, T], F32R, s_F)
        s_H = ExitStack()
        h2_in = sb("h2_in", [P, KT, 2 * TG], F32, s_H)
        s_H.close()
        y_acc = sb("y_acc", [P, NT, D], F32, s_F)
        f_in = sb("f_in", [P, 2, F_IN], F32, s_F)
        f_cv = sb("f_cv", [P, 2, F_OUT], F32, s_F)
        g_hi = sb("g_hi", [P, 2, T], F32R, s_F)
        g_lo = sb("g_lo", [P, 2, T], F32R, s_F)
        s_F.close()
        s_E = ExitStack()
        x2t = sb("x2t", [P, NT, D], F32, s_E)
        g2_row = sb("g2_row", [P, 2, D], F32, s_E)
        ej = sb("ej", [P, D], F32, s_E)
        est = sb("est", [P, NT, 4], F32, s_E)
        s_E.close()

        ps = ctx.enter_context(nc.psum_tensor("ps", [P, 8, 512], F32))

        def wslot(n, ring):
            s = n % ring
            return (W_hi[:, s, :], W_lo[:, s, :]) if s < 6 else (W2_hi[:, s - 6, :], W2_lo[:, s - 6, :])

        def wraw(n, ring):
            s = n % ring
            return W_raw[:, s, :] if s < 3 else W2_raw[:, 0, :]

        w_in = a["w_in"][0]
        ada = a["ada_w"][0].rearrange("(k p) n -> p k n", p=P)
        w_in_p = w_in.rearrange("(k p) n -> p k n", p=P)
        w_in_s = w_in.rearrange("(k p) (s c) -> p k s c", p=P, s=8)
        Fv = lambda x: x.bitcast(F32)

        class Semaphores:
            pass
        q = Semaphores()
        q.gnh_ok = sem("gnh_ok")
        q.kv_hi = sem("kv_hi")
        q.kv_lo = sem("kv_lo")
        q.Tv_hi = sem("Tv_hi")
        q.mem_free = sem("mem_free")
        q.dve_own = sem("dve_own")
        q.w_hi = sem("w_hi")
        q.w_lo = sem("w_lo")
        q.vec_in = sem("vec_in")
        q.vecT = sem("vecT")
        q.vec_ok = sem("vec_ok")
        q.x_in0 = sem("x_in0")
        q.ident_ok = sem("ident_ok")
        q.cs_ok = sem("cs_ok")
        q.ada_in0 = sem("ada_in0")
        q.ada_in1 = sem("ada_in1")
        q.ada_used = sem("ada_used")
        q.mod_ok = sem("mod_ok")
        q.ssq_ok = sem("ssq_ok")
        q.rstd_a = sem("rstd_a")
        q.rstd_b = sem("rstd_b")
        q.xn_ok = sem("xn_ok")
        q.hT_ps = sem("hT_ps")
        q.hT_f = sem("hT_f")
        q.hT_lo = sem("hT_lo")
        q.u_ps = sem("u_ps")
        q.u_evac = sem("u_evac")
        q.u_ok = sem("u_ok")
        q.pads_ok = sem("pads_ok")
        q.conv_step = sem("conv_step")
        q.conv_st0 = sem("conv_st0")
        q.conv_st1 = sem("conv_st1")
        q.gate_st0 = sem("gate_st0")
        q.gate_st1 = sem("gate_st1")
        q.adaU_ok = sem("adaU_ok")
        q.q_ps = sem("q_ps")
        q.qk_evac = sem("qk_evac")
        q.vg_evac = sem("vg_evac")
        q.rope_in = sem("rope_in")
        q.rope_ok = sem("rope_ok")
        q.qk_st0 = sem("qk_st0")
        q.qk_st1 = sem("qk_st1")
        q.qk_st2 = sem("qk_st2")
        q.vg_ok = sem("vg_ok")
        q.vg_st0 = sem("vg_st0")
        q.vg_st1 = sem("vg_st1")
        q.vg_st2 = sem("vg_st2")
        q.gain_t = sem("gain_t")
        q.gain_c = sem("gain_c")
        q.gain_st = sem("gain_st")
        q.tab_in = sem("tab_in")
        q.dk_arg = sem("dk_arg")
        q.dk_exp = sem("dk_exp")
        q.hd_ok = sem("hd_ok")
        q.mexp = sem("mexp")
        q.mask_ok = sem("mask_ok")
        q.s0_in = sem("s0_in")
        q.vs_ok = sem("vs_ok")
        q.P_ps = sem("P_ps")
        q.P_evac = sem("P_evac")
        q.st_f_st = sem("st_f_st")
        q.Sscan = sem("Sscan")
        q.T_ps = sem("T_ps")
        q.T_lo_ok = sem("T_lo_ok")
        q.S_hi_ok = sem("S_hi_ok")
        q.S_lo_ok = sem("S_lo_ok")
        q.v_lo_ok = sem("v_lo_ok")
        q.sc_ps = sem("sc_ps")
        q.sm_ok = sem("sm_ok")
        q.sm_hi_ok = sem("sm_hi_ok")
        q.sm_lo_ok = sem("sm_lo_ok")
        q.in_ps = sem("in_ps")
        q.cr_ps = sem("cr_ps")
        q.oa_ok = sem("oa_ok")
        q.ob_ok = sem("ob_ok")
        q.o_ok = sem("o_ok")
        q.gn_s = sem("gn_s")
        q.gn_v = sem("gn_v")
        q.gn_q = sem("gn_q")
        q.gn_r = sem("gn_r")
        q.y_ok = sem("y_ok")
        q.r_ok = sem("r_ok")
        q.rT_ps = sem("rT_ps")
        q.rT_ok = sem("rT_ok")
        q.rT_s0 = sem("rT_s0")
        q.rT_s1 = sem("rT_s1")
        q.g1_in = sem("g1_in")
        q.rc_in = sem("rc_in")
        q.c0_in = sem("c0_in")
        q.r_hi_ok = sem("r_hi_ok")
        q.r_lo_ok = sem("r_lo_ok")
        q.ln_s = sem("ln_s")
        q.ln_mp = sem("ln_mp")
        q.ln_d = sem("ln_d")
        q.ln_sqk = sem("ln_sqk")
        q.ln_acck = sem("ln_acck")
        q.ln_vp = sem("ln_vp")
        q.ln_v = sem("ln_v")
        q.ln_r1 = sem("ln_r1")
        q.ln_z = sem("ln_z")
        q.ln_silu = sem("ln_silu")
        q.c_hi_ok = sem("c_hi_ok")
        q.c_lo_ok = sem("c_lo_ok")
        q.gt_in0 = sem("gt_in0")
        q.gt_in1 = sem("gt_in1")
        q.mr_ps = sem("mr_ps")
        q.mr_evac = sem("mr_evac")
        q.m_hi_ok = sem("m_hi_ok")
        q.m_lo_ok = sem("m_lo_ok")
        q.mo_ps = sem("mo_ps")
        q.mo_ok = sem("mo_ok")
        q.mst_s = sem("mst_s")
        q.mst_v = sem("mst_v")
        q.mst_q = sem("mst_q")
        q.x2_ok = sem("x2_ok")
        q.xn2_ok = sem("xn2_ok")
        q.h2_ps = sem("h2_ps")
        q.h2_f = sem("h2_f")
        q.h2_st = sem("h2_st")
        q.h2s_ok = sem("h2s_ok")
        q.xt_in = sem("xt_in")
        q.xt_st = sem("xt_st")
        q.h2_ld = sem("h2_ld")
        q.B_hi_ok = sem("B_hi_ok")
        q.B_lo_ok = sem("B_lo_ok")
        q.fpad = sem("fpad")
        q.fa_ps = sem("fa_ps")
        q.fg_ps = sem("fg_ps")
        q.fa_ev = sem("fa_ev")
        q.fg_ev = sem("fg_ev")
        q.fa_c0 = sem("fa_c0")
        q.fg_c0 = sem("fg_c0")
        q.fa_c = sem("fa_c")
        q.fg_c = sem("fg_c")
        q.fsilu = sem("fsilu")
        q.fprod = sem("fprod")
        q.gact_hi = sem("gact_hi")
        q.gact_lo = sem("gact_lo")
        q.fd_ps = sem("fd_ps")
        q.y_add = sem("y_add")
        q.x2_in = sem("x2_in")
        q.e_s = sem("e_s")
        q.e_v = sem("e_v")
        q.e_q = sem("e_q")
        q.e_o = sem("e_o")
        q.out_st = sem("out_st")
        wl_in = [sem(f"wl_in{i}") for i in range(4)]
        wr_in = [sem(f"wr_in{i}") for i in range(3)]
        tile_in = [sem(f"tile_in{i}") for i in range(3)]
        x_in = q.x_in0
        ada_in = [q.ada_in0, q.ada_in1]
        conv_st = [q.conv_st0, q.conv_st1]
        gate_st = [q.gate_st0, q.gate_st1]
        qk_st_s = [q.qk_st0, q.qk_st1, q.qk_st2]
        vg_st_s = [q.vg_st0, q.vg_st1, q.vg_st2]
        rT_s = [q.rT_s0, q.rT_s1]
        gt_in = [q.gt_in0, q.gt_in1]

        U_COLS = [(5, 0), (4, 0), (5, 1), (4, 1), (6, 0), (7, 0), (6, 1), (7, 1)]
        M_CHUNKS = 24
        N_L = 64
        N_LM = N_L + NTG * M_CHUNKS

        def f_number(i, role):
            if isinstance(i, int) and i == 0 and role < 2:
                return role
            if isinstance(i, int) and i == FKT // 2 - 1 and role in (2, 3):
                return i * 6 + (role + 2)
            return i * 6 + (role + 4 if role in (2, 3) else role - 2)

        def f_raw(i, role):
            return f_number(i if isinstance(i, int) else 1, role) % 3

        def f_loads(i, role):
            if isinstance(i, int):
                return f_number(i, role) // 3 + 1
            return i * 2 + (1 + (role + 4 if role in (2, 3) else role - 2) // 3)

        def conv_src(g):
            return rc_st if g else conv0

        FIRST, SECOND = (1, 2, 4), (3, 5, 6)

        block = ctx.enter_context(nc.Block())

        @block.sync
        def _(sp):
            r = 0
            for name in ("c", "c_ctx", "norm1_pre", "norm2_pre", "conv_ln_w", "conv_ln_b", "conv_dw_b",
                         "norm1_post", "norm2_post", "ada_b"):
                v = a[name]
                v = (v if len(v.shape) == 1 else v[0]).rearrange("(k p) -> k p", p=P)
                n = v.shape[0]
                if name == "ada_b":
                    assert r == V_ADAB
                sp.dma_start(rows[r:r + n, 0, :], v).then_inc(q.vec_in, 16)
                r += n
            fw = a["ffn_dw_w"][0].rearrange("w (j p) -> (w j) p", p=P)
            fb = a["ffn_dw_b"][0].rearrange("(j p) -> j p", p=P)
            cw = a["conv_dw_w"][0].rearrange("w (k p) -> (w k) p", p=P)
            sp.dma_start(rows[0:88, 1, :], fw[0:88, :]).then_inc(q.vec_in, 16)
            sp.dma_start(rows[0:44, 2, :], fw[88:132, :]).then_inc(q.vec_in, 16)
            sp.dma_start(rows[44:88, 2, :], fb).then_inc(q.vec_in, 16)
            sp.dma_start(rows[0:124, 3, :], cw[0:124, :]).then_inc(q.vec_in, 16)
            sp.dma_start(rows[0:124, 4, :], cw[124:248, :]).then_inc(q.vec_in, 16)
            for m in range(2):
                sp.dma_start(ada_w[:, m, :, :], ada[:, :, m * P:(m + 1) * P]).then_inc(ada_in[m], 16)
            xs = a["x_sample"][0].rearrange("(t p) d -> p t d", p=P)
            sp.dma_start(x_all[:, 0:NL, :], xs).then_inc(x_in, 16)
            sp.dma_start(x_all[:, NL, :], a["x_prompt"][0]).then_inc(x_in, 16)
            for m in range(2, 16):
                sp.wait_ge(q.ada_used, m - 1)
                sp.dma_start(ada_w[:, m % 2, :, :], ada[:, :, m * P:(m + 1) * P]).then_inc(ada_in[m % 2], 16)

            def u_chunk(i, e):
                s, t = U_COLS[e]
                if not (isinstance(i, int) and i == 0 and e < 4):
                    sp.wait_ge(q.w_lo, i * 8 + e - 3)
                sp.dma_start(wraw(e, 4).rearrange("p (k n) -> p k n", k=KT),
                             w_in_p[:, :, bass.ds(i * 256 + (s * 1024 + t * P), P)]).then_inc(wl_in[e % 4], 16)

            for e in range(8):
                u_chunk(0, e)
            with sp.Fori(1, 4) as i:
                for e in range(8):
                    u_chunk(i, e)
            with sp.Fori(0, HEADS) as h:
                for e in range(8):
                    g, j = e // 4, e % 4
                    sp.wait_ge(q.w_lo, h * 8 + (32 + e - 3))
                    for s in range(2):
                        sp.dma_start(wraw(e, 4).rearrange("p (k s n) -> p k s n", k=2, s=2)[:, :, s, :],
                                     w_in_s[:, 2 * j:2 * j + 2, 2 * g + s, bass.ds(h * 256, 256)]).then_inc(wl_in[e % 4], 16)
            def row_of(c):
                return gain_d[c * KT:(c + 1) * KT, :].rearrange("k p -> (k p)").partition_broadcast(P)
            sp.wait_ge(q.gain_c, 1)
            sp.dma_start(gain_d, gmr[:, :]).then_inc(q.gain_st, 16)

            sp.wait_ge(q.qk_evac, NT * HEADS)
            sp.wait_ge(q.vg_evac, NT * HEADS)
            for s_ in qk_st_s + vg_st_s:
                sp.wait_ge(s_, 16 * 3 * HEADS)
            wr, wc, wx = (a[n][0].rearrange("(k p) n -> p k n", p=P) for n in ("ret_w_out", "conv_w_out", "w_mix_out"))
            def m_chunk(n):
                if n == 0:
                    sp.wait_ge(q.w_lo, 64)
                if n >= 3:
                    sp.wait_ge(q.w_lo, N_L + n - 2)
                c = n % M_CHUNKS
                dst = wraw(n, 3)
                if c < 16:
                    w, m = (wr, c) if c < 8 else (wc, c - 8)
                    sp.dma_start(dst.rearrange("p (k n) -> p k n", k=KT), w[:, :, m * P:(m + 1) * P]).then_inc(wr_in[n % 3], 16)
                else:
                    half, j = (c - 16) // 4, (c - 16) % 4
                    sp.dma_start(dst.rearrange("p (k n) -> p k n", k=2),
                                 wx[:, 2 * j:2 * j + 2, half * 512:(half + 1) * 512]).then_inc(wr_in[n % 3], 16)
            for n in range(3):
                m_chunk(n)
            sp.wait_ge(q.gain_st, 16)
            sp.dma_start(tab[:, :], a["shape_table"]).then_inc(q.tab_in, 16)
            for n, name in enumerate(("ret_decay_fwd", "ret_decay_bwd")):
                sp.dma_start(dec[:, n * HEADS:(n + 1) * HEADS], a[name].partition_broadcast(P)).then_inc(q.tab_in, 16)
            def r_loads(h, first):
                for d, (name, slot) in enumerate((("state_ret_fwd", 0), ("state_ret_bwd", NL - 1))):
                    if not first:
                        sp.wait_ge(q.S_lo_ok, h * NL)
                    st = a[name][0, 0].rearrange("h (k p) e -> h p k e", p=P)
                    src = st[0] if first else st[bass.ds(h, 1)].rearrange("o p k e -> (o p) k e")
                    sp.dma_start(S[:, slot, :, d * 256:(d + 1) * 256], src).then_inc(q.s0_in, 16)
                for t in range(0, NT, 3):
                    if not first:
                        sp.wait_ge(q.r_ok, h * NT + (t + 3 - NT))
                    src = qkvg_d[bass.ds(h, 1), t:t + 3].rearrange("o t p n -> p (o t) n")
                    sp.dma_start(qkvg[:, t:t + 3, :, :].rearrange("p t a b -> p t (a b)"), src).then_inc(tile_in[t // 3], 16)

            r_loads(0, True)
            for n in range(3, 6):
                m_chunk(n)
            with sp.Fori(1, HEADS) as h:
                r_loads(h, False)
            sp.wait_ge(q.P_ps, HEADS * NT)
            sp.wait_ge(rT_s[0], 16 * (5 * (HEADS - 1) + 2))
            sp.wait_ge(rT_s[1], 16 * (4 * (HEADS - 1) + 1))
            sp.dma_start(rc_st[:, :, :], rT_d[:, :, 0:TG].rearrange("k p n -> p k n")).then_inc(q.rc_in, 16)
            sp.wait_ge(q.r_ok, HEADS * NT)
            sp.wait_ge(q.rT_ok, HEADS * NT)
            sp.wait_ge(q.st_f_st, 32 * HEADS)
            for s_, n in ((rT_s[0], 5), (rT_s[1], 4)):
                sp.wait_ge(s_, 16 * n * HEADS)
            sp.sem_inc(q.mem_free, 1)
            sp.dma_start(conv0[:, :, :], conv_d[:, :, 0:TG].rearrange("k p n -> p k n")).then_inc(q.c0_in, 16)
            sp.dma_start(g1_row[:, :], row_of(0)).then_inc(q.g1_in, 16)
            for n in range(6, 3 * M_CHUNKS):
                m_chunk(n)

            wu = a["ffn_w_up"][0].rearrange("(k p) n -> p k n", p=P)
            wd = a["ffn_w_down"][0].rearrange("(k p) n -> p k n", p=P)
            def f_chunk(i, role):
                n = f_number(i, role)
                sp.wait_ge(q.w_lo, N_LM + n - 2)
                dst = W_raw[:, f_raw(i, role), :]
                if role in (2, 3):
                    sp.dma_start(dst, wd[:, bass.ds(i * 2 + (role - 2), 1), :].rearrange("p o n -> p (o n)")).then_inc(wr_in[f_raw(i, role)], 16)
                else:
                    p, kind = role // 4, role % 2
                    sp.dma_start(dst.rearrange("p (k n) -> p k n", k=KT),
                                 wu[:, :, bass.ds(i * 256 + (p * P + kind * FF), P)]).then_inc(wr_in[f_raw(i, role)], 16)
            sp.wait_ge(q.h2_st, 16 * 2 * 3)
            sp.wait_ge(q.c_lo_ok, NTG * KT)
            sp.wait_ge(q.m_lo_ok, NTG * KT)
            sp.dma_start(h2_in[:, :, :], h2T_d[:, :, 0:2 * TG].rearrange("k p n -> p k n")).then_inc(q.h2_ld, 16)
            f_chunk(0, 0)
            f_chunk(0, 1)
            f_chunk(0, 4)
            sp.wait_ge(q.x2_ok, NL)
            sp.dma_start(g1_row[:, :], row_of(1)).then_inc(q.g1_in, 16)
            f_chunk(0, 5)
            sp.wait_ge(q.B_lo_ok, KT + 3)
            sp.wait_ge(q.xt_st, 16 * NT)
            sp.sem_inc(q.mem_free, 1)
            with sp.Fori(1, FKT // 2) as i:
                f_chunk(i, 0)
                f_chunk(i, 1)
                f_chunk(i - 1, 2)
                f_chunk(i - 1, 3)
                f_chunk(i, 4)
                f_chunk(i, 5)
            for role in (2, 3):
                f_chunk(FKT // 2 - 1, role)
            sp.wait_ge(q.fg_ps, FKT)
            for t in range(NT):
                sp.dma_start(x2t[:, t, :], x2_d[t]).then_inc(q.x2_in, 16)
            for c in range(2):
                sp.dma_start(g2_row[:, c, :], row_of(2 + c)).then_inc(q.x2_in, 16)
            for t in range(NT):
                sp.wait_ge(q.e_o, t + 1)
                dst = out_xs[0, t * P:(t + 1) * P, :] if t < NL else out_xp[0]
                sp.dma_start(dst, x2t[:, t, :]).then_inc(q.out_st, 16)
            sp.wait_ge(q.out_st, 16 * NT)
            sp.wait_ge(q.st_f_st, 32 * HEADS)

        @block.tensor
        def _(pe):
            def mm(out, l, r, start, stop):
                return pe.matmul(out, l, r, start=start, stop=stop)

            def fm3(out, wh, wl, ah, al, toks):
                wh, wl = (x.rearrange("p (k n) -> p k n", k=KT) for x in (wh, wl))
                for k in range(KT):
                    mm(out, wh[:, k, :], ah[:, k, toks], k == 0, False)
                    mm(out, wh[:, k, :], al[:, k, toks], False, False)
                    last = mm(out, wl[:, k, :], ah[:, k, toks], False, k == KT - 1)
                return last

            pe.wait_ge(q.ident_ok, 3)
            pe.wait_ge(q.vec_in, 16 * 15)
            pe.transpose(ps[:, 7, 0:120], rows[0:120, 0, :], ident[0:120, 0:120]).then_inc(q.vecT, 1)
            pe.transpose(ps[:, 5, 0:88], rows[0:88, 1, :], ident[0:88, 0:88]).then_inc(q.vecT, 1)
            pe.transpose(ps[:, 5, 128:216], rows[0:88, 2, :], ident[0:88, 0:88]).then_inc(q.vecT, 1)
            pe.transpose(ps[:, 4, 0:124], rows[0:124, 3, :], ident[0:124, 0:124]).then_inc(q.vecT, 1)
            pe.transpose(ps[:, 4, 128:252], rows[0:124, 4, :], ident[0:124, 0:124]).then_inc(q.vecT, 1)
            pe.wait_ge(q.cs_ok, 1)
            def ada_unit(slot, col):
                for k in range(KT):
                    last = mm(ps[:, 6, col:col + 2], ada_w[:, slot, k, :], cs[:, k, :], k == 0, k == KT - 1)
                last.then_inc(q.ada_used, 1)
                return last
            for m in range(16):
                pe.wait_ge(ada_in[m % 2], 16 * (m // 2 + 1))
                ada_unit(m % 2, 2 * m)
            for k in range(KT):
                if k == 0:
                    pe.wait_ge(q.xn_ok, NT)
                    pe.wait_ge(q.vec_ok, 5)
                if k >= 2:
                    pe.wait_ge(q.hT_f, k - 1)
                for t in range(NT):
                    last = pe.transpose(ps[:, 3 * (k % 2) + t // 4, (t % 4) * P:(t % 4 + 1) * P],
                                        x_all[:, t, k * P:(k + 1) * P], ident[:, :])
                last.then_inc(q.hT_ps, 1)

            pe.wait_ge(q.hT_f, KT)
            pe.wait_ge(q.mod_ok, 1)
            def u_step(i, e):
                wh, wl = wslot(e, 8)
                pe.wait_ge(q.w_lo, i * 8 + e + 1)
                if not (isinstance(i, int) and e < 2):
                    pe.wait_ge(q.u_evac, i * 8 + e - 1)
                for g in range(NTG):
                    if isinstance(i, int) and e == 0 and g == 0:
                        pe.wait_ge(q.hT_lo, KT)
                    last = fm3(ps[:, 3 * (e % 2) + g, 0:TG], wh, wl, A_hi, A_lo, slice(g * TG, (g + 1) * TG))
                last.then_inc(q.u_ps, 1)
                if e == 0 and not isinstance(i, int):
                    pe.wait_ge(q.adaU_ok, i)
                pe.wait_ge(ada_in[e % 2], i * 64 + (16 * (9 + e // 2)))
                ada_unit(e % 2, 2 * e)
            for e in range(8):
                u_step(0, e)
            with pe.Fori(1, 4) as i:
                for e in range(8):
                    u_step(i, e)

            pe.wait_ge(q.u_evac, 32)
            def q_step(h, first):
                for n in range(18):
                    g, t = n // 9, n % 9
                    if n < 6 and not first:
                        pe.wait_ge(q.vg_evac, h * NT + (n - 5))
                    elif 6 <= n < 15:
                        pe.wait_ge(q.qk_evac, h * NT + (n - 5))
                    elif n >= 15:
                        pe.wait_ge(q.vg_evac, h * NT + (n - 14))
                    for k in range(KT):
                        j = 4 * g + k // 2
                        wh, wl = (x.rearrange("p (k n) -> p k n", k=2)[:, k % 2, :] for x in wslot(j, 8))
                        if t == 0 and k % 2 == 0:
                            pe.wait_ge(q.w_lo, h * 8 + (32 + j + 1))
                        tok = slice(t * P, (t + 1) * P)
                        o = ps[:, n % 6, :]
                        mm(o, A_hi[:, k, tok], wh, k == 0, False)
                        mm(o, A_hi[:, k, tok], wl, False, False)
                        last = mm(o, A_lo[:, k, tok], wh, False, k == KT - 1)
                    last.then_inc(q.q_ps, 1)
            q_step(0, True)
            pe.wait_ge(q.mod_ok, 4)
            pe.transpose(ps[0:32, 7, 0:P], gm1[:, :], ident[:, :]).then_inc(q.gain_t, 1)
            with pe.Fori(1, HEADS) as h:
                q_step(h, False)

            pe.wait_ge(q.qk_evac, NT * HEADS)
            pe.wait_ge(q.vg_evac, NT * HEADS)
            def r_head(h, first):
                for c in range(NT):
                    b = 2 * (c % 2)
                    p = c % 2
                    pe.wait_ge(q.kv_lo, h * 2 * NT + (2 * c + 2))
                    if c == 0 and not first:
                        pe.wait_ge(q.rT_ok, h * NT)
                        pe.wait_ge(q.o_ok, h * NT)
                        pe.wait_ge(q.ob_ok, h * NL)
                    if not (first and c < 2):
                        pe.wait_ge(q.P_evac, h * NT + c - 1)
                    for k in range(2):
                        o = ps[:, b + k, :]
                        kh, kl = k_hi[:, p, k * P:(k + 1) * P], k_lo[:, p, k * P:(k + 1) * P]
                        mm(o, kh, vs_hi[:, p, :], True, False)
                        mm(o, kh, vs_lo[:, p, :], False, False)
                        last = mm(o, kl, vs_hi[:, p, :], False, True)
                    last.then_inc(q.P_ps, 1)

                def turn(c):
                    if c % 3 == 0:
                        pe.wait_ge(tile_in[c // 3], h * 16 + 16)
                    if not (first and c < 2):
                        pe.wait_ge(q.T_lo_ok, h * NT + c - 1)
                    for n in range(4):
                        last = pe.transpose(ps[:, 4 + c % 2, n * P:(n + 1) * P],
                                            qkvg[:, c, n // 2, (n % 2) * P:(n % 2 + 1) * P], ident[:, :])
                    last.then_inc(q.T_ps, 1)

                def back(c):
                    pe.wait_ge(q.r_ok, h * NT + c + 1)
                    if not (first and c == 0):
                        pe.wait_ge(q.rT_ok, h * NT + c)
                    for k in range(2):
                        last = pe.transpose(ps[:, 2, k * P:(k + 1) * P], o_r[:, c % 2, k * P:(k + 1) * P], ident[:, :])
                    last.then_inc(q.rT_ps, 1)

                turn(0)
                for c in range(NT):
                    p = c % 2
                    qT = [[x[:, p, k * P:(k + 1) * P] for k in range(2)] for x in (T_hi, T_lo)]
                    kT = [[x[:, p, (2 + k) * P:(3 + k) * P] for k in range(2)] for x in (T_hi, T_lo)]
                    pe.wait_ge(q.T_lo_ok, h * NT + c + 1)
                    if not (first and c == 0):
                        pe.wait_ge(q.sm_ok, h * NT + c)
                    for k in range(2):
                        o = ps[:, 6, 0:P]
                        mm(o, kT[0][k], qT[0][k], k == 0, False)
                        mm(o, kT[0][k], qT[1][k], False, False)
                        last = mm(o, kT[1][k], qT[0][k], False, k == 1)
                    last.then_inc(q.sc_ps, 1)
                    if c + 1 < NT:
                        turn(c + 1)
                    if c < NL:
                        pe.wait_ge(q.S_lo_ok, h * NL + c + 1)
                        if c >= 2:
                            pe.wait_ge(q.ob_ok, h * NL + c - 1)
                        elif c == 0:
                            pe.wait_ge(q.P_evac, h * NT + NT)
                        for k in range(2):
                            o = ps[:, c % 2, :]
                            sh, sl = S_hi[:, p, k * 512:(k + 1) * 512], S_lo[:, p, k * 512:(k + 1) * 512]
                            mm(o, qT[0][k], sh, k == 0, False)
                            mm(o, qT[0][k], sl, False, False)
                            last = mm(o, qT[1][k], sh, False, k == 1)
                        last.then_inc(q.cr_ps, 1)
                    if c >= 2:
                        back(c - 2)
                    pe.wait_ge(q.sm_lo_ok, h * NT + c + 1)
                    pe.wait_ge(q.v_lo_ok, h * NT + c + 1)
                    if c >= 2:
                        pe.wait_ge(q.o_ok, h * NT + c - 1)
                    o = ps[:, 7 if p else 3, 0:256]
                    mm(o, sm_hi[:, p, :], v_hi[:, p, :], True, False)
                    mm(o, sm_hi[:, p, :], v_lo[:, p, :], False, False)
                    mm(o, sm_lo[:, p, :], v_hi[:, p, :], False, True).then_inc(q.in_ps, 1)
                back(NT - 2)
                back(NT - 1)
            r_head(0, True)
            with pe.Fori(1, HEADS) as h:
                r_head(h, False)

            pe.wait_ge(q.rT_ok, HEADS * NT)
            pe.wait_ge(q.o_ok, HEADS * NT)
            def tile(g, which, m):
                hi, lo = ((r_hi, r_lo), (c_hi, c_lo))[which]
                n = g * M_CHUNKS + which * 8 + m
                e = g * 16 + which * 8 + m
                pe.wait_ge(q.w_lo, N_L + n + 1)
                if e >= 2:
                    pe.wait_ge(q.mr_evac, e - 1)
                wh, wl = wslot(n, 6)
                fm3(ps[:, e % 2, 0:TG], wh, wl, hi, lo, slice(0, TG)).then_inc(q.mr_ps, 1)
            def ln_mean(g):
                pe.wait_ge(q.ln_s, g + 1)
                if g > 1:
                    pe.wait_ge(q.h2_f, 6 * (g - 1))
                mm(ps[:, 6, 0:TG], mean_w[:, :], ln_a[:, :], True, True).then_inc(q.ln_mp, 1)
            def ln_var(g):
                pe.wait_ge(q.ln_acck, KT * (g + 1))
                pe.wait_ge(q.ln_d, g + 1)
                mm(ps[:, 6, 0:TG], mean_w[:, :], ln_acc[:, :], True, True).then_inc(q.ln_vp, 1)
            def h2_turns(g, t):
                n = 3 * g + t
                for half in range(2):
                    pe.wait_ge(q.xn2_ok, n + 1)
                    if n:
                        pe.wait_ge(q.h2_f, 2 * n)
                    for k in range(4):
                        kk = 4 * half + k
                        last = pe.transpose(ps[:, 7 - half, k * P:(k + 1) * P], mo[:, t, kk * P:(kk + 1) * P], ident[:, :])
                    last.then_inc(q.h2_ps, 1)
            for g in range(NTG):
                pe.wait_ge(q.r_lo_ok, KT * (g + 1))
                for m in range(KT):
                    tile(g, 0, m)
                    if g == 0 and m == 2:
                        ln_mean(g)
                    if g == 0 and m == 6:
                        ln_var(g)
                    if g and m >= 4 and m < 7:
                        pe.wait_ge(q.ln_v, g + 1)
                        h2_turns(g - 1, m - 4)
                pe.wait_ge(q.c_lo_ok, KT * (g + 1))
                for m in range(KT):
                    tile(g, 1, m)
                for half in range(2):
                    for t in range(3):
                        n = 6 * g + 3 * half + t
                        if n >= 4:
                            pe.wait_ge(q.mo_ok, n - 3)
                        o = ps[:, 2 + n % 4, :]
                        for k in range(KT):
                            cn = g * M_CHUNKS + 16 + half * 4 + k // 2
                            if t == 0:
                                pe.wait_ge(q.w_lo, N_L + cn + 1)
                            if half == 0 and t == 0:
                                pe.wait_ge(q.m_lo_ok, KT * g + k + 1)
                            wh, wl = (x.rearrange("p (k n) -> p k n", k=2)[:, k % 2, :] for x in wslot(cn, 6))
                            tok = slice(t * P, (t + 1) * P)
                            mm(o, m_hi[:, k, tok], wh, k == 0, False)
                            mm(o, m_hi[:, k, tok], wl, False, False)
                            last = mm(o, m_lo[:, k, tok], wh, False, k == KT - 1)
                        last.then_inc(q.mo_ps, 1)
                        if g + 1 < NTG and (half, t) == (0, 1):
                            ln_mean(g + 1)
                        if g + 1 < NTG and (half, t) == (1, 2):
                            ln_var(g + 1)

            def up(i, p, kind, groups=range(NTG), first=False):
                role = 4 * p + kind
                wh, wl = W_hi[:, role, :], W_lo[:, role, :]
                pe.wait_ge(q.w_lo, N_LM + 1 + f_number(i, role))
                if not first:
                    pe.wait_ge((q.fa_ev, q.fg_ev)[kind], i * 2 + p)
                for g in groups:
                    last = fm3(ps[:, 3 * kind + g, 0:TG], wh, wl, B_hi, B_lo, slice(g * TG, (g + 1) * TG))
                if NTG - 1 in groups:
                    last.then_inc((q.fa_ps, q.fg_ps)[kind], 1)
            def down(i, first=False):
                w = [(W_hi[:, role, :], W_lo[:, role, :]) for role in (2, 3)]
                pe.wait_ge(q.w_lo, N_LM + 1 + f_number(i, 3))
                pe.wait_ge(q.gact_lo, i * 2 + 2)
                for n in range(2 * NT):
                    t, half = n // 2, n % 2
                    if not (first and n < 2):
                        pe.wait_ge(q.y_add, i * 2 * NT + (n - 1))
                    o = ps[:, 6 + half, :]
                    tok, col = slice(t * P, (t + 1) * P), slice(half * 512, (half + 1) * 512)
                    for p in range(2):
                        wh, wl = w[p]
                        mm(o, g_hi[:, p, tok], wh[:, col], p == 0, False)
                        mm(o, g_hi[:, p, tok], wl[:, col], False, False)
                        last = mm(o, g_lo[:, p, tok], wh[:, col], False, p == 1)
                    last.then_inc(q.fd_ps, 1)
            pe.wait_ge(q.ln_v, NTG)
            pe.wait_ge(q.mr_evac, 16 * NTG)
            pe.wait_ge(q.mo_ok, 6 * NTG)
            h2_turns(NTG - 1, 0)
            pe.wait_ge(q.B_lo_ok, KT)
            up(0, 0, 0, (0,), True)
            h2_turns(NTG - 1, 1)
            up(0, 0, 0, (1,), True)
            h2_turns(NTG - 1, 2)
            up(0, 0, 1, (0, 1), True)
            pe.wait_ge(q.B_lo_ok, KT + 3)
            up(0, 0, 0, (2,), True)
            up(0, 0, 1, (2,), True)
            up(0, 1, 0)
            up(0, 1, 1)
            pe.wait_ge(q.h2_f, 2 * NT)
            def pair(i, first):
                up(i, 0, 0)
                up(i, 0, 1)
                down(i - 1, first)
                up(i, 1, 0)
                up(i, 1, 1)
            pair(1, True)
            with pe.Fori(2, FKT // 2) as i:
                pair(i, False)
            down(FKT // 2 - 1)

        @block.scalar
        def _(act):
            def copy(dst, src):
                return act.activation(dst, src, ACT.Copy)

            act.wait_ge(q.vec_ok, 1)
            act.activation(cs[:, :, :].rearrange("p k c -> p c k"),
                           V0[:, 0:16].rearrange("p (c k) -> p c k", c=2), ACT.Silu).then_inc(q.cs_ok, 1)
            for t in range(NT):
                act.wait_ge(x_in, 32)
                if t:
                    act.wait_ge(q.ssq_ok, t)
                act.activation(hf[:, 0:D], x_all[:, t, :], ACT.Square, accum_out=ssq[:, t:t + 1]).then_inc(q.ssq_ok, 1)
            act.wait_ge(q.rstd_a, 1)
            act.activation(ssq[:, :], rst[:, :], ACT.Sqrt).then_inc(q.rstd_b, 1)
            act.wait_ge(q.mod_ok, 2)
            for k in range(KT):
                act.wait_ge(q.hT_ps, k + 1)
                if k:
                    act.wait_ge(q.hT_lo, k)
                b = 3 * (k % 2)
                act.activation(hf[:, 0:LAT].rearrange("p (b n) -> p b n", b=2), ps[:, b:b + 2, :], ACT.Identity,
                               bias=mod[:, SH1 * KT + k, 0:1], scale=hscale[:, k, 0:1])
                act.activation(hf[:, LAT:T], ps[:, b + 2, 0:P], ACT.Identity,
                               bias=mod[:, SH1 * KT + k, 1:2], scale=hscale[:, k, 1:2]).then_inc(q.hT_f, 1)

            def split_w(n, per, used=None):
                act.wait_ge(wl_in[n % 4], per)
                if used is not None:
                    act.wait_ge(*used)
                copy(wslot(n, 8)[0], wraw(n, 4)).then_inc(q.w_hi, 1)

            for n in range(4):
                split_w(n, 16)

            def ada_load(i, e):
                act.wait_ge(q.ada_used, i * 8 + e + 15)
                act.dma_start(ada_w[:, e % 2, :, :], ada[:, :, bass.ds(i * 1024 + (16 + e) * P, P)]).then_inc(ada_in[e % 2], 16)
            def u_step(i, e):
                s, t = U_COLS[e]
                act.wait_ge(q.u_ps, i * 8 + e + 1)
                src = ps[:, 3 * (e % 2):3 * (e % 2) + 3, 0:TG]
                v3 = lambda x: x.rearrange("p (b n) -> p b n", b=3)
                first = isinstance(i, int)
                if s == 5:
                    if not (first and t == 0):
                        act.wait_ge(q.u_ok, i * 2 + t)
                    act.activation(v3(sig[:, :]), src, ACT.Sigmoid).then_inc(q.u_evac, 1)
                elif s == 4:
                    act.activation(v3(u_a[:, :]), src, ACT.Copy).then_inc(q.u_evac, 1)
                else:
                    if not (first and t == 0):
                        act.wait_ge(gate_st[s - 6], i * 32 + 16 * t)
                    act.activation(v3(gates[:, s - 6, :]), src, ACT.Sigmoid).then_inc(q.u_evac, 1)
                    act.wait_ge(q.u_evac, i * 8 + e + 1)
                    act.dma_start(gate_d[s - 6, bass.ds(i * 2 + t, 1)].rearrange("o p n -> (o p) n"), gates[:, s - 6, :]).then_inc(gate_st[s - 6], 16)
                if e + 2 < 8:
                    ada_load(i, e + 2)
                else:
                    if not (isinstance(i, int) and i == 3):
                        ada_load(i + 1, e - 6)
                n = e + 4
                if first and i == 0 and n < 8:
                    used = None
                else:
                    used = (q.u_ps, i * 8 + n - 7)
                per = (i * 32) + 16 * (n // 4 + 1)
                if isinstance(i, int) and i == 3 and n >= 8:
                    per = 16 * (8 + 0) + 32
                split_w(n, per, used)
                if e == 7:
                    act.wait_ge(q.ada_used, i * 8 + 24)
                    copy(mod[:, bass.ds(i * 8 + 16, 8), :].rearrange("p k c -> p (k c)"), ps[:, 6, 0:16]).then_inc(q.adaU_ok, 1)
            for n in range(2):
                ada_load(0, n)
            for e in range(8):
                u_step(0, e)
            with act.Fori(1, 3) as i:
                for e in range(8):
                    u_step(i, e)
            for e in range(8):
                u_step(3, e)

            act.wait_ge(q.conv_step, CW * KT)
            for s_ in conv_st + gate_st:
                act.wait_ge(s_, 16 * KT)
            act.dma_start(rope[:, :, :, :], a["rope_table"].rearrange("t p (c n) -> p t c n", c=2)).then_inc(q.rope_in, 16)
            act.dma_start(gn_row[:, :], a["ret_gn_w"][0].partition_broadcast(P)).then_inc(q.rope_in, 16)
            def w_q(h, n, first):
                per = h * 64 + (16 * 8 + 32 * (n // 4 + 1))
                used = (q.u_ps, 32) if (first and n < 8) else (q.q_ps, h * 18 + ((n - 4) // 4) * 9)
                split_w(n, per, used)
            def q_step(h, first, last):
                for t in range(NT):
                    if t < 4:
                        w_q(h, 4 + t, first)
                    act.wait_ge(q.rope_ok, h * NT + t + 1)
                    act.dma_start(qkvg_d[bass.ds(h, 1), t, :, 0:512].rearrange("o p n -> (o p) n"),
                                  qk_st[:, t % 3, :]).then_inc(qk_st_s[t % 3], 16)
                def vg_store(t):
                    act.wait_ge(q.vg_ok, h * NT + t + 1)
                    act.dma_start(qkvg_d[bass.ds(h, 1), t, :, 512:1024].rearrange("o p n -> (o p) n"),
                                  vg_st[:, t % 3, :]).then_inc(vg_st_s[t % 3], 16)
                for t in range(NT):
                    if t < 4 and not last:
                        w_q(h, 8 + t, False)
                    act.wait_ge(q.q_ps, h * 18 + (10 + t))
                    if not (first and t < 3):
                        act.wait_ge(vg_st_s[t % 3], h * 48 + 16 * (t // 3))
                    src = ps[:, (9 + t) % 6, :]
                    copy(vg_st[:, t % 3, 0:256], src[:, 0:256])
                    act.activation(vg_st[:, t % 3, 256:512], src[:, 256:512], ACT.Silu).then_inc(q.vg_evac, 1)
                    if t:
                        vg_store(t - 1)
                vg_store(NT - 1)
            q_step(0, True, False)
            with act.Fori(1, HEADS - 1) as h:
                q_step(h, False, False)
            act.wait_ge(q.gain_t, 1)
            copy(gmr[:, :], ps[0:32, 7, 0:P]).then_inc(q.gain_c, 1)
            q_step(HEADS - 1, False, True)

            act.wait_ge(q.dk_arg, 1)
            act.activation(lgt[:, 1, :], lgt[:, 0, :], ACT.Exp, scale=-1.0).then_inc(q.dk_exp, 1)
            act.wait_ge(q.dk_arg, 7)
            act.activation(dk_c[:, :, :], dk_a[:, :, :], ACT.Exp).then_inc(q.dk_exp, 1)

            def split_m(n):
                if n < 6:
                    act.wait_ge(q.q_ps, 18 * HEADS)
                else:
                    c = (n - 6) % M_CHUNKS
                    g = (n - 6) // M_CHUNKS
                    if c < 16:
                        act.wait_ge(q.mr_ps, g * 16 + c + 1)
                    else:
                        act.wait_ge(q.mo_ps, 6 * g + 3 * ((c - 16) // 4 + 1))
                act.wait_ge(wr_in[n % 3], 16 * (n // 3 + 1))
                copy(wslot(n, 6)[0], wraw(n, 3)).then_inc(q.w_hi, 1)

            def r_head(h, first):
                act.wait_ge(q.hd_ok, h + 1)
                if not first:
                    act.wait_ge(q.mask_ok, h * 2)
                for d in range(2):
                    ins = act.activation(mtmp[:, d, :], tab[:, NPOS + d * P:NPOS + (d + 1) * P], ACT.Exp,
                                         scale=hd[:, 6 + d:7 + d])
                ins.then_inc(q.mexp, 1)
                for c in range(NT):
                    p = c % 2
                    act.wait_ge(tile_in[c // 3], h * 16 + 16)
                    if not (first and c < 2):
                        act.wait_ge(q.P_ps, h * NT + c - 1)
                    copy(k_hi[:, p, :], qkvg[:, c, 1, :]).then_inc(q.kv_hi, 1)
                    act.wait_ge(q.vs_ok, h * NT + c + 1)
                    copy(vs_hi[:, p, :], vs[:, p, :]).then_inc(q.kv_hi, 1)
                    if c >= 1:
                        state_evac(h, c - 1, first)
                state_evac(h, NT - 1, first)
                def prep(c):
                    p = c % 2
                    act.wait_ge(q.T_ps, h * NT + c + 1)
                    if not (first and c < 2):
                        act.wait_ge(q.in_ps, h * NT + c - 1)
                    copy(T_hi[:, p, :], ps[:, 4 + p, :]).then_inc(q.Tv_hi, 1)
                    copy(v_hi[:, p, :], qkvg[:, c, 2, :]).then_inc(q.Tv_hi, 1)
                    if c < NL:
                        act.wait_ge(q.Sscan, h * 14 + (14 - c))
                        copy(S_hi[:, p, :].rearrange("p (k n) -> p k n", k=2), S[:, c, :, :]).then_inc(q.S_hi_ok, 1)
                prep(0)
                for c in range(NT):
                    p = c % 2
                    act.wait_ge(q.sm_ok, h * NT + c + 1)
                    copy(sm_hi[:, p, :], sm[:, p, :]).then_inc(q.sm_hi_ok, 1)
                    if c + 1 < NT:
                        prep(c + 1)
                    if c < NL:
                        act.wait_ge(q.cr_ps, h * NL + c + 1)
                        if c >= 2:
                            act.wait_ge(q.ob_ok, h * NL + c - 1)
                        act.activation(o_a[:, p, :], ps[:, p, 0:256], ACT.Copy, scale=hd[:, 0:1]).then_inc(q.oa_ok, 1)
                    if c >= 1:
                        out_part(h, c - 1, first)
                out_part(h, NT - 1, first)

            def state_evac(h, c, first):
                b = 2 * (c % 2)
                act.wait_ge(q.P_ps, h * NT + c + 1)
                if c < NL:
                    src = ps[:, b:b + 2, :]
                    ins = None
                    if c == 0:
                        act.wait_ge(q.s0_in, h * 32 + 32)
                    if c < NL - 1:
                        ins = copy(S[:, c + 1, :, 0:256], src[:, :, 0:256])
                    if c > 0:
                        ins = copy(S[:, c - 1, :, 256:512], src[:, :, 256:512])
                    ins.then_inc(q.P_evac, 1)
                else:
                    if not first:
                        act.wait_ge(q.st_f_st, h * 32)
                    copy(st_out[:, :, :, :], ps[:, b:b + 2, :].rearrange("p k (d e) -> p d k e", d=2)).then_inc(q.P_evac, 1)
                    act.wait_ge(q.P_evac, h * NT + NT)
                    for d, dst in enumerate((out_sf, out_sb)):
                        act.dma_start(dst[0, 0, bass.ds(h, 1)].rearrange("o (k p) e -> p (o k) e", p=P),
                                      st_out[:, d, :, :]).then_inc(q.st_f_st, 16)

            def out_part(h, c, first):
                p = c % 2
                act.wait_ge(q.gn_v, h * NT + c + 1)
                act.activation(gstd[:, p, 1:2], gstd[:, p, 0:1], ACT.Sqrt).then_inc(q.gn_q, 1)
                if c >= 1:
                    rT_out(h, c - 1, first)
                if c == NT - 1:
                    rT_out(h, c, first)

            def rT_out(h, c, first):
                p = c % 2
                act.wait_ge(q.rT_ps, h * NT + c + 1)
                if not (first and c < 2):
                    act.wait_ge(rT_s[p], rt_count(h, c))
                copy(rT_st[:, p, :, :].rearrange("p k n -> p (k n)"), ps[:, 2, 0:256]).then_inc(q.rT_ok, 1)
                act.wait_ge(q.rT_ok, h * NT + c + 1)
                act.dma_start(rT_d[bass.ds(h * 2, 2), :, c * P:(c + 1) * P].rearrange("k p n -> p k n"),
                              rT_st[:, p, :, :]).then_inc(rT_s[p], 16)

            def rt_count(h, c):
                per = 5 if c % 2 == 0 else 4
                return h * (16 * per) + 16 * (c // 2)
            for n in range(6):
                split_m(n)
            r_head(0, True)
            with act.Fori(1, HEADS) as h:
                r_head(h, False)

            act.wait_ge(q.mem_free, 1)

            def rc_load(g, which):
                if which:
                    act.wait_ge(q.r_lo_ok, KT * (g + 1))
                elif g:
                    act.wait_ge(q.c_lo_ok, KT * g)
                src = (rT_d, conv_d)[which][:, :, g * TG:(g + 1) * TG]
                act.dma_start(rc_st[:, :, :], src.rearrange("k p n -> p k n")).then_inc(q.rc_in, 16)
            def gate_load(e):
                if e >= 16 * NTG or e % 2:
                    return
                g, w, m = e // 16, (e // 8) % 2, e % 8
                if e >= 4:
                    act.wait_ge(q.mr_evac, e - 2)
                act.dma_start(gate_t[:, e % 4:e % 4 + 2, :],
                              gate_d[w, m:m + 2, :, g * TG:(g + 1) * TG].rearrange("m p n -> p m n")).then_inc(gt_in[(e // 2) % 2], 16)
            def r_hi_part(g):
                act.wait_ge(q.rc_in, 32 * g if g else 16)
                if g:
                    act.wait_ge(q.mr_ps, 16 * (g - 1) + 8)
                for k in range(KT):
                    copy(r_hi[:, k, :], rc_st[:, k, :]).then_inc(q.r_hi_ok, 1)
            def squares(g):
                act.wait_ge(q.ln_d, g + 1)
                for k in range(KT):
                    n = g * KT + k
                    if n >= 2:
                        act.wait_ge(q.ln_acck, n - 1)
                    act.activation(ln_sq[:, n % 2, :], conv_src(g)[:, k, :], ACT.Square).then_inc(q.ln_sqk, 1)
            def c_hi_part(g):
                act.wait_ge(q.ln_z, g + 1)
                for k in range(KT):
                    act.activation(conv_src(g)[:, k, :], conv_src(g)[:, k, :], ACT.Silu, bias=V0[:, V_LNB + k:V_LNB + k + 1],
                                   scale=V0[:, V_LNW + k:V_LNW + k + 1]).then_inc(q.ln_silu, 1)
                if g:
                    act.wait_ge(q.mr_ps, 16 * g)
                for k in range(KT):
                    act.wait_ge(q.ln_silu, g * KT + k + 1)
                    copy(c_hi[:, k, :], conv_src(g)[:, k, :]).then_inc(q.c_hi_ok, 1)
            def xt_load(g):
                if g:
                    act.wait_ge(q.xt_st, 48 * g)
                    act.wait_ge(q.xn2_ok, 3 * g)
                if g < NTG - 1:
                    act.dma_start(xt[:, :, :], a["x_sample"][0, g * TG:(g + 1) * TG, :].rearrange("(t p) d -> p t d", p=P)).then_inc(q.xt_in, 16)
                else:
                    act.dma_start(xt[:, 0:2, :], a["x_sample"][0, g * TG:LAT, :].rearrange("(t p) d -> p t d", p=P)).then_inc(q.xt_in, 16)
                    act.dma_start(xt[:, 2, :], a["x_prompt"][0]).then_inc(q.xt_in, 16)
            def tail_step(g, m):
                if 0 <= m - 3 < 3:
                    t = m - 3
                    act.wait_ge(q.mst_v, 6 * g + SECOND[t])
                    act.activation(mst[:, t, 6:7], mst[:, t, 5:6], ACT.Sqrt).then_inc(q.mst_q, 1)
                if 0 <= m - 2 < 3:
                    t = m - 2
                    act.wait_ge(q.x2_ok, 3 * g + t + 1)
                    act.dma_start(x2_d[3 * g + t], xt[:, t, :]).then_inc(q.xt_st, 16)
                    act.wait_ge(q.mst_s, 6 * g + SECOND[t] - 1)
                    act.activation(sq_junk[:, :], xt[:, t, :], ACT.Square, accum_out=mst[:, t, 4:5]).then_inc(q.mst_s, 1)
                if 0 <= m - 1 < 3:
                    t = m - 1
                    act.wait_ge(q.mst_v, 6 * g + FIRST[t])
                    act.activation(mst[:, t, 2:3], mst[:, t, 1:2], ACT.Sqrt).then_inc(q.mst_q, 1)
                if m < 3:
                    t = m
                    act.wait_ge(q.mo_ok, 6 * g + 4 + t)
                    if g or t:
                        act.wait_ge(q.mst_s, 6 * g + FIRST[t] - 1)
                    act.activation(sq_junk[:, :], mo[:, t, :], ACT.Square, accum_out=mst[:, t, 0:1]).then_inc(q.mst_s, 1)
            def h2_out(g, t):
                n = 3 * g + t
                cond = 0 if n < NL else 1
                act.wait_ge(q.h2s_ok, 1)
                if 0 < n < 3 * NTG - 2:
                    act.wait_ge(q.h2_st, 16 * n)
                elif n:
                    act.wait_ge(q.B_lo_ok, KT + t)
                for half in range(2):
                    act.wait_ge(q.h2_ps, 2 * n + half + 1)
                    for k in range(4):
                        kk = 4 * half + k
                        ins = act.activation(h2o[:, kk, :], ps[:, 7 - half, k * P:(k + 1) * P], ACT.Identity,
                                             bias=mod[:, SH2 * KT + kk, cond:cond + 1], scale=h2s[:, kk, cond:cond + 1])
                    ins.then_inc(q.h2_f, 1)
                act.wait_ge(q.h2_f, 2 * n + 2)
                if g < NTG - 1:
                    act.dma_start(h2T_d[:, :, n * P:(n + 1) * P].rearrange("k p n -> p k n"), h2o[:, :, :]).then_inc(q.h2_st, 16)
                else:
                    copy(B_hi[:, :, n * P:(n + 1) * P], h2o[:, :, :]).then_inc(q.B_hi_ok, 1)

            split_to = [6]
            def more_w(upto):
                while split_to[0] < min(upto, 3 * M_CHUNKS):
                    split_m(split_to[0])
                    split_to[0] += 1
            r_hi_part(0)
            for e in range(4):
                gate_load(e)
            def ln_root(g):
                act.wait_ge(q.ln_v, g + 1)
                act.activation(ln_a[:, :], ln_acc[:, :], ACT.Sqrt).then_inc(q.ln_r1, 1)
            def B_part(ks):
                act.wait_ge(q.h2_ld, 16)
                for k in ks:
                    copy(B_hi[:, k, 0:2 * TG], h2_in[:, k, :]).then_inc(q.B_hi_ok, 1)
            def split_f(i, role, used=None):
                if used is not None:
                    act.wait_ge(*used)
                slot = f_raw(i, role)
                act.wait_ge(wr_in[slot], (f_loads(i, role) + NTG * M_CHUNKS // 3) * 16)
                copy(W_hi[:, role, :], W_raw[:, slot, :]).then_inc(q.w_hi, 1)
            for g in range(NTG):
                for m in range(KT):
                    e = g * 16 + m
                    act.wait_ge(q.mr_evac, e + 1)
                    gate_load(e + 3)
                    more_w(g * M_CHUNKS + m + 7)
                    if g == 0 and m == 3:
                        squares(g)
                    if g == 0 and m == 6:
                        ln_root(g)
                    if g == 0 and m == 7:
                        c_hi_part(g)
                    if g and m == 1:
                        c_hi_part(g)
                    if g and m < 6:
                        tail_step(g - 1, m)
                    if g and m >= 4 and m < 7:
                        h2_out(g - 1, m - 4)
                for m in range(KT):
                    e = g * 16 + 8 + m
                    act.wait_ge(q.mr_evac, e + 1)
                    if g and m == 0:
                        act.wait_ge(q.mo_ps, 6 * g)
                    copy(m_hi[:, m, :], m_part[:, m, :]).then_inc(q.m_hi_ok, 1)
                    gate_load(e + 3)
                    more_w(g * M_CHUNKS + 8 + m + 7)
                    if m == 1 and g + 1 < NTG:
                        rc_load(g + 1, 0)
                    if m == 4 and g + 1 < NTG:
                        r_hi_part(g + 1)
                    if m == 6 and g + 1 < NTG:
                        rc_load(g + 1, 1)
                xt_load(g)
                for n in range(6):
                    half, t = n // 3, n % 3
                    act.wait_ge(q.mo_ps, 6 * g + n + 1)
                    if g:
                        act.wait_ge(q.h2_ps, 6 * g)
                    copy(mo[:, t, half * 512:(half + 1) * 512], ps[:, 2 + (6 * g + n) % 4, :]).then_inc(q.mo_ok, 1)
                    if n == 2:
                        more_w(g * M_CHUNKS + 26)
                    if g + 1 < NTG and n == 3:
                        squares(g + 1)
                    if g == NTG - 1 and n >= 3:
                        tail_step(g, n - 3)
                more_w(g * M_CHUNKS + 30)
                if g + 1 < NTG:
                    ln_root(g + 1)
            split_f(0, 0, (q.mo_ps, 6 * NTG))
            tail_step(NTG - 1, 3)
            B_part(range(0, 4))
            tail_step(NTG - 1, 4)
            B_part(range(4, KT))
            tail_step(NTG - 1, 5)
            h2_out(NTG - 1, 0)
            split_f(0, 1)
            h2_out(NTG - 1, 1)
            h2_out(NTG - 1, 2)
            split_f(0, 4)
            split_f(0, 5)

            def f_step(i, p, first=False):
                for kind in range(2):
                    ev, c0, cv = ((q.fa_ev, q.fa_c0, q.fa_c), (q.fg_ev, q.fg_c0, q.fg_c))[kind]
                    act.wait_ge((q.fa_ps, q.fg_ps)[kind], i * 2 + p + 1)
                    if not first:
                        act.wait_ge(cv, i * 4 + 2 * p)
                    b = 3 * kind
                    copy(f_in[:, kind, 1:1 + 2 * TG].rearrange("p (b n) -> p b n", b=2), ps[:, b:b + 2, 0:TG])
                    copy(f_in[:, kind, 1 + 2 * TG:1 + LAT], ps[:, b + 2, 0:LAT - 2 * TG])
                    copy(f_in[:, kind, 2 + LAT:2 + T], ps[:, b + 2, LAT - 2 * TG:TG]).then_inc(ev, 1)
                    act.wait_ge(ev, i * 2 + p + 1)
                    if not first:
                        act.wait_ge((q.gact_lo, q.fprod)[kind], i * 2 + p)
                    act.activation(f_cv[:, kind, :], f_in[:, kind, 1:1 + F_OUT], ACT.Identity,
                                   bias=VF[:, bass.ds(i * 2 + (6 * FKT + kind * FKT + p), 1)],
                                   scale=VF[:, bass.ds(i * 2 + (2 * FKT + kind * FKT + p), 1)]).then_inc(c0, 1)
                    if kind == 0:
                        act.wait_ge(q.fa_c, i * 4 + (2 * p + 2))
                        act.activation(f_cv[:, 0, :], f_cv[:, 0, :], ACT.Silu).then_inc(q.fsilu, 1)
            def f_hi(i, p, first):
                act.wait_ge(q.fprod, i * 2 + p + 1)
                if not first:
                    act.wait_ge(q.fd_ps, i * 2 * NT)
                for d0, s0, n_ in ((0, 0, LAT), (LAT, LAT + 1, CTX)):
                    ins = copy(g_hi[:, p, d0:d0 + n_], f_cv[:, 0, s0:s0 + n_])
                ins.then_inc(q.gact_hi, 1)
            def f_pair(i, first, last):
                f_step(i, 0, first)
                if not last:
                    split_f(i + 1, 0, (q.fa_ps, i * 2 + 1))
                    split_f(i + 1, 1, (q.fg_ps, i * 2 + 1))
                for role in (2, 3):
                    split_f(i, role, None if first else (q.fd_ps, i * 2 * NT))
                f_hi(i, 0, first)
                f_step(i, 1)
                if not last:
                    split_f(i + 1, 4, (q.fa_ps, i * 2 + 2))
                    split_f(i + 1, 5, (q.fg_ps, i * 2 + 2))
                f_hi(i, 1, first)
            act.wait_ge(q.mem_free, 2)
            act.wait_ge(q.fpad, 1)
            f_pair(0, True, False)
            with act.Fori(1, FKT // 2 - 1) as i:
                f_pair(i, False, False)
            f_pair(FKT // 2 - 1, False, True)

            act.wait_ge(q.fg_ps, FKT)
            act.wait_ge(q.fd_ps, 2 * NT * (FKT // 2 - 1))
            for t in range(NT):
                act.wait_ge(q.y_add, 2 * NT * (FKT // 2 - 1) + 2 * t + 2)
                if t:
                    act.wait_ge(q.e_s, t)
                act.activation(ej[:, :], y_acc[:, t, :], ACT.Square, accum_out=est[:, t, 0:1]).then_inc(q.e_s, 1)
                if t:
                    act.wait_ge(q.e_v, t)
                    act.activation(est[:, t - 1, 2:3], est[:, t - 1, 1:2], ACT.Sqrt).then_inc(q.e_q, 1)
            act.wait_ge(q.e_v, NT)
            act.activation(est[:, NT - 1, 2:3], est[:, NT - 1, 1:2], ACT.Sqrt).then_inc(q.e_q, 1)

        @block.gpsimd
        def _(pool):
            def sub(dst, x, hi):
                return pool.tensor_tensor(dst, x, Fv(hi), ALU.subtract)

            pool.memset(ident[:, :], 0.0).then_inc(q.ident_ok, 1)
            pool.memset(mean_w[:, :], 1.0 / D).then_inc(q.ident_ok, 1)
            pool.wait_ge(q.ident_ok, 2)
            pool.affine_select(out=ident[:, :], in_=ident[:, :], compare_op=ALU.not_equal, fill=1.0, base=0,
                               pattern=[[-1, P]], channel_multiplier=1).then_inc(q.ident_ok, 1)

            def lo_w(n, ring, rawring, count):
                pool.wait_ge(q.w_hi, count)
                h_, l_ = wslot(n, ring)
                sub(l_, wraw(n, rawring), h_).then_inc(q.w_lo, 1)

            for n in range(4):
                lo_w(n, 8, 4, n + 1)
            pool.wait_ge(q.hT_lo, KT)
            pool.memset(u_in[:, :, :], 0.0).then_inc(q.pads_ok, 1)
            pool.wait_ge(q.pads_ok, 1)
            def conv_store(i, t):
                for c0, y0, n in ((0, 0, LAT), (LAT, LAT + HALO, CTX)):
                    pool.dma_start(conv_d[bass.ds(i * 2 + t, 1), :, c0:c0 + n].rearrange("o p n -> (o p) n"),
                                   conv_y[:, t, y0:y0 + n]).then_inc(conv_st[t], 16)
            def u_step(i, e):
                s, t = U_COLS[e]
                if s == 4:
                    pool.wait_ge(q.u_evac, i * 8 + e + 1)
                    if not (isinstance(i, int) and i == 0):
                        pool.wait_ge(q.conv_step, i * 2 * CW + (t - 1) * CW)
                    pool.tensor_tensor(u_in[:, t, HALO:HALO + LAT], u_a[:, 0:LAT], sig[:, 0:LAT], ALU.mult)
                    pool.tensor_tensor(u_in[:, t, 2 * HALO + LAT:2 * HALO + T], u_a[:, LAT:T], sig[:, LAT:T],
                                       ALU.mult).then_inc(q.u_ok, 1)
                    if not (isinstance(i, int) and i == 0):
                        conv_store(i - 1, t)
                lo_w(e + 4, 8, 4, i * 8 + (e + 5))
            for e in range(8):
                u_step(0, e)
            with pool.Fori(1, 4) as i:
                for e in range(8):
                    u_step(i, e)
            for t in range(2):
                pool.wait_ge(q.conv_step, CW * (KT - 1 + t))
                conv_store(3, t)
            pool.wait_ge(q.rope_in, 32)
            def q_step(h, first, last):
                if not first:
                    pool.wait_ge(q.vg_ok, h * NT)
                for t in range(4):
                    lo_w(4 + t, 8, 4, h * 8 + (32 + 4 + t + 1))
                    if t == 0:
                        pool.tensor_copy(gn_head[:, :], gn_row[:, bass.ds(h * 256, 256)]).then_inc(q.gnh_ok, 1)
                pool.wait_ge(q.gnh_ok, h + 1)
                for t in range(NT):
                    if t < 4 and not last:
                        lo_w(8 + t, 8, 4, h * 8 + (32 + 8 + t + 1))
                    pool.wait_ge(q.vg_evac, h * NT + (t + 1))
                    g_ = vg_st[:, t % 3, 256:512]
                    pool.tensor_tensor(g_, g_, gn_head[:, :], ALU.mult).then_inc(q.vg_ok, 1)
            q_step(0, True, False)
            with pool.Fori(1, HEADS - 1) as h:
                q_step(h, False, False)
            q_step(HEADS - 1, False, True)

            for n in range(6):
                lo_w(n, 6, 3, N_L + n + 1)
            def r_head(h, first):
                for c in range(NT):
                    p = c % 2
                    pool.wait_ge(q.kv_hi, h * 2 * NT + (2 * c + 1))
                    sub(k_lo[:, p, :], qkvg[:, c, 1, :], k_hi[:, p, :]).then_inc(q.kv_lo, 1)
                    pool.wait_ge(q.kv_hi, h * 2 * NT + (2 * c + 2))
                    sub(vs_lo[:, p, :], vs[:, p, :], vs_hi[:, p, :]).then_inc(q.kv_lo, 1)
                def prep(c):
                    p = c % 2
                    pool.wait_ge(q.Tv_hi, h * 2 * NT + (2 * c + 2))
                    sub(v_lo[:, p, :], qkvg[:, c, 2, :], v_hi[:, p, :]).then_inc(q.v_lo_ok, 1)
                    if c < NL:
                        pool.wait_ge(q.S_hi_ok, h * NL + c + 1)
                        sub(S_lo[:, p, :].rearrange("p (k n) -> p k n", k=2), S[:, c, :, :],
                            S_hi[:, p, :].rearrange("p (k n) -> p k n", k=2)).then_inc(q.S_lo_ok, 1)
                def gated(c):
                    pool.wait_ge(q.y_ok, h * NT + c + 1)
                    if not (first and c < 2):
                        pool.wait_ge(q.rT_ps, h * NT + c - 1)
                    pool.tensor_tensor(o_r[:, c % 2, :], o_y[:, c % 2, :], qkvg[:, c, 3, :], ALU.mult).then_inc(q.r_ok, 1)
                prep(0)
                for c in range(NT):
                    pool.wait_ge(q.sm_hi_ok, h * NT + c + 1)
                    sub(sm_lo[:, c % 2, :], sm[:, c % 2, :], sm_hi[:, c % 2, :]).then_inc(q.sm_lo_ok, 1)
                    if c + 1 < NT:
                        prep(c + 1)
                    if c >= 1:
                        gated(c - 1)
                gated(NT - 1)
            r_head(0, True)
            with pool.Fori(1, HEADS) as h:
                r_head(h, False)

            split_to = [6]
            def more_w(upto):
                while split_to[0] < min(upto, 3 * M_CHUNKS):
                    n = split_to[0]
                    lo_w(n, 6, 3, N_L + n + 1)
                    split_to[0] += 1
            def square_sum(g):
                for k in range(KT):
                    n = g * KT + k
                    pool.wait_ge(q.ln_sqk, n + 1)
                    if k:
                        pool.wait_ge(q.ln_acck, n)
                        pool.tensor_tensor(ln_acc[:, :], ln_acc[:, :], ln_sq[:, n % 2, :], ALU.add).then_inc(q.ln_acck, 1)
                    else:
                        if g:
                            pool.wait_ge(q.ln_z, g)
                        pool.tensor_copy(ln_acc[:, :], ln_sq[:, n % 2, :]).then_inc(q.ln_acck, 1)
            for g in range(NTG):
                for m in range(KT):
                    more_w(g * M_CHUNKS + m + 7)
                    if g == 0 and m == 3:
                        square_sum(g)
                for m in range(KT):
                    pool.wait_ge(q.m_hi_ok, g * KT + m + 1)
                    sub(m_lo[:, m, :], m_part[:, m, :], m_hi[:, m, :]).then_inc(q.m_lo_ok, 1)
                    more_w(g * M_CHUNKS + 8 + m + 7)
                more_w(g * M_CHUNKS + 26)
                if g + 1 < NTG:
                    square_sum(g + 1)
                more_w(g * M_CHUNKS + 30)

            def lo_f(i, role):
                pool.wait_ge(q.w_hi, N_LM + 1 + f_number(i, role))
                sub(W_lo[:, role, :], W_raw[:, f_raw(i, role), :], W_hi[:, role, :]).then_inc(q.w_lo, 1)
            for role in (0, 1, 4, 5):
                lo_f(0, role)
            pool.wait_ge(q.mem_free, 2)
            pool.memset(f_in[:, :, :], 0.0).then_inc(q.fpad, 1)
            for t in range(NT):
                ins = pool.memset(y_acc[:, t, :], 0.0)
            ins.then_inc(q.fpad, 1)
            def product(i, p):
                pool.wait_ge(q.fg_c, i * 4 + (2 * p + 2))
                pool.wait_ge(q.fsilu, i * 2 + p + 1)
                pool.tensor_tensor(f_cv[:, 0, :], f_cv[:, 0, :], f_cv[:, 1, :], ALU.mult).then_inc(q.fprod, 1)
            def product_lo(i, p):
                pool.wait_ge(q.gact_hi, i * 2 + p + 1)
                for d0, s0, n_ in ((0, 0, LAT), (LAT, LAT + 1, CTX)):
                    ins = sub(g_lo[:, p, d0:d0 + n_], f_cv[:, 0, s0:s0 + n_], g_hi[:, p, d0:d0 + n_])
                ins.then_inc(q.gact_lo, 1)
            def f_pair(i, last):
                product(i, 0)
                if not last:
                    lo_f(i + 1, 0)
                    lo_f(i + 1, 1)
                for role in (2, 3):
                    lo_f(i, role)
                product_lo(i, 0)
                product(i, 1)
                if not last:
                    lo_f(i + 1, 4)
                    lo_f(i + 1, 5)
                product_lo(i, 1)
            f_pair(0, False)
            with pool.Fori(1, FKT // 2 - 1) as i:
                f_pair(i, False)
            f_pair(FKT // 2 - 1, True)

        @block.vector
        def _(dve):
            steps = [0]
            def then(ins):
                steps[0] += 1
                ins.then_inc(q.dve_own, 1)
                dve.wait_ge(q.dve_own, steps[0])

            for n, (dst, src) in enumerate(((V0[:, 0:120], ps[:, 7, 0:120]), (VF[:, 0:88], ps[:, 5, 0:88]),
                                            (VF[:, 88:176], ps[:, 5, 128:216]), (VC[:, 0:124], ps[:, 4, 0:124]),
                                            (VC[:, 124:248], ps[:, 4, 128:252]))):
                dve.wait_ge(q.vecT, 5)
                dve.tensor_copy(dst, src).then_inc(q.vec_ok, 1)
            dve.wait_ge(q.ssq_ok, NT)
            dve.tensor_scalar(rst[:, :], ssq[:, :], 1.0 / D, EPS, ALU.mult, ALU.add).then_inc(q.rstd_a, 1)
            dve.wait_ge(q.rstd_b, 1)
            then(dve.reciprocal(rst[:, :], ssq[:, :]))
            for t in range(NT):
                dve.tensor_scalar(x_all[:, t, :], x_all[:, t, :], rst[:, t:t + 1], None, ALU.mult).then_inc(q.xn_ok, 1)
            def col2(c, n):
                return V0[:, c:c + n].unsqueeze(2).broadcast_to([P, n, 2])
            dve.wait_ge(q.ada_used, 16)
            dve.wait_ge(q.vec_ok, 1)
            dve.tensor_tensor(mod[:, 0:16, :], ps[:, 6, 0:32].rearrange("p (k c) -> p k c", c=2), col2(V_ADAB, 16),
                              ALU.add).then_inc(q.mod_ok, 1)
            dve.wait_ge(q.mod_ok, 1)
            dve.scalar_tensor_tensor(out=hscale[:, :, :], in0=mod[:, SC1 * KT:SC1 * KT + KT, :], scalar=1.0,
                                     in1=col2(V_N1PRE, KT), op0=ALU.add, op1=ALU.mult).then_inc(q.mod_ok, 1)
            for k in range(KT):
                dve.wait_ge(q.hT_f, k + 1)
                then(dve.tensor_copy(A_hi[:, k, :], hf[:, :]))
                dve.tensor_tensor(A_lo[:, k, :], hf[:, :], Fv(A_hi[:, k, :]), ALU.subtract).then_inc(q.hT_lo, 1)

            def conv(i, t):
                first = isinstance(i, int)
                dve.wait_ge(q.u_ok, i * 2 + t + 1)
                if not first:
                    dve.wait_ge(conv_st[t], i * 32)
                y = conv_y[:, t, :]
                for w in range(CW):
                    tap = VC[:, bass.ds(i * 2 + (w * KT + t), 1)]
                    x = u_in[:, t, w:w + U_OUT]
                    if w == 0:
                        dve.tensor_scalar(y, x, tap, V0[:, bass.ds(i * 2 + (V_CDB + t), 1)], ALU.mult, ALU.add).then_inc(q.conv_step, 1)
                    else:
                        dve.wait_ge(q.conv_step, i * 2 * CW + (t * CW + w))
                        dve.scalar_tensor_tensor(out=y, in0=x, scalar=tap, in1=y, op0=ALU.mult, op1=ALU.add).then_inc(q.conv_step, 1)
            for t in range(2):
                conv(0, t)
            with dve.Fori(1, 4) as i:
                for t in range(2):
                    conv(i, t)

            dve.wait_ge(q.rope_in, 32)
            dve.wait_ge(q.adaU_ok, 4)
            dve.tensor_tensor(mod[:, 16:48, :], mod[:, 16:48, :], col2(V_ADAB + 16, 32), ALU.add).then_inc(q.mod_ok, 1)
            dve.wait_ge(q.mod_ok, 3)
            for n, (g_, v) in enumerate(((G1, V_N1POST), (G2, V_N2POST))):
                for c in range(2):
                    ins = dve.tensor_tensor(gm1[:, (2 * n + c) * KT:(2 * n + c + 1) * KT], mod[:, g_ * KT:(g_ + 1) * KT, c],
                                            V0[:, v:v + KT], ALU.mult)
            ins.then_inc(q.mod_ok, 1)
            def q_step(h, first):
                for t in range(NT):
                    src = ps[:, t % 6, :]
                    dst = qk_st[:, t % 3, :]
                    dve.wait_ge(q.q_ps, h * 18 + (t + 1))
                    if not (first and t == 0):
                        dve.wait_ge(q.rope_ok, h * NT + t)
                    if t < NL:
                        q2 = lambda x: x.rearrange("p (s n) -> p s n", s=2)
                        dve.tensor_tensor(q2(rope_c[:, :]), q2(src), rope[:, t, 0, :].unsqueeze(1).broadcast_to([P, 2, 256]), ALU.mult)
                        parts = lambda x: x.rearrange("p (s h a f) -> p s h a f", s=2, h=2, a=2)
                        sn = rope[:, t, 1, :].rearrange("p (h a f) -> p h a f", h=2, a=2)
                        for a_ in range(2):
                            for s_ in range(2):
                                ins = dve.tensor_tensor(parts(rope_s[:, :])[:, s_, :, a_, :], parts(src)[:, s_, :, 1 - a_, :],
                                                        sn[:, :, a_, :], ALU.mult)
                        ins.then_inc(q.qk_evac, 1)
                        dve.wait_ge(q.qk_evac, h * NT + (t + 1))
                        if not (first and t < 3):
                            dve.wait_ge(qk_st_s[t % 3], h * 48 + 16 * (t // 3))
                        dve.tensor_tensor(dst, rope_c[:, :], rope_s[:, :], ALU.add).then_inc(q.rope_ok, 1)
                    else:
                        dve.tensor_copy(rope_c[:, :], src).then_inc(q.qk_evac, 1)
                        dve.wait_ge(q.qk_evac, h * NT + (t + 1))
                        if not (first and t < 3):
                            dve.wait_ge(qk_st_s[t % 3], h * 48 + 16 * (t // 3))
                        dve.tensor_copy(dst, rope_c[:, :]).then_inc(q.rope_ok, 1)
            q_step(0, True)
            with dve.Fori(1, HEADS) as h:
                q_step(h, False)

            dve.wait_ge(q.tab_in, 48)
            dve.scalar_tensor_tensor(out=lgt[:, 0, :], in0=dec[:, :], scalar=-1.0, in1=dec[:, :],
                                     op0=ALU.mult, op1=ALU.max).then_inc(q.dk_arg, 1)
            dve.wait_ge(q.dk_exp, 1)
            e_, d_, z_, zz, p_ = (lgt[:, n, :] for n in range(1, 6))
            then(dve.tensor_scalar(d_, e_, 2.0, None, ALU.add))
            then(dve.reciprocal(z_, d_))
            then(dve.tensor_tensor(z_, z_, e_, ALU.mult))
            then(dve.tensor_tensor(zz, z_, z_, ALU.mult))
            then(dve.tensor_scalar(p_, zz, 1.0 / 15, None, ALU.mult))
            for m in (13, 11, 9, 7, 5, 3):
                then(dve.scalar_tensor_tensor(out=p_, in0=p_, scalar=1.0 / m, in1=zz, op0=ALU.add, op1=ALU.mult))
            then(dve.scalar_tensor_tensor(out=p_, in0=p_, scalar=1.0, in1=z_, op0=ALU.add, op1=ALU.mult))
            then(dve.tensor_scalar(p_, p_, 2.0, None, ALU.mult))
            then(dve.scalar_tensor_tensor(out=lg[:, :], in0=dec[:, :], scalar=0.0, in1=p_, op0=ALU.min, op1=ALU.subtract))
            for n in range(4):
                dve.tensor_scalar(dk_a[:, :, n], lg[:, (n % 2) * HEADS:(n % 2 + 1) * HEADS], tab[:, n:n + 1], None,
                                  ALU.mult).then_inc(q.dk_arg, 1)
            for n in range(2):
                dve.tensor_scalar(dk_a[:, :, 4 + n], lg[:, n * HEADS:(n + 1) * HEADS], float(P), None,
                                  ALU.mult).then_inc(q.dk_arg, 1)
            dve.wait_ge(q.dk_exp, 2)
            then(dve.tensor_scalar(dkt[:, :, 0:2], dk_c[:, :, 0:2], DK ** -0.5, None, ALU.mult))
            then(dve.tensor_copy(dkt[:, :, 2:6], dk_c[:, :, 2:6]))
            then(dve.tensor_copy(dkt[:, :, 6:8], lg[:, :].rearrange("p (d h) -> p h d", d=2)))

            def r_head(h, first):
                if not first:
                    dve.wait_ge(q.oa_ok, h * NL)
                dve.tensor_copy(hd[:, :], dkt[:, bass.ds(h, 1), :].rearrange("p o n -> p (o n)")).then_inc(q.hd_ok, 1)
                dve.wait_ge(q.mexp, h + 1)
                for d in range(2):
                    ins = dve.tensor_tensor(mtmp[:, 2 + d, :], mtmp[:, d, :], tab[:, NPOS + (2 + d) * P:NPOS + (3 + d) * P], ALU.mult)
                ins.then_inc(q.mask_ok, 1)
                dve.wait_ge(q.mask_ok, h * 2 + 1)
                dve.tensor_tensor(mask[:, :], mtmp[:, 2, :], mtmp[:, 3, :], ALU.add).then_inc(q.mask_ok, 1)
                dve.wait_ge(q.mask_ok, h * 2 + 2)

                def fwd(c):
                    dve.wait_ge(q.P_evac, h * NT + c + 1)
                    dve.wait_ge(q.Sscan, h * 14 + c) if c or not first else None
                    dve.scalar_tensor_tensor(out=S[:, c + 1, :, 0:256], in0=S[:, c, :, 0:256], scalar=hd[:, 4:5],
                                             in1=S[:, c + 1, :, 0:256], op0=ALU.mult, op1=ALU.add).then_inc(q.Sscan, 1)
                dve.wait_ge(q.s0_in, h * 32 + 32)
                for c in range(NT):
                    p = c % 2
                    dve.wait_ge(tile_in[c // 3], h * 16 + 16)
                    if not (first and c < 2):
                        dve.wait_ge(q.kv_lo, h * 2 * NT + (2 * c - 2))
                    dve.tensor_scalar(vs[:, p, 0:256], qkvg[:, c, 2, :], hd[:, 2:3], None, ALU.mult)
                    dve.tensor_scalar(vs[:, p, 256:512], qkvg[:, c, 2, :], hd[:, 3:4], None, ALU.mult).then_inc(q.vs_ok, 1)
                    if c >= 2:
                        fwd(c - 2) if c - 2 < NL - 1 else None
                dve.wait_ge(q.P_evac, h * NT + NL)
                for c in range(NL - 2, -1, -1):
                    dve.wait_ge(q.Sscan, h * 14 + (13 - c))
                    dve.scalar_tensor_tensor(out=S[:, c, :, 256:512], in0=S[:, c + 1, :, 256:512], scalar=hd[:, 5:6],
                                             in1=S[:, c, :, 256:512], op0=ALU.mult, op1=ALU.add).then_inc(q.Sscan, 1)

                def t_lo(c):
                    p = c % 2
                    dve.wait_ge(q.Tv_hi, h * 2 * NT + (2 * c + 1))
                    dve.tensor_tensor(T_lo[:, p, :], ps[:, 4 + p, :], Fv(T_hi[:, p, :]), ALU.subtract).then_inc(q.T_lo_ok, 1)
                def finish(c):
                    p = c % 2
                    dve.wait_ge(q.gn_q, h * NT + c + 1)
                    dve.reciprocal(gstd[:, p, 2:3], gstd[:, p, 1:2]).then_inc(q.gn_r, 1)
                    dve.wait_ge(q.gn_r, h * NT + c + 1)
                    if not (first and c < 2):
                        dve.wait_ge(q.r_ok, h * NT + c - 1)
                    dve.tensor_scalar(o_y[:, p, :], o_o[:, p, :], bn2[:, p, 0:1], gstd[:, p, 2:3], ALU.subtract, ALU.mult).then_inc(q.y_ok, 1)
                t_lo(0)
                for c in range(NT):
                    p = c % 2
                    dve.wait_ge(q.sc_ps, h * NT + c + 1)
                    if not (first and c < 2):
                        dve.wait_ge(q.sm_lo_ok, h * NT + c - 1)
                    dve.tensor_tensor(sm[:, p, :], ps[:, 6, 0:P], mask[:, :], ALU.mult).then_inc(q.sm_ok, 1)
                    if c + 1 < NT:
                        t_lo(c + 1)
                    if c < NL:
                        dve.wait_ge(q.oa_ok, h * NL + c + 1)
                        dve.scalar_tensor_tensor(out=o_b[:, p, :], in0=ps[:, p, 256:512], scalar=hd[:, 1:2],
                                                 in1=o_a[:, p, :], op0=ALU.mult, op1=ALU.add).then_inc(q.ob_ok, 1)
                    if c >= 1:
                        finish(c - 1)
                    dve.wait_ge(q.in_ps, h * NT + c + 1)
                    o_ = ps[:, 7 if p else 3, 0:256]
                    if c < NL:
                        dve.wait_ge(q.ob_ok, h * NL + c + 1)
                        dve.tensor_tensor(o_o[:, p, :], o_, o_b[:, p, :], ALU.add).then_inc(q.o_ok, 1)
                    else:
                        dve.tensor_copy(o_o[:, p, :], o_).then_inc(q.o_ok, 1)
                    dve.wait_ge(q.o_ok, h * NT + c + 1)
                    dve.bn_stats(bn6[:, p, :], o_o[:, p, :]).then_inc(q.gn_s, 1)
                    dve.wait_ge(q.gn_s, h * 2 * NT + 2 * c + 1)
                    dve.memset(gstd[:, p, 3:4], 0.0)
                    dve.bn_aggr(bn2[:, p, :], bn6[:, p, :]).then_inc(q.gn_s, 1)
                    dve.wait_ge(q.gn_s, h * 2 * NT + 2 * c + 2)
                    dve.tensor_scalar(gstd[:, p, 0:1], bn2[:, p, 1:2], GN_EPS, None, ALU.add).then_inc(q.gn_v, 1)
                finish(NT - 1)
            r_head(0, True)
            with dve.Fori(1, HEADS) as h:
                r_head(h, False)

            dve.wait_ge(q.mem_free, 1)
            dve.scalar_tensor_tensor(out=h2s[:, :, :], in0=mod[:, SC2 * KT:SC2 * KT + KT, :], scalar=1.0,
                                     in1=col2(V_N2PRE, KT), op0=ALU.add, op1=ALU.mult).then_inc(q.h2s_ok, 1)
            def r_lo_part(g):
                for k in range(KT):
                    dve.wait_ge(q.r_hi_ok, g * KT + k + 1)
                    dve.tensor_tensor(r_lo[:, k, :], rc_st[:, k, :], Fv(r_hi[:, k, :]), ALU.subtract).then_inc(q.r_lo_ok, 1)
            def over_k(x):
                return x.unsqueeze(1).broadcast_to([P, KT, TG])
            def tail_step(g, m):
                if 0 <= m - 3 < 3:
                    t = m - 3
                    dve.wait_ge(q.mst_q, 6 * g + SECOND[t])
                    then(dve.reciprocal(mst[:, t, 7:8], mst[:, t, 6:7]))
                    dve.tensor_scalar(mo[:, t, :], xt[:, t, :], mst[:, t, 7:8], None, ALU.mult).then_inc(q.xn2_ok, 1)
                if 0 <= m - 2 < 3:
                    t = m - 2
                    dve.wait_ge(q.mst_s, 6 * g + SECOND[t])
                    dve.tensor_scalar(mst[:, t, 5:6], mst[:, t, 4:5], 1.0 / D, EPS, ALU.mult, ALU.add).then_inc(q.mst_v, 1)
                if 0 <= m - 1 < 3:
                    t = m - 1
                    n = 3 * g + t
                    dve.wait_ge(q.mst_q, 6 * g + FIRST[t])
                    then(dve.reciprocal(mst[:, t, 3:4], mst[:, t, 2:3]))
                    dve.wait_ge(q.g1_in, 16 if n < NL else 32)
                    then(dve.scalar_tensor_tensor(out=mo[:, t, :], in0=mo[:, t, :], scalar=mst[:, t, 3:4], in1=g1_row[:, :],
                                                  op0=ALU.mult, op1=ALU.mult))
                    dve.wait_ge(q.xt_in, (16, 32, 64)[g])
                    dve.tensor_tensor(xt[:, t, :], xt[:, t, :], mo[:, t, :], ALU.add).then_inc(q.x2_ok, 1)
                if m < 3:
                    dve.wait_ge(q.mst_s, 6 * g + FIRST[m])
                    dve.tensor_scalar(mst[:, m, 1:2], mst[:, m, 0:1], 1.0 / D, EPS, ALU.mult, ALU.add).then_inc(q.mst_v, 1)
            def ln_sum(g):
                if g:
                    dve.wait_ge(q.rc_in, 32 * g + 16)
                else:
                    dve.wait_ge(q.c0_in, 16)
                dve.tensor_reduce(ln_a[:, :], conv_src(g)[:, :, :].rearrange("p k t -> p t k"), AX.X, ALU.add).then_inc(q.ln_s, 1)
            def ln_center(g):
                dve.wait_ge(q.ln_mp, g + 1)
                dve.tensor_tensor(conv_src(g)[:, :, :], conv_src(g)[:, :, :], over_k(ps[:, 6, 0:TG]), ALU.subtract).then_inc(q.ln_d, 1)
            def ln_variance(g):
                dve.wait_ge(q.ln_vp, g + 1)
                dve.tensor_scalar(ln_acc[:, :], ps[:, 6, 0:TG], GN_EPS, None, ALU.add).then_inc(q.ln_v, 1)
            def ln_scale(g):
                dve.wait_ge(q.ln_r1, g + 1)
                then(dve.reciprocal(ln_acc[:, :], ln_a[:, :]))
                dve.tensor_tensor(conv_src(g)[:, :, :], conv_src(g)[:, :, :], over_k(ln_acc[:, :]), ALU.mult).then_inc(q.ln_z, 1)
            def c_lo_part(g):
                for k in range(KT):
                    dve.wait_ge(q.c_hi_ok, g * KT + k + 1)
                    dve.tensor_tensor(c_lo[:, k, :], conv_src(g)[:, k, :], Fv(c_hi[:, k, :]), ALU.subtract).then_inc(q.c_lo_ok, 1)
            r_lo_part(0)
            for g in range(NTG):
                for m in range(KT):
                    e = 16 * g + m
                    dve.wait_ge(q.mr_ps, e + 1)
                    dve.wait_ge(gt_in[(e // 2) % 2], 16 * (e // 4 + 1))
                    if g:
                        dve.wait_ge(q.m_lo_ok, KT * (g - 1) + m + 1)
                    dve.tensor_tensor(m_part[:, m, :], ps[:, e % 2, 0:TG], gate_t[:, e % 4, :], ALU.mult).then_inc(q.mr_evac, 1)
                    if g == 0:
                        if m == 1:
                            ln_sum(g)
                        if m == 3:
                            ln_center(g)
                        if m == 6:
                            ln_variance(g)
                        if m == 7:
                            ln_scale(g)
                            c_lo_part(g)
                    elif m < 6:
                        tail_step(g - 1, m)
                        if m == 2:
                            c_lo_part(g)
                for m in range(KT):
                    e = 16 * g + 8 + m
                    dve.wait_ge(q.mr_ps, e + 1)
                    dve.wait_ge(gt_in[(e // 2) % 2], 16 * (e // 4 + 1))
                    then(dve.tensor_tensor(gate_t[:, e % 4, :], ps[:, e % 2, 0:TG], gate_t[:, e % 4, :], ALU.mult))
                    dve.tensor_tensor(m_part[:, m, :], m_part[:, m, :], gate_t[:, e % 4, :], ALU.add).then_inc(q.mr_evac, 1)
                    if m == 5 and g + 1 < NTG:
                        r_lo_part(g + 1)
                if g + 1 < NTG:
                    ln_sum(g + 1)
                    ln_center(g + 1)
                    ln_variance(g + 1)
                    ln_scale(g + 1)
            def B_part(ks):
                dve.wait_ge(q.h2_ld, 16)
                for k in ks:
                    dve.wait_ge(q.B_hi_ok, k + 1)
                    dve.tensor_tensor(B_lo[:, k, 0:2 * TG], h2_in[:, k, :], Fv(B_hi[:, k, 0:2 * TG]), ALU.subtract).then_inc(q.B_lo_ok, 1)
            for m in range(4):
                tail_step(NTG - 1, m)
            B_part(range(0, 4))
            tail_step(NTG - 1, 4)
            B_part(range(4, KT))
            tail_step(NTG - 1, 5)
            for t in range(3):
                tok = slice((3 * (NTG - 1) + t) * P, (3 * (NTG - 1) + t + 1) * P)
                dve.wait_ge(q.B_hi_ok, KT + t + 1)
                dve.tensor_tensor(B_lo[:, :, tok], h2o[:, :, :], Fv(B_hi[:, :, tok]), ALU.subtract).then_inc(q.B_lo_ok, 1)

            dve.wait_ge(q.fpad, 2)
            def taps(i, p, kind):
                c0, cv = ((q.fa_c0, q.fa_c), (q.fg_c0, q.fg_c))[kind]
                dve.wait_ge(c0, i * 2 + p + 1)
                for n, w in enumerate((0, 2)):
                    if n:
                        dve.wait_ge(cv, i * 4 + (2 * p + 1))
                    dve.scalar_tensor_tensor(out=f_cv[:, kind, :], in0=f_in[:, kind, w:w + F_OUT],
                                             scalar=VF[:, bass.ds(i * 2 + (w * 2 * FKT + kind * FKT + p), 1)],
                                             in1=f_cv[:, kind, :], op0=ALU.mult, op1=ALU.add).then_inc(cv, 1)
            def add_down(i, ns):
                for n in ns:
                    t, half = n // 2, n % 2
                    dve.wait_ge(q.fd_ps, i * 2 * NT + (n + 1))
                    y = y_acc[:, t, half * 512:(half + 1) * 512]
                    dve.tensor_tensor(y, ps[:, 6 + half, :], y, ALU.add).then_inc(q.y_add, 1)
            taps(0, 0, 0)
            taps(0, 0, 1)
            taps(0, 1, 0)
            taps(0, 1, 1)
            with dve.Fori(1, FKT // 2) as i:
                taps(i, 0, 0)
                add_down(i - 1, range(0, 4))
                taps(i, 0, 1)
                add_down(i - 1, range(4, 2 * NT))
                taps(i, 1, 0)
                taps(i, 1, 1)
            add_down(FKT // 2 - 1, range(2 * NT))

            def e_apply(t):
                cond = 0 if t < NL else 1
                dve.wait_ge(q.e_q, t + 1)
                then(dve.reciprocal(est[:, t, 3:4], est[:, t, 2:3]))
                then(dve.scalar_tensor_tensor(out=y_acc[:, t, :], in0=y_acc[:, t, :], scalar=est[:, t, 3:4], in1=g2_row[:, cond, :],
                                              op0=ALU.mult, op1=ALU.mult))
                dve.tensor_tensor(x2t[:, t, :], x2t[:, t, :], y_acc[:, t, :], ALU.add).then_inc(q.e_o, 1)
            dve.wait_ge(q.x2_in, 16 * (NT + 2))
            for t in range(NT):
                dve.wait_ge(q.e_s, t + 1)
                dve.tensor_scalar(est[:, t, 1:2], est[:, t, 0:1], 1.0 / D, EPS, ALU.mult, ALU.add).then_inc(q.e_v, 1)
                if t:
                    e_apply(t - 1)
            e_apply(NT - 1)


_INS = ["x_prompt", "x_sample", "state_ret_fwd", "state_ret_bwd", "c", "c_ctx", "norm1_pre", "norm1_post", "norm2_pre",
        "norm2_post", "ada_w", "ada_b", "w_in", "ret_decay_fwd", "ret_decay_bwd", "ret_gn_w", "ret_w_out", "conv_dw_w",
        "conv_dw_b", "conv_ln_w", "conv_ln_b", "conv_w_out", "w_mix_out", "ffn_w_up", "ffn_dw_w", "ffn_dw_b", "ffn_w_down"]
_OUTS = [(1, CTX, D), (1, LAT, D), (1, 1, HEADS, DK, DV), (1, 1, HEADS, DK, DV)]


def kernel(**inputs):
    import concourse.bacc as bacc
    from concourse.bass_utils import run_bass_kernel_spmd

    nc = bacc.Bacc("TRN2", target_bir_lowering=False, num_devices=1)
    arrays, aps = {}, {}
    rope_table, shape_table = shape_tables()
    for name, v in [(n, inputs[n]) for n in _INS] + [("rope_table", rope_table), ("shape_table", shape_table)]:
        v = np.ascontiguousarray(v)
        arrays[f"in_{name}"] = v
        aps[name] = nc.dram_tensor(f"in_{name}", v.shape, mybir.dt.from_np(v.dtype), kind="ExternalInput").ap()
    outs = [nc.dram_tensor(f"out_{i}", s, F32, kind="ExternalOutput").ap() for i, s in enumerate(_OUTS)]
    build(nc, aps, *outs)
    r = run_bass_kernel_spmd(nc, [arrays], core_ids=[0])
    return tuple(r.results[0][f"out_{i}"] for i in range(len(_OUTS)))
```

```python
from contextlib import ExitStack

import numpy as np
import concourse.bass as bass
from concourse import mybir

P = 128
D = 1024
KT = D // P
LAT, CTX = 1024, 128
T = LAT + CTX
NT = T // P
NL = LAT // P
TG = 384
NTG = T // TG
HEADS, DK, DV = 4, 256, 256
CW = 31
HALO = CW // 2
FF = 2816
FKT = FF // P
EPS, GN_EPS = 1e-6, 1e-5
GRID_W = 64
CHW = 1024
U_OUT = LAT + HALO + CTX
U_IN = U_OUT + 2 * HALO
F_OUT = LAT + 1 + CTX
F_IN = F_OUT + 2
NPOS = 4

F32, F32R = mybir.dt.float32, mybir.dt.float32r
ALU = mybir.AluOpType
ACT = mybir.ActivationFunctionType
AX = mybir.AxisListType

V_C, V_CC, V_N1PRE, V_N2PRE, V_LNW, V_LNB, V_CDB, V_N1POST, V_N2POST, V_ADAB = 0, 8, 16, 24, 32, 40, 48, 56, 64, 72
SH1, SC1, G1, SH2, SC2, G2 = range(6)


def shape_tables():
    nf = DK // 4
    inv = (10000.0 ** (-np.arange(nf, dtype=np.float32) / nf)).astype(np.float32)
    tok = np.arange(LAT)
    rope = np.zeros((NL, P, 2, 2, 2, nf), np.float32)
    for half, pos in enumerate((tok // GRID_W, tok % GRID_W)):
        ang = (pos[:, None].astype(np.float32) * inv[None, :]).astype(np.float32)
        c, s = np.cos(ang).reshape(NL, P, nf), np.sin(ang).reshape(NL, P, nf)
        rope[:, :, 0, half, 0], rope[:, :, 0, half, 1] = c, c
        rope[:, :, 1, half, 0], rope[:, :, 1, half, 1] = -s, s
    i = np.arange(P, dtype=np.float32)
    pos = np.stack([i + 1, P - i, P - 1 - i, i], 1)
    rel = i[None, :] - i[:, None]
    scale = DK ** -0.5
    dist = np.stack([np.maximum(rel, 0), np.maximum(-rel, 0), (rel >= 0) * scale, (rel <= 0) * scale], 1)
    table = np.concatenate([pos, dist.reshape(P, 4 * P)], 1).astype(np.float32)
    return rope.reshape(NL, P, 4 * P), np.ascontiguousarray(table)


def build(nc, a, out_xp, out_xs, out_sf, out_sb):
    ctx = ExitStack()

    def sb(name, shape, dt=F32, stack=None):
        return (stack or ctx).enter_context(nc.sbuf_tensor(name, shape, dt))

    def sem(name):
        return ctx.enter_context(nc.semaphore(name))

    with ctx:
        conv_d = nc.dram_tensor("conv_d", [KT, P, T], F32, kind="Internal").ap()
        gate_d = nc.dram_tensor("gate_d", [2, KT, P, T], F32, kind="Internal").ap()
        qkvg_d = nc.dram_tensor("qkvg_d", [HEADS, NT, P, 1024], F32, kind="Internal").ap()
        rT_d = nc.dram_tensor("rT_d", [KT, P, T], F32, kind="Internal").ap()
        x2_d = nc.dram_tensor("x2_d", [NT, P, D], F32, kind="Internal").ap()
        h2T_d = nc.dram_tensor("h2T_d", [KT, P, T], F32, kind="Internal").ap()
        gain_d = nc.dram_tensor("gain_d", [32, P], F32, kind="Internal").ap()

        W_hi = sb("W_hi", [P, 6, CHW], F32R)
        W_lo = sb("W_lo", [P, 6, CHW], F32R)
        W_raw = sb("W_raw", [P, 3, CHW])
        V0 = sb("V0", [P, P])
        VF = sb("VF", [P, 4 * FKT * 2])
        mod = sb("mod", [P, 48, 2])
        ident = sb("ident", [P, P])
        mean_w = sb("mean_w", [P, P])

        s_L = ExitStack()
        s_A = ExitStack()
        ada_p = sb("ada_p", [P, 8, KT, 2 * P], F32, s_A)
        mod_row = sb("mod_row", [2, 2 * D], F32, s_A)
        s_A.close()
        A_hi = sb("A_hi", [P, NT, KT, P], F32R, s_L)
        A_lo = sb("A_lo", [P, NT, KT, P], F32R, s_L)
        W2_hi = sb("W2_hi", [P, 2, CHW], F32R, s_L)
        W2_lo = sb("W2_lo", [P, 2, CHW], F32R, s_L)
        W2_raw = sb("W2_raw", [P, 1, CHW], F32, s_L)
        VC = sb("VC", [P, CW * KT], F32, s_L)
        s_PU = ExitStack()
        cs = sb("cs", [P, KT, 2], F32, s_PU)
        s_P = ExitStack()
        x_all = sb("x_all", [P, NT, D], F32, s_P)
        rows = sb("rows", [P, 5, P], F32, s_P)
        hf = sb("hf", [P, 2, T], F32, s_P)
        ssq = sb("ssq", [P, NT], F32, s_P)
        rst = sb("rst", [P, NT], F32, s_P)
        hscale = sb("hscale", [P, KT, 2], F32, s_P)
        s_P.close()
        s_U = ExitStack()
        u_in = sb("u_in", [P, 2, U_IN], F32, s_U)
        sig = sb("sig", [P, T], F32, s_U)
        u_a = sb("u_a", [P, T], F32, s_U)
        conv_y = sb("conv_y", [P, 2, U_OUT], F32, s_U)
        gates = sb("gates", [P, 2, T], F32, s_U)
        ada_w = sb("ada_w", [P, 2, KT, P], F32, s_U)
        s_U.close()
        s_PU.close()
        s_Q = ExitStack()
        gn_row = sb("gn_row", [P, D], F32, s_Q)
        gn_head = sb("gn_head", [P, 256], F32, s_Q)
        qk_st = sb("qk_st", [P, 3, 512], F32, s_Q)
        vg_st = sb("vg_st", [P, 3, 512], F32, s_Q)
        rope_c = sb("rope_c", [P, 512], F32, s_Q)
        rope_s = sb("rope_s", [P, 512], F32, s_Q)
        sb("rope_gap", [P, 2 * U_IN + 2 * T + 2 * U_OUT + 64 - (D + 256 + 6 * 512 + 2 * 512)], F32, s_Q)
        rope = sb("rope", [P, NL, 2, 256], F32, s_Q)
        gm1 = sb("gm1", [P, 32], F32, s_Q)
        gmr = sb("gmr", [32, P], F32, s_Q)
        s_Q.close()
        s_L.close()
        s_R = ExitStack()
        qkvg = sb("qkvg", [P, NT, 4, 256], F32, s_R)
        S = sb("S", [P, NL, 2, 512], F32, s_R)
        k_hi = sb("k_hi", [P, 3, 256], F32R, s_R)
        k_lo = sb("k_lo", [P, 3, 256], F32R, s_R)
        vs = sb("vs", [P, 3, 512], F32, s_R)
        vs_hi = sb("vs_hi", [P, 3, 512], F32R, s_R)
        vs_lo = sb("vs_lo", [P, 3, 512], F32R, s_R)
        st_out = sb("st_out", [P, 2, 2, 256], F32, s_R)
        T_hi = sb("T_hi", [P, 2, 512], F32R, s_R)
        T_lo = sb("T_lo", [P, 2, 512], F32R, s_R)
        S_hi = sb("S_hi", [P, 2, 1024], F32R, s_R)
        S_lo = sb("S_lo", [P, 2, 1024], F32R, s_R)
        v_hi = sb("v_hi", [P, 2, 256], F32R, s_R)
        v_lo = sb("v_lo", [P, 2, 256], F32R, s_R)
        sm = sb("sm", [P, 2, P], F32, s_R)
        sm_hi = sb("sm_hi", [P, 2, P], F32R, s_R)
        sm_lo = sb("sm_lo", [P, 2, P], F32R, s_R)
        o_a = sb("o_a", [P, 2, 256], F32, s_R)
        o_b = sb("o_b", [P, 2, 256], F32, s_R)
        o_o = sb("o_o", [P, 2, 256], F32, s_R)
        o_y = sb("o_y", [P, 2, 256], F32, s_R)
        o_r = sb("o_r", [P, 2, 256], F32, s_R)
        bn6 = sb("bn6", [P, 2, 6], F32, s_R)
        bn2 = sb("bn2", [P, 2, 2], F32, s_R)
        gstd = sb("gstd", [P, 2, 4], F32, s_R)
        rT_st = sb("rT_st", [P, 2, 2, P], F32, s_R)
        tab = sb("tab", [P, NPOS + 4 * P], F32, s_R)
        dec = sb("dec", [P, 2 * HEADS], F32, s_R)
        lg = sb("lg", [P, 2 * HEADS], F32, s_R)
        lgt = sb("lgt", [P, 6, 2 * HEADS], F32, s_R)
        dk_a = sb("dk_a", [P, HEADS, 6], F32, s_R)
        dk_c = sb("dk_c", [P, HEADS, 6], F32, s_R)
        hd = sb("hd", [P, 8], F32, s_R)
        dkt = sb("dkt", [P, HEADS, 8], F32, s_R)
        mask = sb("mask", [P, P], F32, s_R)
        mtmp = sb("mtmp", [P, 4, P], F32, s_R)
        s_R.close()
        s_M = ExitStack()
        r_hi = sb("r_hi", [P, KT, TG], F32R, s_M)
        r_lo = sb("r_lo", [P, KT, TG], F32R, s_M)
        c_hi = sb("c_hi", [P, KT, TG], F32R, s_M)
        c_lo = sb("c_lo", [P, KT, TG], F32R, s_M)
        s_C = ExitStack()
        conv0 = sb("conv0", [P, KT, TG], F32, s_C)
        s_C.close()
        m_hi = sb("m_hi", [P, KT, TG], F32R, s_M)
        m_lo = sb("m_lo", [P, KT, TG], F32R, s_M)
        rc_st = sb("rc_st", [P, KT, TG], F32, s_M)
        m_part = sb("m_part", [P, KT, TG], F32, s_M)
        gate_t = sb("gate_t", [P, 4, TG], F32, s_M)
        ln_a = sb("ln_a", [P, TG], F32, s_M)
        ln_sq = sb("ln_sq", [P, 2, TG], F32, s_M)
        ln_acc = sb("ln_acc", [P, TG], F32, s_M)
        g1_row = sb("g1_row", [P, D], F32, s_M)
        mo = sb("mo", [P, 3, D], F32, s_M)
        h2o = sb("h2o", [P, KT, P], F32, s_M)
        xt = sb("xt", [P, 3, D], F32, s_M)
        sq_junk = sb("sq_junk", [P, D], F32, s_M)
        mst = sb("mst", [P, 3, 8], F32, s_M)
        h2s = sb("h2s", [P, KT, 2], F32, s_M)
        s_M.close()
        s_F = ExitStack()
        B_hi = sb("B_hi", [P, KT, T], F32R, s_F)
        B_lo = sb("B_lo", [P, KT, T], F32R, s_F)
        s_H = ExitStack()
        h2_in = sb("h2_in", [P, KT, 2 * TG], F32, s_H)
        s_H.close()
        y_acc = sb("y_acc", [P, NT, D], F32, s_F)
        f_in = sb("f_in", [P, 2, F_IN], F32, s_F)
        f_cv = sb("f_cv", [P, 2, F_OUT], F32, s_F)
        g_hi = sb("g_hi", [P, 2, T], F32R, s_F)
        g_lo = sb("g_lo", [P, 2, T], F32R, s_F)
        s_F.close()
        s_E = ExitStack()
        x2t = sb("x2t", [P, NT, D], F32, s_E)
        g2_row = sb("g2_row", [P, 2, D], F32, s_E)
        ej = sb("ej", [P, D], F32, s_E)
        est = sb("est", [P, NT, 4], F32, s_E)
        s_E.close()

        ps = ctx.enter_context(nc.psum_tensor("ps", [P, 8, 512], F32))

        def wslot(n, ring):
            s = n % ring
            return (W_hi[:, s, :], W_lo[:, s, :]) if s < 6 else (W2_hi[:, s - 6, :], W2_lo[:, s - 6, :])

        def wraw(n, ring):
            s = n % ring
            return W_raw[:, s, :] if s < 3 else W2_raw[:, 0, :]

        w_in = a["w_in"][0]
        ada = a["ada_w"][0].rearrange("(k p) n -> p k n", p=P)
        w_in_p = w_in.rearrange("(k p) n -> p k n", p=P)
        w_in_s = w_in.rearrange("(k p) (s c) -> p k s c", p=P, s=8)
        Fv = lambda x: x.bitcast(F32)

        class Semaphores:
            pass
        q = Semaphores()
        q.gnh_ok = sem("gnh_ok")
        q.kv_hi = sem("kv_hi")
        q.kv_lo = sem("kv_lo")
        q.Tv_hi = sem("Tv_hi")
        q.mem_free = sem("mem_free")
        q.dve_own = sem("dve_own")
        q.w_hi = sem("w_hi")
        q.w_lo = sem("w_lo")
        q.vec_in = sem("vec_in")
        q.vecT = sem("vecT")
        q.vec_ok = sem("vec_ok")
        q.x_in0 = sem("x_in0")
        q.ident_ok = sem("ident_ok")
        q.cs_ok = sem("cs_ok")
        q.ada_in0 = sem("ada_in0")
        q.ada_in1 = sem("ada_in1")
        q.ada_rows = sem("ada_rows")
        q.ada_used = sem("ada_used")
        q.mod_ok = sem("mod_ok")
        q.ssq_ok = sem("ssq_ok")
        q.rstd_a = sem("rstd_a")
        q.rstd_b = sem("rstd_b")
        q.xn_ok = sem("xn_ok")
        q.hT_ps = sem("hT_ps")
        q.hT_f = sem("hT_f")
        q.hT_lo = sem("hT_lo")
        q.u_ps = sem("u_ps")
        q.u_evac = sem("u_evac")
        q.u_ok = sem("u_ok")
        q.pads_ok = sem("pads_ok")
        q.conv_step = sem("conv_step")
        q.conv_st0 = sem("conv_st0")
        q.conv_st1 = sem("conv_st1")
        q.gate_st0 = sem("gate_st0")
        q.gate_st1 = sem("gate_st1")
        q.adaU_ok = sem("adaU_ok")
        q.q_ps = sem("q_ps")
        q.qk_evac = sem("qk_evac")
        q.vg_evac = sem("vg_evac")
        q.rope_in = sem("rope_in")
        q.rope_ok = sem("rope_ok")
        q.qk_st0 = sem("qk_st0")
        q.qk_st1 = sem("qk_st1")
        q.qk_st2 = sem("qk_st2")
        q.vg_ok = sem("vg_ok")
        q.vg_st0 = sem("vg_st0")
        q.vg_st1 = sem("vg_st1")
        q.vg_st2 = sem("vg_st2")
        q.gain_t = sem("gain_t")
        q.gain_c = sem("gain_c")
        q.gain_st = sem("gain_st")
        q.tab_in = sem("tab_in")
        q.dk_arg = sem("dk_arg")
        q.dk_exp = sem("dk_exp")
        q.hd_ok = sem("hd_ok")
        q.mexp = sem("mexp")
        q.mask_ok = sem("mask_ok")
        q.s0f_in = sem("s0f_in")
        q.s0b_in = sem("s0b_in")
        q.vs_ok = sem("vs_ok")
        q.P_ps = sem("P_ps")
        q.P_evac = sem("P_evac")
        q.st_f_st = sem("st_f_st")
        q.Sscan = sem("Sscan")
        q.T_ps = sem("T_ps")
        q.T_lo_ok = sem("T_lo_ok")
        q.S_hi_ok = sem("S_hi_ok")
        q.S_lo_ok = sem("S_lo_ok")
        q.S_lo2_ok = sem("S_lo2_ok")
        q.v_lo_ok = sem("v_lo_ok")
        q.sc_ps = sem("sc_ps")
        q.sm_ok = sem("sm_ok")
        q.sm_hi_ok = sem("sm_hi_ok")
        q.sm_lo_ok = sem("sm_lo_ok")
        q.in_ps = sem("in_ps")
        q.cr_ps = sem("cr_ps")
        q.oa_ok = sem("oa_ok")
        q.ob_ok = sem("ob_ok")
        q.o_ok = sem("o_ok")
        q.gn_s = sem("gn_s")
        q.gn_v = sem("gn_v")
        q.gn_q = sem("gn_q")
        q.gn_r = sem("gn_r")
        q.y_ok = sem("y_ok")
        q.r_ok = sem("r_ok")
        q.rT_ps = sem("rT_ps")
        q.rT_ok = sem("rT_ok")
        q.rT_s0 = sem("rT_s0")
        q.rT_s1 = sem("rT_s1")
        q.g1_in = sem("g1_in")
        q.rc_in = sem("rc_in")
        q.c0_in = sem("c0_in")
        q.r_hi_ok = sem("r_hi_ok")
        q.r_lo_ok = sem("r_lo_ok")
        q.ln_s = sem("ln_s")
        q.ln_mp = sem("ln_mp")
        q.ln_d = sem("ln_d")
        q.ln_sqk = sem("ln_sqk")
        q.ln_acck = sem("ln_acck")
        q.ln_vp = sem("ln_vp")
        q.ln_v = sem("ln_v")
        q.ln_r1 = sem("ln_r1")
        q.ln_z = sem("ln_z")
        q.ln_silu = sem("ln_silu")
        q.c_lo_ok = sem("c_lo_ok")
        q.gt_in0 = sem("gt_in0")
        q.gt_in1 = sem("gt_in1")
        q.mr_ps = sem("mr_ps")
        q.mr_evac = sem("mr_evac")
        q.m_hi_ok = sem("m_hi_ok")
        q.m_lo_ok = sem("m_lo_ok")
        q.mo_ps = sem("mo_ps")
        q.mo_ok = sem("mo_ok")
        q.mst_s = sem("mst_s")
        q.mst_v = sem("mst_v")
        q.mst_q = sem("mst_q")
        q.x2_ok = sem("x2_ok")
        q.xn2_ok = sem("xn2_ok")
        q.h2_ps = sem("h2_ps")
        q.h2_f = sem("h2_f")
        q.h2_st = sem("h2_st")
        q.xt_in = sem("xt_in")
        q.xt_st = sem("xt_st")
        q.B_hi_ok = sem("B_hi_ok")
        q.B_lo_ok = sem("B_lo_ok")
        q.fpad = sem("fpad")
        q.fa_ps = sem("fa_ps")
        q.fg_ps = sem("fg_ps")
        q.fa_ev = sem("fa_ev")
        q.fg_ev = sem("fg_ev")
        q.fa_c0 = sem("fa_c0")
        q.fg_c0 = sem("fg_c0")
        q.fa_c = sem("fa_c")
        q.fg_c = sem("fg_c")
        q.fsilu = sem("fsilu")
        q.fprod = sem("fprod")
        q.gact_hi = sem("gact_hi")
        q.gact_lo = sem("gact_lo")
        q.fd_ps = sem("fd_ps")
        q.y_add = sem("y_add")
        q.e_s = sem("e_s")
        q.e_v = sem("e_v")
        q.e_q = sem("e_q")
        q.e_o = sem("e_o")
        q.out_st = sem("out_st")
        wl_in = [sem(f"wl_in{i}") for i in range(4)]
        wr_in = [sem(f"wr_in{i}") for i in range(3)]
        tile_in = [sem(f"tile_in{i}") for i in range(3)]
        x_in = q.x_in0
        ada_in = [q.ada_in0, q.ada_in1]
        conv_st = [q.conv_st0, q.conv_st1]
        gate_st = [q.gate_st0, q.gate_st1]
        qk_st_s = [q.qk_st0, q.qk_st1, q.qk_st2]
        vg_st_s = [q.vg_st0, q.vg_st1, q.vg_st2]
        rT_s = [q.rT_s0, q.rT_s1]
        x2_in = [sem("x2_in0"), sem("x2_in1")]
        gt_in = [q.gt_in0, q.gt_in1]

        U_COLS = [(5, 0), (4, 0), (5, 1), (4, 1), (6, 0), (7, 0), (6, 1), (7, 1)]
        M_CHUNKS = 24
        N_L = 64
        N_LM = N_L + NTG * M_CHUNKS

        def f_number(i, role):
            if isinstance(i, int) and i == 0 and role < 2:
                return role
            if isinstance(i, int) and i == FKT // 2 - 1 and role in (2, 3):
                return i * 6 + (role + 2)
            return i * 6 + (role + 4 if role in (2, 3) else role - 2)

        def f_raw(i, role):
            return f_number(i if isinstance(i, int) else 1, role) % 3

        def f_loads(i, role):
            if isinstance(i, int):
                return f_number(i, role) // 3 + 1
            return i * 2 + (1 + (role + 4 if role in (2, 3) else role - 2) // 3)

        def conv_src(g):
            return rc_st if g else conv0

        OUT = [NL] + list(range(NL))

        def turned_bank(j):
            return 2 if j < NT - 2 else 4 + (j - (NT - 2))

        def T_number(j):
            return j + 1 if j < 2 else 2 * j + 1

        def v_number(j):
            return 2 * j + 2 if j else 3

        def slot_before(h, j):
            return h * NT + (j - 1 if j else 0)

        FIRST, SECOND = (1, 2, 4), (3, 5, 6)

        block = ctx.enter_context(nc.Block())

        @block.sync
        def _(sp):
            r = 0
            for name in ("c", "c_ctx", "norm1_pre", "norm2_pre", "conv_ln_w", "conv_ln_b", "conv_dw_b",
                         "norm1_post", "norm2_post", "ada_b"):
                v = a[name]
                v = (v if len(v.shape) == 1 else v[0]).rearrange("(k p) -> k p", p=P)
                n = v.shape[0]
                if name == "ada_b":
                    assert r == V_ADAB
                sp.dma_start(rows[r:r + n, 0, :], v).then_inc(q.vec_in, 16)
                r += n
            fw = a["ffn_dw_w"][0].rearrange("w (j p) -> (w j) p", p=P)
            fb = a["ffn_dw_b"][0].rearrange("(j p) -> j p", p=P)
            cw = a["conv_dw_w"][0].rearrange("w (k p) -> (w k) p", p=P)
            sp.dma_start(rows[0:88, 1, :], fw[0:88, :]).then_inc(q.vec_in, 16)
            sp.dma_start(rows[0:44, 2, :], fw[88:132, :]).then_inc(q.vec_in, 16)
            sp.dma_start(rows[44:88, 2, :], fb).then_inc(q.vec_in, 16)
            sp.dma_start(rows[0:124, 3, :], cw[0:124, :]).then_inc(q.vec_in, 16)
            sp.dma_start(rows[0:124, 4, :], cw[124:248, :]).then_inc(q.vec_in, 16)
            xs = a["x_sample"][0].rearrange("(t p) d -> p t d", p=P)
            sp.dma_start(x_all[:, 0:NL, :], xs).then_inc(x_in, 16)
            sp.dma_start(x_all[:, NL, :], a["x_prompt"][0]).then_inc(x_in, 16)
            for n in range(8):
                if n >= 2:
                    sp.wait_ge(ada_in[n % 2], 16 * (n // 2))
                sp.dma_start(ada_p[:, n, :, :], ada[:, :, n * 2 * P:(n + 1) * 2 * P]).then_inc(ada_in[n % 2], 16)

            def u_chunk(i, e):
                s, t = U_COLS[e]
                if not (isinstance(i, int) and i == 0 and e < 4):
                    sp.wait_ge(q.w_lo, i * 8 + e - 3)
                sp.dma_start(wraw(e, 4).rearrange("p (k n) -> p k n", k=KT),
                             w_in_p[:, :, bass.ds(i * 256 + (s * 1024 + t * P), P)]).then_inc(wl_in[e % 4], 16)

            for e in range(8):
                u_chunk(0, e)
            with sp.Fori(1, 4) as i:
                for e in range(8):
                    u_chunk(i, e)
            with sp.Fori(0, HEADS) as h:
                for e in range(8):
                    g, j = e // 4, e % 4
                    sp.wait_ge(q.w_lo, h * 8 + (32 + e - 3))
                    for s in range(2):
                        sp.dma_start(wraw(e, 4).rearrange("p (k s n) -> p k s n", k=2, s=2)[:, :, s, :],
                                     w_in_s[:, 2 * j:2 * j + 2, 2 * g + s, bass.ds(h * 256, 256)]).then_inc(wl_in[e % 4], 16)
            def row_of(c):
                return gain_d[c * KT:(c + 1) * KT, :].rearrange("k p -> (k p)").partition_broadcast(P)
            sp.wait_ge(q.gain_c, 1)
            sp.dma_start(gain_d, gmr[:, :]).then_inc(q.gain_st, 16)

            wr, wc, wx = (a[n][0].rearrange("(k p) n -> p k n", p=P) for n in ("ret_w_out", "conv_w_out", "w_mix_out"))
            def m_chunk(n):
                if n == 0:
                    sp.wait_ge(q.w_lo, 64)
                if n >= 3:
                    sp.wait_ge(q.w_lo, N_L + n - 2)
                c = n % M_CHUNKS
                dst = wraw(n, 3)
                if c < 16:
                    w, m = (wr, c) if c < 8 else (wc, c - 8)
                    sp.dma_start(dst.rearrange("p (k n) -> p k n", k=KT), w[:, :, m * P:(m + 1) * P]).then_inc(wr_in[n % 3], 16)
                else:
                    half, j = (c - 16) // 4, (c - 16) % 4
                    sp.dma_start(dst.rearrange("p (k n) -> p k n", k=2),
                                 wx[:, 2 * j:2 * j + 2, half * 512:(half + 1) * 512]).then_inc(wr_in[n % 3], 16)
            def tile_loads(h, first, groups=range(0, NT, 3)):
                for t in groups:
                    if first:
                        sp.wait_ge(q.q_ps, 18 * (HEADS - 1) + NT + t + 3)
                    else:
                        sp.wait_ge(q.r_ok, h * NT + (min(t + 4, NT) - NT))
                    src = qkvg_d[bass.ds(h, 1), t:t + 3].rearrange("o t p n -> p (o t) n")
                    sp.dma_start(qkvg[:, t:t + 3, :, :].rearrange("p t a b -> p t (a b)"), src).then_inc(tile_in[t // 3], 16)
            def state_loads(h, first):
                for d, (name, slot) in enumerate((("state_ret_fwd", 0), ("state_ret_bwd", NL - 1))):
                    if not first:
                        sp.wait_ge(q.S_lo_ok, h * NL - (NL - 1) * (1 - d))
                        sp.wait_ge(q.S_lo2_ok, h * NL - (NL - 1) * (1 - d))
                    st = a[name][0, 0].rearrange("h (k p) e -> h p k e", p=P)
                    src = st[0] if first else st[bass.ds(h, 1)].rearrange("o p k e -> (o p) k e")
                    sp.dma_start(S[:, slot, :, d * 256:(d + 1) * 256], src).then_inc((q.s0f_in, q.s0b_in)[d], 16)

            for s_ in qk_st_s + vg_st_s:
                sp.wait_ge(s_, 16 * 3)
            tile_loads(0, True)
            sp.wait_ge(q.q_ps, 18 * HEADS)
            state_loads(0, True)
            for n in range(3):
                m_chunk(n)
            for s_ in qk_st_s + vg_st_s:
                sp.wait_ge(s_, 16 * 3 * HEADS)
            def head_loads(h):
                tile_loads(h, False, (0, 3))
                state_loads(h, False)
                tile_loads(h, False, (6,))
            with sp.Fori(1, HEADS) as h:
                head_loads(h)
            sp.wait_ge(q.P_ps, HEADS * NT)
            sp.wait_ge(rT_s[0], 16 * (5 * (HEADS - 1) + 2))
            sp.wait_ge(rT_s[1], 16 * (4 * (HEADS - 1) + 2))
            sp.dma_start(rc_st[:, :, :], rT_d[:, :, 0:TG].rearrange("k p n -> p k n")).then_inc(q.rc_in, 16)
            sp.wait_ge(q.r_ok, HEADS * NT)
            sp.wait_ge(q.rT_ok, HEADS * NT)
            sp.wait_ge(q.st_f_st, 32 * HEADS)
            for s_, n in ((rT_s[0], 5), (rT_s[1], 4)):
                sp.wait_ge(s_, 16 * n * HEADS)
            sp.sem_inc(q.mem_free, 1)
            sp.dma_start(conv0[:, :, :], conv_d[:, :, 0:TG].rearrange("k p n -> p k n")).then_inc(q.c0_in, 16)
            sp.dma_start(g1_row[:, :], row_of(0)).then_inc(q.g1_in, 16)
            for n in range(3, 3 * M_CHUNKS):
                m_chunk(n)

            wu = a["ffn_w_up"][0].rearrange("(k p) n -> p k n", p=P)
            wd = a["ffn_w_down"][0].rearrange("(k p) n -> p k n", p=P)
            def f_chunk(i, role):
                n = f_number(i, role)
                sp.wait_ge(q.w_lo, N_LM + n - 2)
                dst = W_raw[:, f_raw(i, role), :]
                if role in (2, 3):
                    sp.dma_start(dst, wd[:, bass.ds(i * 2 + (role - 2), 1), :].rearrange("p o n -> p (o n)")).then_inc(wr_in[f_raw(i, role)], 16)
                else:
                    p, kind = role // 4, role % 2
                    sp.dma_start(dst.rearrange("p (k n) -> p k n", k=KT),
                                 wu[:, :, bass.ds(i * 256 + (p * P + kind * FF), P)]).then_inc(wr_in[f_raw(i, role)], 16)
            sp.wait_ge(q.h2_st, 16 * 2 * 3)
            sp.wait_ge(q.c_lo_ok, NTG * KT)
            sp.wait_ge(q.m_lo_ok, NTG * KT)
            sp.dma_start(h2_in[:, :, :], h2T_d[:, :, 0:2 * TG].rearrange("k p n -> p k n")).then_inc(q.rc_in, 16)
            f_chunk(0, 0)
            f_chunk(0, 1)
            f_chunk(0, 4)
            sp.wait_ge(q.x2_ok, NL)
            sp.dma_start(g1_row[:, :], row_of(1)).then_inc(q.g1_in, 16)
            f_chunk(0, 5)
            sp.wait_ge(q.B_lo_ok, KT + 3)
            sp.wait_ge(q.xt_st, 16 * NT)
            sp.sem_inc(q.mem_free, 1)
            with sp.Fori(1, FKT // 2) as i:
                f_chunk(i, 0)
                f_chunk(i, 1)
                f_chunk(i - 1, 2)
                f_chunk(i - 1, 3)
                f_chunk(i, 4)
                f_chunk(i, 5)
            for role in (2, 3):
                f_chunk(FKT // 2 - 1, role)
            sp.wait_ge(q.fg_ps, FKT)
            for c in range(2):
                sp.dma_start(g2_row[:, c, :], row_of(2 + c)).then_inc(q.g1_in, 16)
            for t in range(NT):
                if t >= 2:
                    sp.wait_ge(x2_in[t % 2], 16 * (t // 2))
                sp.dma_start(x2t[:, t, :], x2_d[t]).then_inc(x2_in[t % 2], 16)
            for t in range(NT):
                sp.wait_ge(q.e_o, t + 1)
                dst = out_xs[0, t * P:(t + 1) * P, :] if t < NL else out_xp[0]
                sp.dma_start(dst, x2t[:, t, :]).then_inc(q.out_st, 16)
            sp.wait_ge(q.out_st, 16 * NT)
            sp.wait_ge(q.st_f_st, 32 * HEADS)

        @block.tensor
        def _(pe):
            def mm(out, l, r, start, stop):
                return pe.matmul(out, l, r, start=start, stop=stop)

            def fm3(out, wh, wl, a_hi, a_lo, ready=None):
                wh, wl = (x.rearrange("p (k n) -> p k n", k=KT) for x in (wh, wl))
                for k in range(KT):
                    if ready is not None:
                        pe.wait_ge(ready, k + 1)
                    mm(out, wh[:, k, :], a_hi(k), k == 0, False)
                    mm(out, wh[:, k, :], a_lo(k), False, False)
                    last = mm(out, wl[:, k, :], a_hi(k), False, k == KT - 1)
                return last

            pe.wait_ge(q.ident_ok, 3)
            pe.wait_ge(q.vec_in, 16 * 15)
            pe.transpose(ps[:, 7, 0:120], rows[0:120, 0, :], ident[0:120, 0:120]).then_inc(q.vecT, 1)
            pe.transpose(ps[:, 5, 0:88], rows[0:88, 1, :], ident[0:88, 0:88]).then_inc(q.vecT, 1)
            pe.transpose(ps[:, 5, 128:216], rows[0:88, 2, :], ident[0:88, 0:88]).then_inc(q.vecT, 1)
            pe.transpose(ps[:, 4, 0:124], rows[0:124, 3, :], ident[0:124, 0:124]).then_inc(q.vecT, 1)
            pe.transpose(ps[:, 4, 128:252], rows[0:124, 4, :], ident[0:124, 0:124]).then_inc(q.vecT, 1)
            pe.wait_ge(q.cs_ok, 1)
            def ada_unit(w, col):
                for k in range(KT):
                    last = mm(ps[:, 6, col:col + 2], w[:, k, :], cs[:, k, :], k == 0, k == KT - 1)
                last.then_inc(q.ada_used, 1)
                return last
            for n in range(8):
                pe.wait_ge(ada_in[n % 2], 16 * (n // 2 + 1))
                for k in range(KT):
                    last = mm(ps[0:2, n // 2, (n % 2) * 256:(n % 2 + 1) * 256], cs[:, k, :], ada_p[:, n, k, :], k == 0, k == KT - 1)
            last.then_inc(q.ada_rows, 1)
            for m in range(16):
                if m == 0:
                    pe.wait_ge(q.vec_ok, 6)
                pe.transpose(ps[:, 6, 2 * m:2 * m + 2], mod_row[0:2, m * P:(m + 1) * P], ident[0:2, 0:2]).then_inc(q.ada_used, 1)
            for k in range(KT):
                if k == 0:
                    pe.wait_ge(q.xn_ok, NT)
                    pe.wait_ge(q.vec_ok, 6)
                if k >= 2:
                    pe.wait_ge(q.hT_f, k - 1)
                for t in range(NT):
                    last = pe.transpose(ps[:, 3 * (k % 2) + t // 4, (t % 4) * P:(t % 4 + 1) * P],
                                        x_all[:, t, k * P:(k + 1) * P], ident[:, :])
                last.then_inc(q.hT_ps, 1)

            pe.wait_ge(q.hT_f, KT)
            pe.wait_ge(q.mod_ok, 1)
            def u_step(i, e):
                wh, wl = wslot(e, 8)
                pe.wait_ge(q.w_lo, i * 8 + e + 1)
                if not (isinstance(i, int) and e < 2):
                    pe.wait_ge(q.u_evac, i * 8 + e - 1)
                for g in range(NTG):
                    tiles = slice(g * TG // P, (g + 1) * TG // P)
                    last = fm3(ps[:, 3 * (e % 2) + g, 0:TG].rearrange("p (t n) -> p t n", n=P), wh, wl,
                               lambda k: A_hi[:, tiles, k, :], lambda k: A_lo[:, tiles, k, :],
                               ready=q.hT_lo if isinstance(i, int) and e == g == 0 else None)
                last.then_inc(q.u_ps, 1)
                if e == 0 and not isinstance(i, int):
                    pe.wait_ge(q.adaU_ok, i)
                pe.wait_ge(ada_in[e % 2], i * 64 + (16 * (5 + e // 2)))
                ada_unit(ada_w[:, e % 2, :, :], 2 * e)
            for e in range(8):
                u_step(0, e)
            with pe.Fori(1, 4) as i:
                for e in range(8):
                    u_step(i, e)

            pe.wait_ge(q.u_evac, 32)
            def q_step(h, first):
                for n in range(18):
                    g, t = n // 9, n % 9
                    if n < 6 and not first:
                        pe.wait_ge(q.vg_evac, h * NT + (n - 5))
                    elif 6 <= n < 15:
                        pe.wait_ge(q.qk_evac, h * NT + (n - 5))
                    elif n >= 15:
                        pe.wait_ge(q.vg_evac, h * NT + (n - 14))
                    for k in range(KT):
                        j = 4 * g + k // 2
                        wh, wl = (x.rearrange("p (k n) -> p k n", k=2)[:, k % 2, :] for x in wslot(j, 8))
                        if t == 0 and k % 2 == 0:
                            pe.wait_ge(q.w_lo, h * 8 + (32 + j + 1))
                        o = ps[:, n % 6, :]
                        mm(o, A_hi[:, t, k, :], wh, k == 0, False)
                        mm(o, A_hi[:, t, k, :], wl, False, False)
                        last = mm(o, A_lo[:, t, k, :], wh, False, k == KT - 1)
                    last.then_inc(q.q_ps, 1)
            q_step(0, True)
            pe.wait_ge(q.mod_ok, 4)
            pe.transpose(ps[0:32, 7, 0:P], gm1[:, :], ident[:, :]).then_inc(q.gain_t, 1)
            with pe.Fori(1, HEADS) as h:
                q_step(h, False)

            pe.wait_ge(q.qk_evac, NT * HEADS)
            pe.wait_ge(q.vg_evac, NT * HEADS)
            def turned(h, j, first=False):
                pe.wait_ge(q.r_ok, h * NT + (j + 1))
                if j < NT - 2 and not (first and j == 0):
                    pe.wait_ge(q.rT_ok, h * NT + j)
                for k in range(2):
                    last = pe.transpose(ps[:, turned_bank(j), k * P:(k + 1) * P], o_r[:, j % 2, k * P:(k + 1) * P], ident[:, :])
                last.then_inc(q.rT_ps, 1)

            def r_head(h, first):
                for c in range(NT):
                    b = 2 * (c % 2)
                    s = c % 3
                    pe.wait_ge(q.kv_lo, h * 2 * NT + (2 * c + 2))
                    if c == 0 and not first:
                        pe.wait_ge(q.ob_ok, h * NL)
                    if c == 1 and not first:
                        pe.wait_ge(q.rT_ok, h * NT - 2)
                        pe.wait_ge(q.o_ok, h * NT - 1)
                    if c >= 2:
                        pe.wait_ge(q.Sscan, h * 14 + (c - 1))
                    if c >= 3:
                        pe.wait_ge(q.P_evac, h * NL + (c - 2))
                    for d in range(2):
                        for k in range(2):
                            o = ps[:, b + d, k * 256:(k + 1) * 256]
                            dv = slice(d * 256, (d + 1) * 256)
                            kh, kl = k_hi[:, s, k * P:(k + 1) * P], k_lo[:, s, k * P:(k + 1) * P]
                            mm(o, kh, vs_hi[:, s, dv], True, False)
                            mm(o, kh, vs_lo[:, s, dv], False, False)
                            last = mm(o, kl, vs_hi[:, s, dv], False, True)
                    last.then_inc(q.P_ps, 1)
                    if c in (1, 2) and not first:
                        turned(h - 1, NT - 3 + c)

                def turn(j):
                    c = OUT[j]
                    pe.wait_ge(tile_in[c // 3], h * 16 + 16)
                    if not (first and j < 2):
                        pe.wait_ge(q.T_lo_ok, slot_before(h, j))
                    if j == 0 and not first:
                        pe.wait_ge(q.rT_ok, h * NT)
                    for n in range(4):
                        last = pe.transpose(ps[:, 4 + j % 2, n * P:(n + 1) * P],
                                            qkvg[:, c, n // 2, (n % 2) * P:(n % 2 + 1) * P], ident[:, :])
                    last.then_inc(q.T_ps, 1)

                def parts(x, j):
                    return [[x[:, j % 2, (2 * w + k) * P:(2 * w + k + 1) * P] for k in range(2)] for w in range(2)]

                def scores(j):
                    (qh, kh), (ql, kl) = parts(T_hi, j), parts(T_lo, j)
                    pe.wait_ge(q.T_lo_ok, h * NT + j + 1)
                    if not (first and j == 0):
                        pe.wait_ge(q.sm_ok, h * NT + j)
                    for k in range(2):
                        o = ps[:, 6, 0:P]
                        mm(o, kh[k], qh[k], k == 0, False)
                        mm(o, kh[k], ql[k], False, False)
                        last = mm(o, kl[k], qh[k], False, k == 1)
                    last.then_inc(q.sc_ps, 1)

                turn(0)
                turn(1)
                scores(0)
                for j in range(NT):
                    p = j % 2
                    if j + 1 < NT:
                        scores(j + 1)
                    if j + 2 < NT:
                        turn(j + 2)
                    if j >= 1:
                        (qh, _), (ql, _) = parts(T_hi, j), parts(T_lo, j)
                        pe.wait_ge(q.S_lo_ok, h * NL + j)
                        pe.wait_ge(q.S_lo2_ok, h * NL + j)
                        if j >= 3:
                            pe.wait_ge(q.ob_ok, h * NL + j - 2)
                        elif j == 1:
                            pe.wait_ge(q.P_evac, h * NL + NL)
                        for k in range(2):
                            o = ps[:, j % 2, :]
                            sh, sl = S_hi[:, p, k * 512:(k + 1) * 512], S_lo[:, p, k * 512:(k + 1) * 512]
                            mm(o, qh[k], sh, k == 0, False)
                            mm(o, qh[k], sl, False, False)
                            last = mm(o, ql[k], sh, False, k == 1)
                        last.then_inc(q.cr_ps, 1)
                    if j >= 2:
                        turned(h, j - 2, first)
                    pe.wait_ge(q.sm_lo_ok, h * NT + j + 1)
                    pe.wait_ge(q.v_lo_ok, h * NT + j + 1)
                    if not (first and j < 2):
                        pe.wait_ge(q.o_ok, slot_before(h, j))
                    o = ps[:, 3 if p else 7, 0:256]
                    mm(o, sm_hi[:, p, :], v_hi[:, p, :], True, False)
                    mm(o, sm_hi[:, p, :], v_lo[:, p, :], False, False)
                    mm(o, sm_lo[:, p, :], v_hi[:, p, :], False, True).then_inc(q.in_ps, 1)
            r_head(0, True)
            with pe.Fori(1, HEADS) as h:
                r_head(h, False)
            for j in (NT - 2, NT - 1):
                turned(HEADS - 1, j)

            pe.wait_ge(q.rT_ok, HEADS * NT)
            pe.wait_ge(q.o_ok, HEADS * NT)
            def tile(g, which, m):
                hi, lo = ((r_hi, r_lo), (c_hi, c_lo))[which]
                n = g * M_CHUNKS + which * 8 + m
                e = g * 16 + which * 8 + m
                pe.wait_ge(q.w_lo, N_L + n + 1)
                if e >= 2:
                    pe.wait_ge(q.mr_evac, e - 1)
                wh, wl = wslot(n, 6)
                fm3(ps[:, e % 2, 0:TG], wh, wl, lambda k: hi[:, k, :], lambda k: lo[:, k, :]).then_inc(q.mr_ps, 1)
            def ln_mean(g):
                pe.wait_ge(q.ln_s, g + 1)
                if g > 1:
                    pe.wait_ge(q.h2_f, 6 * (g - 1))
                mm(ps[:, 6, 0:TG], mean_w[:, :], ln_a[:, :], True, True).then_inc(q.ln_mp, 1)
            def ln_var(g):
                pe.wait_ge(q.ln_acck, KT * (g + 1))
                pe.wait_ge(q.ln_d, g + 1)
                mm(ps[:, 6, 0:TG], mean_w[:, :], ln_acc[:, :], True, True).then_inc(q.ln_vp, 1)
            def h2_turns(g, t):
                n = 3 * g + t
                for half in range(2):
                    pe.wait_ge(q.xn2_ok, n + 1)
                    if n:
                        pe.wait_ge(q.h2_f, 2 * n)
                    for k in range(4):
                        kk = 4 * half + k
                        last = pe.transpose(ps[:, 7 - half, k * P:(k + 1) * P], mo[:, t, kk * P:(kk + 1) * P], ident[:, :])
                    last.then_inc(q.h2_ps, 1)
            for g in range(NTG):
                pe.wait_ge(q.r_lo_ok, KT * (g + 1))
                for m in range(KT):
                    tile(g, 0, m)
                    if g == 0 and m == 1:
                        ln_mean(g)
                    if g == 0 and m == 4:
                        ln_var(g)
                pe.wait_ge(q.c_lo_ok, KT * (g + 1))
                for m in range(KT):
                    tile(g, 1, m)
                    if g and m < 3:
                        pe.wait_ge(q.ln_v, g + 1)
                        h2_turns(g - 1, m)
                for half in range(2):
                    for t in range(3):
                        n = 6 * g + 3 * half + t
                        if n >= 4:
                            pe.wait_ge(q.mo_ok, n - 3)
                        o = ps[:, 2 + n % 4, :]
                        for k in range(KT):
                            cn = g * M_CHUNKS + 16 + half * 4 + k // 2
                            if t == 0:
                                pe.wait_ge(q.w_lo, N_L + cn + 1)
                            if half == 0 and t == 0:
                                pe.wait_ge(q.m_lo_ok, KT * g + k + 1)
                            wh, wl = (x.rearrange("p (k n) -> p k n", k=2)[:, k % 2, :] for x in wslot(cn, 6))
                            tok = slice(t * P, (t + 1) * P)
                            mm(o, m_hi[:, k, tok], wh, k == 0, False)
                            mm(o, m_hi[:, k, tok], wl, False, False)
                            last = mm(o, m_lo[:, k, tok], wh, False, k == KT - 1)
                        last.then_inc(q.mo_ps, 1)
                        if g + 1 < NTG and (half, t) == (0, 1):
                            ln_mean(g + 1)
                        if g + 1 < NTG and (half, t) == (1, 1):
                            ln_var(g + 1)

            def up(i, p, kind, groups=range(NTG), first=False):
                role = 4 * p + kind
                wh, wl = W_hi[:, role, :], W_lo[:, role, :]
                pe.wait_ge(q.w_lo, N_LM + 1 + f_number(i, role))
                if not first:
                    pe.wait_ge((q.fa_ev, q.fg_ev)[kind], i * 2 + p)
                for g in groups:
                    tok = slice(g * TG, (g + 1) * TG)
                    last = fm3(ps[:, 3 * kind + g, 0:TG], wh, wl, lambda k: B_hi[:, k, tok], lambda k: B_lo[:, k, tok],
                               ready=q.B_lo_ok if first and kind == g == 0 else None)
                if NTG - 1 in groups:
                    last.then_inc((q.fa_ps, q.fg_ps)[kind], 1)
            def down(i, first=False):
                w = [(W_hi[:, role, :], W_lo[:, role, :]) for role in (2, 3)]
                pe.wait_ge(q.w_lo, N_LM + 1 + f_number(i, 3))
                pe.wait_ge(q.gact_lo, i * 2 + 2)
                for n in range(2 * NT):
                    t, half = n // 2, n % 2
                    if not (first and n < 2):
                        pe.wait_ge(q.y_add, i * 2 * NT + (n - 1))
                    o = ps[:, 6 + half, :]
                    tok, col = slice(t * P, (t + 1) * P), slice(half * 512, (half + 1) * 512)
                    for p in range(2):
                        wh, wl = w[p]
                        mm(o, g_hi[:, p, tok], wh[:, col], p == 0, False)
                        mm(o, g_hi[:, p, tok], wl[:, col], False, False)
                        last = mm(o, g_lo[:, p, tok], wh[:, col], False, p == 1)
                    last.then_inc(q.fd_ps, 1)
            pe.wait_ge(q.ln_v, NTG)
            pe.wait_ge(q.mr_evac, 16 * NTG)
            pe.wait_ge(q.mo_ok, 6 * NTG)
            up(0, 0, 0, (0,), True)
            h2_turns(NTG - 1, 0)
            up(0, 0, 0, (1,), True)
            h2_turns(NTG - 1, 1)
            up(0, 0, 1, (0,), True)
            h2_turns(NTG - 1, 2)
            up(0, 0, 1, (1,), True)
            pe.wait_ge(q.B_lo_ok, KT + 3)
            up(0, 0, 0, (2,), True)
            up(0, 0, 1, (2,), True)
            up(0, 1, 0)
            up(0, 1, 1)
            pe.wait_ge(q.h2_f, 2 * NT)
            def pair(i, first):
                up(i, 0, 0)
                up(i, 0, 1)
                down(i - 1, first)
                up(i, 1, 0)
                up(i, 1, 1)
            pair(1, True)
            with pe.Fori(2, FKT // 2) as i:
                pair(i, False)
            down(FKT // 2 - 1)

        @block.scalar
        def _(act):
            def copy(dst, src):
                return act.activation(dst, src, ACT.Copy)

            def split_w(n, per, used=None):
                act.wait_ge(wl_in[n % 4], per)
                if used is not None:
                    act.wait_ge(*used)
                copy(wslot(n, 8)[0], wraw(n, 4)).then_inc(q.w_hi, 1)

            act.wait_ge(q.vec_ok, 1)
            act.activation(cs[:, :, :].rearrange("p k c -> p c k"),
                           V0[:, 0:16].rearrange("p (c k) -> p c k", c=2), ACT.Silu).then_inc(q.cs_ok, 1)
            for t in range(NT):
                act.wait_ge(x_in, 32)
                if t >= 2:
                    act.wait_ge(q.ssq_ok, t - 1)
                act.activation(hf[:, t % 2, 0:D], x_all[:, t, :], ACT.Square, accum_out=ssq[:, t:t + 1]).then_inc(q.ssq_ok, 1)
            act.wait_ge(q.rstd_a, 1)
            act.activation(ssq[:, :], rst[:, :], ACT.Sqrt).then_inc(q.rstd_b, 1)
            act.wait_ge(q.mod_ok, 2)
            for k in range(KT):
                act.wait_ge(q.hT_ps, k + 1)
                if k >= 2:
                    act.wait_ge(q.hT_lo, k - 1)
                b = 3 * (k % 2)
                h_ = hf[:, k % 2, :]
                act.activation(h_[:, 0:LAT].rearrange("p (b n) -> p b n", b=2), ps[:, b:b + 2, :], ACT.Identity,
                               bias=mod[:, SH1 * KT + k, 0:1], scale=hscale[:, k, 0:1])
                act.activation(h_[:, LAT:T], ps[:, b + 2, 0:P], ACT.Identity,
                               bias=mod[:, SH1 * KT + k, 1:2], scale=hscale[:, k, 1:2]).then_inc(q.hT_f, 1)
                if k in (3, 5):
                    split_w((k - 3) // 2, 16)
            for n in range(2, 4):
                split_w(n, 16)

            def ada_load(i, e):
                act.wait_ge(q.ada_used, i * 8 + e + 15)
                act.dma_start(ada_w[:, e % 2, :, :], ada[:, :, bass.ds(i * 1024 + (16 + e) * P, P)]).then_inc(ada_in[e % 2], 16)
            def u_step(i, e):
                s, t = U_COLS[e]
                act.wait_ge(q.u_ps, i * 8 + e + 1)
                src = ps[:, 3 * (e % 2):3 * (e % 2) + 3, 0:TG]
                v3 = lambda x: x.rearrange("p (b n) -> p b n", b=3)
                first = isinstance(i, int) and i == 0
                if s == 5:
                    if not (first and t == 0):
                        act.wait_ge(q.u_ok, i * 2 + t)
                    act.activation(v3(sig[:, :]), src, ACT.Sigmoid).then_inc(q.u_evac, 1)
                elif s == 4:
                    act.activation(v3(u_a[:, :]), src, ACT.Copy).then_inc(q.u_evac, 1)
                else:
                    if not (first and t == 0):
                        act.wait_ge(gate_st[s - 6], i * 32 + 16 * t)
                    act.activation(v3(gates[:, s - 6, :]), src, ACT.Sigmoid).then_inc(q.u_evac, 1)
                    act.wait_ge(q.u_evac, i * 8 + e + 1)
                    act.dma_start(gate_d[s - 6, bass.ds(i * 2 + t, 1)].rearrange("o p n -> (o p) n"), gates[:, s - 6, :]).then_inc(gate_st[s - 6], 16)
                if e + 2 < 8:
                    ada_load(i, e + 2)
                else:
                    if not (isinstance(i, int) and i == 3):
                        ada_load(i + 1, e - 6)
                n = e + 4
                if first and n < 8:
                    used = None
                else:
                    used = (q.u_ps, i * 8 + n - 7)
                per = (i * 32) + 16 * (n // 4 + 1)
                if isinstance(i, int) and i == 3 and n >= 8:
                    per = 16 * (8 + 0) + 32
                split_w(n, per, used)
                if e == 7:
                    act.wait_ge(q.ada_used, i * 8 + 24)
                    copy(mod[:, bass.ds(i * 8 + 16, 8), :].rearrange("p k c -> p (k c)"), ps[:, 6, 0:16]).then_inc(q.adaU_ok, 1)
            act.wait_ge(q.hT_lo, KT)
            for n in range(2):
                ada_load(0, n)
            for e in range(8):
                u_step(0, e)
            with act.Fori(1, 3) as i:
                for e in range(8):
                    u_step(i, e)
            for e in range(8):
                u_step(3, e)

            act.wait_ge(q.ada_used, 48)
            for s_ in gate_st:
                act.wait_ge(s_, 16 * KT)
            act.dma_start(rope[:, :, :, :], a["rope_table"].rearrange("t p (c n) -> p t c n", c=2)).then_inc(q.rope_in, 16)
            act.dma_start(tab[:, :], a["shape_table"]).then_inc(q.tab_in, 16)
            for n, name in enumerate(("ret_decay_fwd", "ret_decay_bwd")):
                act.dma_start(dec[:, n * HEADS:(n + 1) * HEADS], a[name].partition_broadcast(P)).then_inc(q.tab_in, 16)
            act.wait_ge(q.conv_step, CW * KT)
            for s_ in conv_st:
                act.wait_ge(s_, 16 * KT)
            act.dma_start(gn_row[:, :], a["ret_gn_w"][0].partition_broadcast(P)).then_inc(q.tab_in, 16)
            def w_q(h, n, first):
                per = h * 64 + (16 * 8 + 32 * (n // 4 + 1))
                used = (q.u_ps, 32) if (first and n < 8) else (q.q_ps, h * 18 + ((n - 4) // 4) * 9)
                split_w(n, per, used)
            def q_step(h, first, last):
                for t in range(NT):
                    if t < 4:
                        w_q(h, 4 + t, first)
                    act.wait_ge(q.rope_ok, h * NT + t + 1)
                    act.dma_start(qkvg_d[bass.ds(h, 1), t, :, 0:512].rearrange("o p n -> (o p) n"),
                                  qk_st[:, t % 3, :]).then_inc(qk_st_s[t % 3], 16)
                def vg_store(t):
                    act.wait_ge(q.vg_ok, h * NT + t + 1)
                    act.dma_start(qkvg_d[bass.ds(h, 1), t, :, 512:1024].rearrange("o p n -> (o p) n"),
                                  vg_st[:, t % 3, :]).then_inc(vg_st_s[t % 3], 16)
                for t in range(NT):
                    if t < 4 and not last:
                        w_q(h, 8 + t, False)
                    act.wait_ge(q.q_ps, h * 18 + (10 + t))
                    if not (first and t < 3):
                        act.wait_ge(vg_st_s[t % 3], h * 48 + 16 * (t // 3))
                    src = ps[:, (9 + t) % 6, :]
                    copy(vg_st[:, t % 3, 0:256], src[:, 0:256])
                    act.activation(vg_st[:, t % 3, 256:512], src[:, 256:512], ACT.Silu).then_inc(q.vg_evac, 1)
                    if t:
                        vg_store(t - 1)
                vg_store(NT - 1)
            q_step(0, True, False)
            act.wait_ge(q.dk_arg, 1)
            act.activation(lgt[:, 1, :], lgt[:, 0, :], ACT.Exp, scale=-1.0).then_inc(q.dk_exp, 1)
            act.wait_ge(q.dk_arg, 7)
            act.activation(dk_c[:, :, :], dk_a[:, :, :], ACT.Exp).then_inc(q.dk_exp, 1)
            with act.Fori(1, HEADS - 1) as h:
                q_step(h, False, False)
            act.wait_ge(q.gain_t, 1)
            copy(gmr[:, :], ps[0:32, 7, 0:P]).then_inc(q.gain_c, 1)
            q_step(HEADS - 1, False, True)

            def split_m(n):
                if n < 6:
                    act.wait_ge(q.q_ps, 18 * HEADS)
                else:
                    c = (n - 6) % M_CHUNKS
                    g = (n - 6) // M_CHUNKS
                    if c < 16:
                        act.wait_ge(q.mr_ps, g * 16 + c + 1)
                    else:
                        act.wait_ge(q.mo_ps, 6 * g + 3 * ((c - 16) // 4 + 1))
                act.wait_ge(wr_in[n % 3], 16 * (n // 3 + 1))
                copy(wslot(n, 6)[0], wraw(n, 3)).then_inc(q.w_hi, 1)

            def r_head(h, first):
                for c in range(NT):
                    s = c % 3
                    act.wait_ge(tile_in[c // 3], h * 16 + 16)
                    if c >= 3:
                        act.wait_ge(q.P_ps, h * NT + c - 2)
                    copy(k_hi[:, s, :], qkvg[:, c, 1, :]).then_inc(q.kv_hi, 1)
                    act.wait_ge(q.vs_ok, h * NT + c + 1)
                    copy(vs_hi[:, s, :], vs[:, s, :]).then_inc(q.kv_hi, 1)
                    if c >= 3:
                        state_evac(h, c - 2, first)
                    if c == 0 and not first:
                        norm_root(h - 1, NT - 1)
                    if c in (4, 5) and not first:
                        rT_out(h - 1, NT - 6 + c, False)
                    if c == 6:
                        act.wait_ge(q.hd_ok, h + 1)
                        if not first:
                            act.wait_ge(q.mask_ok, h * 2)
                        for d in range(2):
                            ins = act.activation(mtmp[:, d, :], tab[:, NPOS + d * P:NPOS + (d + 1) * P], ACT.Exp,
                                                 scale=hd[:, 6 + d:7 + d])
                        ins.then_inc(q.mexp, 1)
                state_evac(h, NL - 1, first)
                if first:
                    for s_ in qk_st_s + vg_st_s:
                        act.wait_ge(s_, 16 * 3 * HEADS)
                def T_part(j):
                    p = j % 2
                    act.wait_ge(q.T_ps, h * NT + j + 1)
                    if j >= 2:
                        act.wait_ge(q.sc_ps, h * NT + j - 1)
                        if j >= 3:
                            act.wait_ge(q.cr_ps, h * NL + j - 2)
                    copy(T_hi[:, p, :], ps[:, 4 + p, :]).then_inc(q.Tv_hi, 1)
                def vS_part(j):
                    p = j % 2
                    c = OUT[j]
                    if not (first and j < 2):
                        act.wait_ge(q.in_ps, slot_before(h, j))
                    copy(v_hi[:, p, :], qkvg[:, c, 2, :]).then_inc(q.Tv_hi, 1)
                    if c < NL:
                        if j == 1:
                            act.wait_ge(q.Sscan, h * 14 + 14)
                        if j >= 3:
                            act.wait_ge(q.cr_ps, h * NL + j - 2)
                        copy(S_hi[:, p, :].rearrange("p (k n) -> p k n", k=2), S[:, c, :, :]).then_inc(q.S_hi_ok, 1)
                def sm_part(j):
                    act.wait_ge(q.sm_ok, h * NT + j + 1)
                    if not (first and j < 2):
                        act.wait_ge(q.in_ps, slot_before(h, j))
                    copy(sm_hi[:, j % 2, :], sm[:, j % 2, :]).then_inc(q.sm_hi_ok, 1)
                T_part(0)
                T_part(1)
                vS_part(0)
                state_evac(h, NL, first)
                sm_part(0)
                for j in range(NT):
                    p = j % 2
                    if j + 1 < NT:
                        vS_part(j + 1)
                        sm_part(j + 1)
                    if j >= 1:
                        act.wait_ge(q.cr_ps, h * NL + j)
                        if j >= 3:
                            act.wait_ge(q.ob_ok, h * NL + j - 2)
                        act.activation(o_a[:, p, :], ps[:, p, 0:256], ACT.Copy, scale=hd[:, 0:1]).then_inc(q.oa_ok, 1)
                    if j + 2 < NT:
                        T_part(j + 2)
                    if j >= 1:
                        norm_root(h, j - 1)
                    if j >= 2:
                        rT_out(h, j - 2, first)

            def state_evac(h, c, first):
                b = 2 * (c % 2)
                act.wait_ge(q.P_ps, h * NT + c + 1)
                if c < NL:
                    if c == 1:
                        if not first:
                            act.wait_ge(q.S_lo_ok, h * NL)
                            act.wait_ge(q.S_lo2_ok, h * NL)
                        else:
                            act.wait_ge(q.q_ps, 18 * HEADS)
                    copy(S[:, c - 1, :, 256:512], ps[:, b + 1, :].rearrange("p (k e) -> p k e", k=2)).then_inc(q.P_evac, 1)
                else:
                    if not first:
                        act.wait_ge(q.st_f_st, h * 32)
                    copy(st_out[:, :, :, :], ps[:, b:b + 2, :].rearrange("p d (k e) -> p d k e", k=2)).then_inc(q.P_evac, 1)
                    act.wait_ge(q.P_evac, h * NL + NL)
                    for d, dst in enumerate((out_sf, out_sb)):
                        act.dma_start(dst[0, 0, bass.ds(h, 1)].rearrange("o (k p) e -> p (o k) e", p=P),
                                      st_out[:, d, :, :]).then_inc(q.st_f_st, 16)

            def norm_root(h, j):
                p = j % 2
                act.wait_ge(q.gn_v, h * NT + (j + 1))
                act.activation(gstd[:, p, 1:2], gstd[:, p, 0:1], ACT.Sqrt).then_inc(q.gn_q, 1)

            def rT_out(h, j, first):
                p = j % 2
                c = OUT[j]
                act.wait_ge(q.rT_ps, h * NT + (j + 1))
                if not (first and j < 2):
                    act.wait_ge(rT_s[p], rt_count(h, j))
                copy(rT_st[:, p, :, :].rearrange("p k n -> p (k n)"), ps[:, turned_bank(j), 0:256]).then_inc(q.rT_ok, 1)
                act.wait_ge(q.rT_ok, h * NT + (j + 1))
                act.dma_start(rT_d[bass.ds(h * 2, 2), :, c * P:(c + 1) * P].rearrange("k p n -> p k n"),
                              rT_st[:, p, :, :]).then_inc(rT_s[p], 16)

            def rt_count(h, c):
                per = 5 if c % 2 == 0 else 4
                return h * (16 * per) + 16 * (c // 2)
            act.wait_ge(q.q_ps, 18 * HEADS)
            r_head(0, True)
            with act.Fori(1, HEADS) as h:
                r_head(h, False)
            norm_root(HEADS - 1, NT - 1)
            for j in (NT - 2, NT - 1):
                rT_out(HEADS - 1, j, False)
            for n in range(3):
                split_m(n)

            act.wait_ge(q.mem_free, 1)

            def rc_load(g, which):
                if which:
                    act.wait_ge(q.r_lo_ok, KT * (g + 1))
                elif g:
                    act.wait_ge(q.c_lo_ok, KT * g)
                src = (rT_d, conv_d)[which][:, :, g * TG:(g + 1) * TG]
                act.dma_start(rc_st[:, :, :], src.rearrange("k p n -> p k n")).then_inc(q.rc_in, 16)
            def gate_load(e):
                if e >= 16 * NTG or e % 2:
                    return
                g, w, m = e // 16, (e // 8) % 2, e % 8
                if e >= 4:
                    act.wait_ge(q.mr_evac, e - 2)
                act.dma_start(gate_t[:, e % 4:e % 4 + 2, :],
                              gate_d[w, m:m + 2, :, g * TG:(g + 1) * TG].rearrange("m p n -> p m n")).then_inc(gt_in[(e // 2) % 2], 16)
            def r_hi_part(g):
                act.wait_ge(q.rc_in, 32 * g if g else 16)
                if g:
                    act.wait_ge(q.mr_ps, 16 * (g - 1) + 8)
                for k in range(KT):
                    copy(r_hi[:, k, :], rc_st[:, k, :]).then_inc(q.r_hi_ok, 1)
            def squares(g):
                act.wait_ge(q.ln_d, g + 1)
                for k in range(KT):
                    n = g * KT + k
                    if n >= 2:
                        act.wait_ge(q.ln_acck, n - 1)
                    act.activation(ln_sq[:, n % 2, :], conv_src(g)[:, k, :], ACT.Square).then_inc(q.ln_sqk, 1)
            def silus(g):
                act.wait_ge(q.ln_z, g + 1)
                for k in range(KT):
                    act.activation(conv_src(g)[:, k, :], conv_src(g)[:, k, :], ACT.Silu, bias=V0[:, V_LNB + k:V_LNB + k + 1],
                                   scale=V0[:, V_LNW + k:V_LNW + k + 1]).then_inc(q.ln_silu, 1)
            def xt_load(g):
                if g:
                    act.wait_ge(q.xt_st, 48 * g)
                    act.wait_ge(q.xn2_ok, 3 * g)
                if g < NTG - 1:
                    act.dma_start(xt[:, :, :], a["x_sample"][0, g * TG:(g + 1) * TG, :].rearrange("(t p) d -> p t d", p=P)).then_inc(q.xt_in, 16)
                else:
                    act.dma_start(xt[:, 0:2, :], a["x_sample"][0, g * TG:LAT, :].rearrange("(t p) d -> p t d", p=P)).then_inc(q.xt_in, 16)
                    act.dma_start(xt[:, 2, :], a["x_prompt"][0]).then_inc(q.xt_in, 16)
            def tail_step(g, m):
                if 0 <= m - 3 < 3:
                    t = m - 3
                    act.wait_ge(q.mst_v, 6 * g + SECOND[t])
                    act.activation(mst[:, t, 6:7], mst[:, t, 5:6], ACT.Sqrt).then_inc(q.mst_q, 1)
                if 0 <= m - 2 < 3:
                    t = m - 2
                    act.wait_ge(q.x2_ok, 3 * g + t + 1)
                    act.dma_start(x2_d[3 * g + t], xt[:, t, :]).then_inc(q.xt_st, 16)
                    act.wait_ge(q.mst_s, 6 * g + SECOND[t] - 1)
                    act.activation(sq_junk[:, :], xt[:, t, :], ACT.Square, accum_out=mst[:, t, 4:5]).then_inc(q.mst_s, 1)
                if 0 <= m - 1 < 3:
                    t = m - 1
                    act.wait_ge(q.mst_v, 6 * g + FIRST[t])
                    act.activation(mst[:, t, 2:3], mst[:, t, 1:2], ACT.Sqrt).then_inc(q.mst_q, 1)
                if m < 3:
                    t = m
                    act.wait_ge(q.mo_ok, 6 * g + 4 + t)
                    if g or t:
                        act.wait_ge(q.mst_s, 6 * g + FIRST[t] - 1)
                    act.activation(sq_junk[:, :], mo[:, t, :], ACT.Square, accum_out=mst[:, t, 0:1]).then_inc(q.mst_s, 1)
            def h2_out(g, t):
                n = 3 * g + t
                cond = 0 if n < NL else 1
                act.wait_ge(q.xn2_ok, n + 1)
                if 0 < n < 3 * NTG - 2:
                    act.wait_ge(q.h2_st, 16 * n)
                elif n:
                    act.wait_ge(q.B_lo_ok, KT + t)
                for half in range(2):
                    act.wait_ge(q.h2_ps, 2 * n + half + 1)
                    for k in range(4):
                        kk = 4 * half + k
                        ins = act.activation(h2o[:, kk, :], ps[:, 7 - half, k * P:(k + 1) * P], ACT.Identity,
                                             bias=mod[:, SH2 * KT + kk, cond:cond + 1], scale=h2s[:, kk, cond:cond + 1])
                    ins.then_inc(q.h2_f, 1)
                act.wait_ge(q.h2_f, 2 * n + 2)
                if g < NTG - 1:
                    act.dma_start(h2T_d[:, :, n * P:(n + 1) * P].rearrange("k p n -> p k n"), h2o[:, :, :]).then_inc(q.h2_st, 16)
                else:
                    copy(B_hi[:, :, n * P:(n + 1) * P], h2o[:, :, :]).then_inc(q.B_hi_ok, 1)

            split_to = [3]
            def more_w(upto):
                while split_to[0] < min(upto, 3 * M_CHUNKS):
                    split_m(split_to[0])
                    split_to[0] += 1
            r_hi_part(0)
            for e in range(4):
                gate_load(e)
            def ln_root(g):
                act.wait_ge(q.ln_v, g + 1)
                act.activation(ln_a[:, :], ln_acc[:, :], ACT.Sqrt).then_inc(q.ln_r1, 1)
            def B_part():
                act.wait_ge(q.rc_in, 32 * NTG)
                for k in range(KT):
                    copy(B_hi[:, k, 0:2 * TG], h2_in[:, k, :]).then_inc(q.B_hi_ok, 1)
            def split_f(i, role, used=None):
                if used is not None:
                    act.wait_ge(*used)
                slot = f_raw(i, role)
                act.wait_ge(wr_in[slot], (f_loads(i, role) + NTG * M_CHUNKS // 3) * 16)
                copy(W_hi[:, role, :], W_raw[:, slot, :]).then_inc(q.w_hi, 1)
            for g in range(NTG):
                for m in range(KT):
                    e = g * 16 + m
                    act.wait_ge(q.mr_evac, e + 1)
                    gate_load(e + 3)
                    more_w(g * M_CHUNKS + m + 7)
                    if g == 0 and m == 2:
                        squares(g)
                    if g == 0 and m == 4:
                        ln_root(g)
                    if g == 0 and m == 5:
                        silus(g)
                    if g and m < 6:
                        tail_step(g - 1, m)
                for m in range(KT):
                    e = g * 16 + 8 + m
                    act.wait_ge(q.mr_evac, e + 1)
                    if g and m == 0:
                        act.wait_ge(q.mo_ps, 6 * g)
                    copy(m_hi[:, m, :], m_part[:, m, :]).then_inc(q.m_hi_ok, 1)
                    gate_load(e + 3)
                    more_w(g * M_CHUNKS + 8 + m + 7)
                    if g and m < 3:
                        h2_out(g - 1, m)
                    if m == 1 and g + 1 < NTG:
                        rc_load(g + 1, 0)
                    if m == 4 and g + 1 < NTG:
                        r_hi_part(g + 1)
                    if m == 6 and g + 1 < NTG:
                        rc_load(g + 1, 1)
                xt_load(g)
                for n in range(6):
                    half, t = n // 3, n % 3
                    act.wait_ge(q.mo_ps, 6 * g + n + 1)
                    if g:
                        act.wait_ge(q.h2_ps, 6 * g)
                    copy(mo[:, t, half * 512:(half + 1) * 512], ps[:, 2 + (6 * g + n) % 4, :]).then_inc(q.mo_ok, 1)
                    if n == 2:
                        more_w(g * M_CHUNKS + 26)
                    if g + 1 < NTG and n == 2:
                        squares(g + 1)
                    if g + 1 < NTG and n == 4:
                        ln_root(g + 1)
                    if g == NTG - 1 and n >= 3:
                        tail_step(g, n - 3)
                    if g == NTG - 1 and n == 3:
                        split_f(0, 0, (q.mo_ps, 6 * g + 3))
                    if g == NTG - 1 and n == 4:
                        B_part()
                if g + 1 < NTG:
                    more_w(g * M_CHUNKS + 28)
                    silus(g + 1)
                more_w(g * M_CHUNKS + 30)
            tail_step(NTG - 1, 3)
            split_f(0, 1)
            tail_step(NTG - 1, 4)
            h2_out(NTG - 1, 0)
            tail_step(NTG - 1, 5)
            h2_out(NTG - 1, 1)
            h2_out(NTG - 1, 2)
            split_f(0, 4, (q.mo_ps, 6 * NTG))
            split_f(0, 5)

            def f_step(i, p, first=False):
                for kind in range(2):
                    ev, c0, cv = ((q.fa_ev, q.fa_c0, q.fa_c), (q.fg_ev, q.fg_c0, q.fg_c))[kind]
                    act.wait_ge((q.fa_ps, q.fg_ps)[kind], i * 2 + p + 1)
                    if not first:
                        act.wait_ge(cv, i * 4 + 2 * p)
                    b = 3 * kind
                    copy(f_in[:, kind, 1:1 + 2 * TG].rearrange("p (b n) -> p b n", b=2), ps[:, b:b + 2, 0:TG])
                    copy(f_in[:, kind, 1 + 2 * TG:1 + LAT], ps[:, b + 2, 0:LAT - 2 * TG])
                    copy(f_in[:, kind, 2 + LAT:2 + T], ps[:, b + 2, LAT - 2 * TG:TG]).then_inc(ev, 1)
                    act.wait_ge(ev, i * 2 + p + 1)
                    if not first:
                        act.wait_ge((q.gact_lo, q.fprod)[kind], i * 2 + p)
                    act.activation(f_cv[:, kind, :], f_in[:, kind, 1:1 + F_OUT], ACT.Identity,
                                   bias=VF[:, bass.ds(i * 2 + (6 * FKT + kind * FKT + p), 1)],
                                   scale=VF[:, bass.ds(i * 2 + (2 * FKT + kind * FKT + p), 1)]).then_inc(c0, 1)
                    if kind == 0:
                        act.wait_ge(q.fa_c, i * 4 + (2 * p + 2))
                        act.activation(f_cv[:, 0, :], f_cv[:, 0, :], ACT.Silu).then_inc(q.fsilu, 1)
            def f_hi(i, p, first):
                act.wait_ge(q.fprod, i * 2 + p + 1)
                if not first:
                    act.wait_ge(q.fd_ps, i * 2 * NT)
                for d0, s0, n_ in ((0, 0, LAT), (LAT, LAT + 1, CTX)):
                    ins = copy(g_hi[:, p, d0:d0 + n_], f_cv[:, 0, s0:s0 + n_])
                ins.then_inc(q.gact_hi, 1)
            def f_pair(i, first, last):
                f_step(i, 0, first)
                if not last:
                    split_f(i + 1, 0, (q.fa_ps, i * 2 + 1))
                    split_f(i + 1, 1, (q.fg_ps, i * 2 + 1))
                for role in (2, 3):
                    split_f(i, role, None if first else (q.fd_ps, i * 2 * NT))
                f_hi(i, 0, first)
                f_step(i, 1)
                if not last:
                    split_f(i + 1, 4, (q.fa_ps, i * 2 + 2))
                    split_f(i + 1, 5, (q.fg_ps, i * 2 + 2))
                f_hi(i, 1, first)
            act.wait_ge(q.mem_free, 2)
            act.wait_ge(q.fpad, 1)
            f_pair(0, True, False)
            with act.Fori(1, FKT // 2 - 1) as i:
                f_pair(i, False, False)
            f_pair(FKT // 2 - 1, False, True)

            act.wait_ge(q.fg_ps, FKT)
            act.wait_ge(q.fd_ps, 2 * NT * (FKT // 2 - 1))
            for t in range(NT):
                act.wait_ge(q.y_add, 2 * NT * (FKT // 2 - 1) + 2 * t + 2)
                if t:
                    act.wait_ge(q.e_s, t)
                act.activation(ej[:, :], y_acc[:, t, :], ACT.Square, accum_out=est[:, t, 0:1]).then_inc(q.e_s, 1)
                if t:
                    act.wait_ge(q.e_v, t)
                    act.activation(est[:, t - 1, 2:3], est[:, t - 1, 1:2], ACT.Sqrt).then_inc(q.e_q, 1)
            act.wait_ge(q.e_v, NT)
            act.activation(est[:, NT - 1, 2:3], est[:, NT - 1, 1:2], ACT.Sqrt).then_inc(q.e_q, 1)

        @block.gpsimd
        def _(pool):
            def sub(dst, x, hi):
                return pool.tensor_tensor(dst, x, Fv(hi), ALU.subtract)

            pool.memset(ident[:, :], 0.0).then_inc(q.ident_ok, 1)
            pool.memset(mean_w[:, :], 1.0 / D).then_inc(q.ident_ok, 1)
            pool.wait_ge(q.ident_ok, 2)
            pool.affine_select(out=ident[:, :], in_=ident[:, :], compare_op=ALU.not_equal, fill=1.0, base=0,
                               pattern=[[-1, P]], channel_multiplier=1).then_inc(q.ident_ok, 1)

            def lo_w(n, ring, rawring, count):
                pool.wait_ge(q.w_hi, count)
                h_, l_ = wslot(n, ring)
                sub(l_, wraw(n, rawring), h_).then_inc(q.w_lo, 1)

            for n in range(4):
                lo_w(n, 8, 4, n + 1)
            pool.wait_ge(q.hT_lo, KT)
            pool.memset(u_in[:, :, :], 0.0).then_inc(q.pads_ok, 1)
            pool.wait_ge(q.pads_ok, 1)
            def conv_store(i, t):
                for c0, y0, n in ((0, 0, LAT), (LAT, LAT + HALO, CTX)):
                    pool.dma_start(conv_d[bass.ds(i * 2 + t, 1), :, c0:c0 + n].rearrange("o p n -> (o p) n"),
                                   conv_y[:, t, y0:y0 + n]).then_inc(conv_st[t], 16)
            def u_step(i, e):
                s, t = U_COLS[e]
                if s == 4:
                    pool.wait_ge(q.u_evac, i * 8 + e + 1)
                    if not (isinstance(i, int) and i == 0):
                        pool.wait_ge(q.conv_step, i * 2 * CW + (t - 1) * CW)
                    pool.tensor_tensor(u_in[:, t, HALO:HALO + LAT], u_a[:, 0:LAT], sig[:, 0:LAT], ALU.mult)
                    pool.tensor_tensor(u_in[:, t, 2 * HALO + LAT:2 * HALO + T], u_a[:, LAT:T], sig[:, LAT:T],
                                       ALU.mult).then_inc(q.u_ok, 1)
                    if not (isinstance(i, int) and i == 0):
                        conv_store(i - 1, t)
                lo_w(e + 4, 8, 4, i * 8 + (e + 5))
            for e in range(8):
                u_step(0, e)
            with pool.Fori(1, 4) as i:
                for e in range(8):
                    u_step(i, e)
            for t in range(2):
                pool.wait_ge(q.conv_step, CW * (KT - 1 + t))
                conv_store(3, t)
            pool.wait_ge(q.tab_in, 64)
            def q_step(h, first, last):
                if not first:
                    pool.wait_ge(q.vg_ok, h * NT)
                for t in range(4):
                    lo_w(4 + t, 8, 4, h * 8 + (32 + 4 + t + 1))
                    if t == 0:
                        pool.tensor_copy(gn_head[:, :], gn_row[:, bass.ds(h * 256, 256)]).then_inc(q.gnh_ok, 1)
                pool.wait_ge(q.gnh_ok, h + 1)
                for t in range(NT):
                    if t < 4 and not last:
                        lo_w(8 + t, 8, 4, h * 8 + (32 + 8 + t + 1))
                    pool.wait_ge(q.vg_evac, h * NT + (t + 1))
                    g_ = vg_st[:, t % 3, 256:512]
                    pool.tensor_tensor(g_, g_, gn_head[:, :], ALU.mult).then_inc(q.vg_ok, 1)
            q_step(0, True, False)
            with pool.Fori(1, HEADS - 1) as h:
                q_step(h, False, False)
            q_step(HEADS - 1, False, True)

            pool.wait_ge(q.q_ps, 18 * HEADS)
            def gated(h, j, first=False):
                pool.wait_ge(q.y_ok, h * NT + (j + 1))
                if not (first and j < 2):
                    pool.wait_ge(q.rT_ps, slot_before(h, j))
                pool.tensor_tensor(o_r[:, j % 2, :], o_y[:, j % 2, :], qkvg[:, OUT[j], 3, :], ALU.mult).then_inc(q.r_ok, 1)
            def r_head(h, first):
                for c in range(NT):
                    s = c % 3
                    pool.wait_ge(q.kv_hi, h * 2 * NT + (2 * c + 1))
                    sub(k_lo[:, s, :], qkvg[:, c, 1, :], k_hi[:, s, :]).then_inc(q.kv_lo, 1)
                    pool.wait_ge(q.kv_hi, h * 2 * NT + (2 * c + 2))
                    sub(vs_lo[:, s, :], vs[:, s, :], vs_hi[:, s, :]).then_inc(q.kv_lo, 1)
                    if c == 1 and not first:
                        gated(h - 1, NT - 1)
                if first:
                    for s_ in qk_st_s + vg_st_s:
                        pool.wait_ge(s_, 16 * 3 * HEADS)
                def vS_part(j):
                    p = j % 2
                    c = OUT[j]
                    pool.wait_ge(q.Tv_hi, h * 2 * NT + v_number(j))
                    sub(v_lo[:, p, :], qkvg[:, c, 2, :], v_hi[:, p, :]).then_inc(q.v_lo_ok, 1)
                    if c < NL:
                        pool.wait_ge(q.S_hi_ok, h * NL + j)
                        sub(S_lo[:, p, 0:512], S[:, c, 0, :], S_hi[:, p, 0:512]).then_inc(q.S_lo_ok, 1)
                def sm_part(j):
                    pool.wait_ge(q.sm_hi_ok, h * NT + j + 1)
                    sub(sm_lo[:, j % 2, :], sm[:, j % 2, :], sm_hi[:, j % 2, :]).then_inc(q.sm_lo_ok, 1)
                vS_part(0)
                sm_part(0)
                for j in range(NT):
                    if j + 1 < NT:
                        vS_part(j + 1)
                        sm_part(j + 1)
                    if j >= 1:
                        gated(h, j - 1, first)
            r_head(0, True)
            with pool.Fori(1, HEADS) as h:
                r_head(h, False)
            gated(HEADS - 1, NT - 1)

            split_to = [0]
            def more_w(upto):
                while split_to[0] < min(upto, 3 * M_CHUNKS):
                    n = split_to[0]
                    lo_w(n, 6, 3, N_L + n + 1)
                    split_to[0] += 1
            for g in range(NTG):
                for m in range(KT):
                    more_w(g * M_CHUNKS + m + 7)
                for m in range(KT):
                    pool.wait_ge(q.m_hi_ok, g * KT + m + 1)
                    sub(m_lo[:, m, :], m_part[:, m, :], m_hi[:, m, :]).then_inc(q.m_lo_ok, 1)
                    more_w(g * M_CHUNKS + 8 + m + 7)
                more_w(g * M_CHUNKS + 30)

            def lo_f(i, role):
                pool.wait_ge(q.w_hi, N_LM + 1 + f_number(i, role))
                sub(W_lo[:, role, :], W_raw[:, f_raw(i, role), :], W_hi[:, role, :]).then_inc(q.w_lo, 1)
            for role in (0, 1, 4, 5):
                lo_f(0, role)
            pool.wait_ge(q.mem_free, 2)
            pool.memset(f_in[:, :, :], 0.0).then_inc(q.fpad, 1)
            for t in range(NT):
                ins = pool.memset(y_acc[:, t, :], 0.0)
            ins.then_inc(q.fpad, 1)
            def product(i, p):
                pool.wait_ge(q.fg_c, i * 4 + (2 * p + 2))
                pool.wait_ge(q.fsilu, i * 2 + p + 1)
                pool.tensor_tensor(f_cv[:, 0, :], f_cv[:, 0, :], f_cv[:, 1, :], ALU.mult).then_inc(q.fprod, 1)
            def product_lo(i, p):
                pool.wait_ge(q.gact_hi, i * 2 + p + 1)
                for d0, s0, n_ in ((0, 0, LAT), (LAT, LAT + 1, CTX)):
                    ins = sub(g_lo[:, p, d0:d0 + n_], f_cv[:, 0, s0:s0 + n_], g_hi[:, p, d0:d0 + n_])
                ins.then_inc(q.gact_lo, 1)
            def f_pair(i, last):
                product(i, 0)
                if not last:
                    lo_f(i + 1, 0)
                    lo_f(i + 1, 1)
                for role in (2, 3):
                    lo_f(i, role)
                product_lo(i, 0)
                product(i, 1)
                if not last:
                    lo_f(i + 1, 4)
                    lo_f(i + 1, 5)
                product_lo(i, 1)
            f_pair(0, False)
            with pool.Fori(1, FKT // 2 - 1) as i:
                f_pair(i, False)
            f_pair(FKT // 2 - 1, True)

        @block.vector
        def _(dve):
            steps = [0]
            def then(ins):
                steps[0] += 1
                ins.then_inc(q.dve_own, 1)
                dve.wait_ge(q.dve_own, steps[0])

            for n, (dst, src) in enumerate(((V0[:, 0:120], ps[:, 7, 0:120]), (VF[:, 0:88], ps[:, 5, 0:88]),
                                            (VF[:, 88:176], ps[:, 5, 128:216]), (VC[:, 0:124], ps[:, 4, 0:124]),
                                            (VC[:, 124:248], ps[:, 4, 128:252]))):
                dve.wait_ge(q.vecT, 5)
                dve.tensor_copy(dst, src).then_inc(q.vec_ok, 1)
            dve.wait_ge(q.ssq_ok, NT)
            dve.tensor_scalar(rst[:, :], ssq[:, :], 1.0 / D, EPS, ALU.mult, ALU.add).then_inc(q.rstd_a, 1)
            dve.wait_ge(q.rstd_b, 1)
            then(dve.reciprocal(rst[:, :], ssq[:, :]))
            for t in range(NT):
                dve.tensor_scalar(x_all[:, t, :], x_all[:, t, :], rst[:, t:t + 1], None, ALU.mult).then_inc(q.xn_ok, 1)
            def col2(c, n):
                return V0[:, c:c + n].unsqueeze(2).broadcast_to([P, n, 2])
            dve.wait_ge(q.ada_rows, 1)
            dve.tensor_copy(mod_row[:, :].rearrange("c (b n) -> c b n", b=4), ps[0:2, 0:4, :]).then_inc(q.vec_ok, 1)
            dve.wait_ge(q.ada_used, 16)
            dve.wait_ge(q.vec_ok, 1)
            dve.tensor_tensor(mod[:, 0:16, :], ps[:, 6, 0:32].rearrange("p (k c) -> p k c", c=2), col2(V_ADAB, 16),
                              ALU.add).then_inc(q.mod_ok, 1)
            dve.wait_ge(q.mod_ok, 1)
            dve.scalar_tensor_tensor(out=hscale[:, :, :], in0=mod[:, SC1 * KT:SC1 * KT + KT, :], scalar=1.0,
                                     in1=col2(V_N1PRE, KT), op0=ALU.add, op1=ALU.mult).then_inc(q.mod_ok, 1)
            for k in range(KT):
                dve.wait_ge(q.hT_f, k + 1)
                h_ = hf[:, k % 2, :].rearrange("p (t n) -> p t n", n=P)
                then(dve.tensor_copy(A_hi[:, :, k, :], h_))
                dve.tensor_tensor(A_lo[:, :, k, :], h_, Fv(A_hi[:, :, k, :]), ALU.subtract).then_inc(q.hT_lo, 1)

            def conv(i, t):
                first = isinstance(i, int)
                dve.wait_ge(q.u_ok, i * 2 + t + 1)
                if not first:
                    dve.wait_ge(conv_st[t], i * 32)
                y = conv_y[:, t, :]
                for w in range(CW):
                    tap = VC[:, bass.ds(i * 2 + (w * KT + t), 1)]
                    x = u_in[:, t, w:w + U_OUT]
                    if w == 0:
                        dve.tensor_scalar(y, x, tap, V0[:, bass.ds(i * 2 + (V_CDB + t), 1)], ALU.mult, ALU.add).then_inc(q.conv_step, 1)
                    else:
                        dve.wait_ge(q.conv_step, i * 2 * CW + (t * CW + w))
                        dve.scalar_tensor_tensor(out=y, in0=x, scalar=tap, in1=y, op0=ALU.mult, op1=ALU.add).then_inc(q.conv_step, 1)
            for t in range(2):
                conv(0, t)
            with dve.Fori(1, 4) as i:
                for t in range(2):
                    conv(i, t)

            dve.wait_ge(q.rope_in, 16)
            for s_ in conv_st:
                dve.wait_ge(s_, 16 * KT)
            dve.wait_ge(q.adaU_ok, 4)
            dve.tensor_tensor(mod[:, 16:48, :], mod[:, 16:48, :], col2(V_ADAB + 16, 32), ALU.add).then_inc(q.mod_ok, 1)
            dve.wait_ge(q.mod_ok, 3)
            for n, (g_, v) in enumerate(((G1, V_N1POST), (G2, V_N2POST))):
                for c in range(2):
                    ins = dve.tensor_tensor(gm1[:, (2 * n + c) * KT:(2 * n + c + 1) * KT], mod[:, g_ * KT:(g_ + 1) * KT, c],
                                            V0[:, v:v + KT], ALU.mult)
            ins.then_inc(q.mod_ok, 1)
            def q_step(h, first):
                for t in range(NT):
                    src = ps[:, t % 6, :]
                    dst = qk_st[:, t % 3, :]
                    dve.wait_ge(q.q_ps, h * 18 + (t + 1))
                    if not (first and t == 0):
                        dve.wait_ge(q.rope_ok, h * NT + t)
                    if t < NL:
                        q2 = lambda x: x.rearrange("p (s n) -> p s n", s=2)
                        dve.tensor_tensor(q2(rope_c[:, :]), q2(src), rope[:, t, 0, :].unsqueeze(1).broadcast_to([P, 2, 256]), ALU.mult)
                        parts = lambda x: x.rearrange("p (s h a f) -> p s h a f", s=2, h=2, a=2)
                        sn = rope[:, t, 1, :].rearrange("p (h a f) -> p h a f", h=2, a=2)
                        for a_ in range(2):
                            for s_ in range(2):
                                ins = dve.tensor_tensor(parts(rope_s[:, :])[:, s_, :, a_, :], parts(src)[:, s_, :, 1 - a_, :],
                                                        sn[:, :, a_, :], ALU.mult)
                        ins.then_inc(q.qk_evac, 1)
                        dve.wait_ge(q.qk_evac, h * NT + (t + 1))
                        if not (first and t < 3):
                            dve.wait_ge(qk_st_s[t % 3], h * 48 + 16 * (t // 3))
                        dve.tensor_tensor(dst, rope_c[:, :], rope_s[:, :], ALU.add).then_inc(q.rope_ok, 1)
                    else:
                        dve.tensor_copy(rope_c[:, :], src).then_inc(q.qk_evac, 1)
                        dve.wait_ge(q.qk_evac, h * NT + (t + 1))
                        if not (first and t < 3):
                            dve.wait_ge(qk_st_s[t % 3], h * 48 + 16 * (t // 3))
                        dve.tensor_copy(dst, rope_c[:, :]).then_inc(q.rope_ok, 1)
            q_step(0, True)
            dve.wait_ge(q.tab_in, 64)
            dve.scalar_tensor_tensor(out=lgt[:, 0, :], in0=dec[:, :], scalar=-1.0, in1=dec[:, :],
                                     op0=ALU.mult, op1=ALU.max).then_inc(q.dk_arg, 1)
            dve.wait_ge(q.dk_exp, 1)
            e_, d_, z_, zz, p_ = (lgt[:, n, :] for n in range(1, 6))
            then(dve.tensor_scalar(d_, e_, 2.0, None, ALU.add))
            then(dve.reciprocal(z_, d_))
            then(dve.tensor_tensor(z_, z_, e_, ALU.mult))
            then(dve.tensor_tensor(zz, z_, z_, ALU.mult))
            then(dve.tensor_scalar(p_, zz, 1.0 / 15, None, ALU.mult))
            for m in (13, 11, 9, 7, 5, 3):
                then(dve.scalar_tensor_tensor(out=p_, in0=p_, scalar=1.0 / m, in1=zz, op0=ALU.add, op1=ALU.mult))
            then(dve.scalar_tensor_tensor(out=p_, in0=p_, scalar=1.0, in1=z_, op0=ALU.add, op1=ALU.mult))
            then(dve.tensor_scalar(p_, p_, 2.0, None, ALU.mult))
            then(dve.scalar_tensor_tensor(out=lg[:, :], in0=dec[:, :], scalar=0.0, in1=p_, op0=ALU.min, op1=ALU.subtract))
            for n in range(4):
                dve.tensor_scalar(dk_a[:, :, n], lg[:, (n % 2) * HEADS:(n % 2 + 1) * HEADS], tab[:, n:n + 1], None,
                                  ALU.mult).then_inc(q.dk_arg, 1)
            for n in range(2):
                dve.tensor_scalar(dk_a[:, :, 4 + n], lg[:, n * HEADS:(n + 1) * HEADS], float(P), None,
                                  ALU.mult).then_inc(q.dk_arg, 1)
            dve.wait_ge(q.dk_exp, 2)
            then(dve.tensor_scalar(dkt[:, :, 0:2], dk_c[:, :, 0:2], DK ** -0.5, None, ALU.mult))
            then(dve.tensor_copy(dkt[:, :, 2:6], dk_c[:, :, 2:6]))
            then(dve.tensor_copy(dkt[:, :, 6:8], lg[:, :].rearrange("p (d h) -> p h d", d=2)))
            with dve.Fori(1, HEADS) as h:
                q_step(h, False)

            dve.wait_ge(q.q_ps, 18 * HEADS)
            def fwd(h, c, first):
                dve.wait_ge(q.P_ps, h * NT + c + 1)
                if c == 0:
                    dve.wait_ge(q.s0f_in, h * 16 + 16)
                    if not first:
                        dve.wait_ge(q.S_lo_ok, h * NL)
                        dve.wait_ge(q.S_lo2_ok, h * NL)
                else:
                    dve.wait_ge(q.Sscan, h * 14 + c)
                dve.scalar_tensor_tensor(out=S[:, c + 1, :, 0:256], in0=S[:, c, :, 0:256], scalar=hd[:, 4:5],
                                         in1=ps[:, 2 * (c % 2), :].rearrange("p (k e) -> p k e", k=2), op0=ALU.mult, op1=ALU.add).then_inc(q.Sscan, 1)
            def finish(h, j, first=False):
                p = j % 2
                dve.wait_ge(q.gn_q, h * NT + (j + 1))
                dve.reciprocal(gstd[:, p, 2:3], gstd[:, p, 1:2]).then_inc(q.gn_r, 1)
                dve.wait_ge(q.gn_r, h * NT + (j + 1))
                if not (first and j < 2):
                    dve.wait_ge(q.r_ok, slot_before(h, j))
                dve.tensor_scalar(o_y[:, p, :], o_o[:, p, :], bn2[:, p, 0:1], gstd[:, p, 2:3], ALU.subtract, ALU.mult).then_inc(q.y_ok, 1)

            def r_head(h, first):
                if not first:
                    dve.wait_ge(q.oa_ok, h * NL)
                dve.tensor_copy(hd[:, :], dkt[:, bass.ds(h, 1), :].rearrange("p o n -> p (o n)")).then_inc(q.hd_ok, 1)
                dve.wait_ge(q.hd_ok, h + 1)
                for c in range(NT):
                    s = c % 3
                    dve.wait_ge(tile_in[c // 3], h * 16 + 16)
                    if c >= 3:
                        dve.wait_ge(q.P_ps, h * NT + (c - 2))
                    dve.tensor_scalar(vs[:, s, 0:256], qkvg[:, c, 2, :], hd[:, 2:3], None, ALU.mult)
                    dve.tensor_scalar(vs[:, s, 256:512], qkvg[:, c, 2, :], hd[:, 3:4], None, ALU.mult).then_inc(q.vs_ok, 1)
                    if c >= 2 and c - 2 < NL - 1:
                        fwd(h, c - 2, first)
                    if c == 1 and not first:
                        finish(h - 1, NT - 1)
                    if c == 8:
                        dve.wait_ge(q.mexp, h + 1)
                        for d in range(2):
                            ins = dve.tensor_tensor(mtmp[:, 2 + d, :], mtmp[:, d, :], tab[:, NPOS + (2 + d) * P:NPOS + (3 + d) * P], ALU.mult)
                        ins.then_inc(q.mask_ok, 1)
                        dve.wait_ge(q.mask_ok, h * 2 + 1)
                        dve.tensor_tensor(mask[:, :], mtmp[:, 2, :], mtmp[:, 3, :], ALU.add).then_inc(q.mask_ok, 1)
                if first:
                    for s_ in qk_st_s + vg_st_s:
                        dve.wait_ge(s_, 16 * 3 * HEADS)

                def T_part(j):
                    p = j % 2
                    dve.wait_ge(q.Tv_hi, h * 2 * NT + T_number(j))
                    dve.tensor_tensor(T_lo[:, p, :], ps[:, 4 + p, :], Fv(T_hi[:, p, :]), ALU.subtract).then_inc(q.T_lo_ok, 1)
                def S_part(j):
                    p = j % 2
                    dve.wait_ge(q.S_hi_ok, h * NL + j)
                    dve.tensor_tensor(S_lo[:, p, 512:1024], S[:, OUT[j], 1, :], Fv(S_hi[:, p, 512:1024]), ALU.subtract).then_inc(q.S_lo2_ok, 1)
                def masked(j):
                    p = j % 2
                    dve.wait_ge(q.sc_ps, h * NT + j + 1)
                    if j == 0:
                        dve.wait_ge(q.mask_ok, h * 2 + 2)
                    if not (first and j < 2):
                        dve.wait_ge(q.sm_lo_ok, slot_before(h, j))
                    dve.tensor_tensor(sm[:, p, :], ps[:, 6, 0:P], mask[:, :], ALU.mult).then_inc(q.sm_ok, 1)
                def bwd(c):
                    dve.wait_ge(q.Sscan, h * 14 + (13 - c))
                    dve.scalar_tensor_tensor(out=S[:, c, :, 256:512], in0=S[:, c + 1, :, 256:512], scalar=hd[:, 5:6],
                                             in1=S[:, c, :, 256:512], op0=ALU.mult, op1=ALU.add).then_inc(q.Sscan, 1)
                dve.wait_ge(q.P_evac, h * NL + NL - 1)
                dve.wait_ge(q.s0b_in, h * 16 + 16)
                for c in (NL - 2, NL - 3):
                    bwd(c)
                T_part(0)
                bwd(NL - 4)
                T_part(1)
                for c in (NL - 5, NL - 6):
                    bwd(c)
                masked(0)
                for c in range(NL - 7, -1, -1):
                    bwd(c)
                for j in range(NT):
                    p = j % 2
                    if j + 1 < NT:
                        masked(j + 1)
                        S_part(j + 1)
                    if j >= 1:
                        dve.wait_ge(q.oa_ok, h * NL + j)
                        dve.scalar_tensor_tensor(out=o_b[:, p, :], in0=ps[:, p, 256:512], scalar=hd[:, 1:2],
                                                 in1=o_a[:, p, :], op0=ALU.mult, op1=ALU.add).then_inc(q.ob_ok, 1)
                    if j + 2 < NT:
                        T_part(j + 2)
                    if j >= 1:
                        finish(h, j - 1, first)
                    dve.wait_ge(q.in_ps, h * NT + j + 1)
                    o_ = ps[:, 3 if p else 7, 0:256]
                    if j >= 1:
                        dve.wait_ge(q.ob_ok, h * NL + j)
                        dve.tensor_tensor(o_o[:, p, :], o_, o_b[:, p, :], ALU.add).then_inc(q.o_ok, 1)
                    else:
                        dve.tensor_copy(o_o[:, p, :], o_).then_inc(q.o_ok, 1)
                    dve.wait_ge(q.o_ok, h * NT + j + 1)
                    dve.bn_stats(bn6[:, p, :], o_o[:, p, :]).then_inc(q.gn_s, 1)
                    dve.wait_ge(q.gn_s, h * 2 * NT + 2 * j + 1)
                    dve.memset(gstd[:, p, 3:4], 0.0)
                    dve.bn_aggr(bn2[:, p, :], bn6[:, p, :]).then_inc(q.gn_s, 1)
                    dve.wait_ge(q.gn_s, h * 2 * NT + 2 * j + 2)
                    dve.tensor_scalar(gstd[:, p, 0:1], bn2[:, p, 1:2], GN_EPS, None, ALU.add).then_inc(q.gn_v, 1)
            r_head(0, True)
            with dve.Fori(1, HEADS) as h:
                r_head(h, False)
            finish(HEADS - 1, NT - 1)

            dve.wait_ge(q.mem_free, 1)
            dve.scalar_tensor_tensor(out=h2s[:, :, :], in0=mod[:, SC2 * KT:SC2 * KT + KT, :], scalar=1.0,
                                     in1=col2(V_N2PRE, KT), op0=ALU.add, op1=ALU.mult)
            def r_lo_part(g):
                for k in range(KT):
                    dve.wait_ge(q.r_hi_ok, g * KT + k + 1)
                    dve.tensor_tensor(r_lo[:, k, :], rc_st[:, k, :], Fv(r_hi[:, k, :]), ALU.subtract).then_inc(q.r_lo_ok, 1)
            def over_k(x):
                return x.unsqueeze(1).broadcast_to([P, KT, TG])
            def tail_step(g, m):
                if 0 <= m - 3 < 3:
                    t = m - 3
                    dve.wait_ge(q.mst_q, 6 * g + SECOND[t])
                    then(dve.reciprocal(mst[:, t, 7:8], mst[:, t, 6:7]))
                    dve.tensor_scalar(mo[:, t, :], xt[:, t, :], mst[:, t, 7:8], None, ALU.mult).then_inc(q.xn2_ok, 1)
                if 0 <= m - 2 < 3:
                    t = m - 2
                    dve.wait_ge(q.mst_s, 6 * g + SECOND[t])
                    dve.tensor_scalar(mst[:, t, 5:6], mst[:, t, 4:5], 1.0 / D, EPS, ALU.mult, ALU.add).then_inc(q.mst_v, 1)
                if 0 <= m - 1 < 3:
                    t = m - 1
                    n = 3 * g + t
                    dve.wait_ge(q.mst_q, 6 * g + FIRST[t])
                    then(dve.reciprocal(mst[:, t, 3:4], mst[:, t, 2:3]))
                    dve.wait_ge(q.g1_in, 16 if n < NL else 32)
                    then(dve.scalar_tensor_tensor(out=mo[:, t, :], in0=mo[:, t, :], scalar=mst[:, t, 3:4], in1=g1_row[:, :],
                                                  op0=ALU.mult, op1=ALU.mult))
                    dve.wait_ge(q.xt_in, (16, 32, 64)[g])
                    dve.tensor_tensor(xt[:, t, :], xt[:, t, :], mo[:, t, :], ALU.add).then_inc(q.x2_ok, 1)
                if m < 3:
                    dve.wait_ge(q.mst_s, 6 * g + FIRST[m])
                    dve.tensor_scalar(mst[:, m, 1:2], mst[:, m, 0:1], 1.0 / D, EPS, ALU.mult, ALU.add).then_inc(q.mst_v, 1)
            def ln_sum(g):
                if g:
                    dve.wait_ge(q.rc_in, 32 * g + 16)
                else:
                    dve.wait_ge(q.c0_in, 16)
                dve.tensor_reduce(ln_a[:, :], conv_src(g)[:, :, :].rearrange("p k t -> p t k"), AX.X, ALU.add).then_inc(q.ln_s, 1)
            def ln_center(g):
                dve.wait_ge(q.ln_mp, g + 1)
                dve.tensor_tensor(conv_src(g)[:, :, :], conv_src(g)[:, :, :], over_k(ps[:, 6, 0:TG]), ALU.subtract).then_inc(q.ln_d, 1)
            def square_sum(g):
                for k in range(KT):
                    n = g * KT + k
                    dve.wait_ge(q.ln_sqk, n + 1)
                    if k:
                        dve.wait_ge(q.ln_acck, n)
                        dve.tensor_tensor(ln_acc[:, :], ln_acc[:, :], ln_sq[:, n % 2, :], ALU.add).then_inc(q.ln_acck, 1)
                    else:
                        dve.tensor_copy(ln_acc[:, :], ln_sq[:, n % 2, :]).then_inc(q.ln_acck, 1)
            def ln_variance(g):
                dve.wait_ge(q.ln_vp, g + 1)
                dve.tensor_scalar(ln_acc[:, :], ps[:, 6, 0:TG], GN_EPS, None, ALU.add).then_inc(q.ln_v, 1)
            def ln_scale(g):
                dve.wait_ge(q.ln_r1, g + 1)
                then(dve.reciprocal(ln_acc[:, :], ln_a[:, :]))
                dve.tensor_tensor(conv_src(g)[:, :, :], conv_src(g)[:, :, :], over_k(ln_acc[:, :]), ALU.mult).then_inc(q.ln_z, 1)
            def c_part(g):
                if g:
                    dve.wait_ge(q.mr_ps, 16 * g)
                for k in range(KT):
                    dve.wait_ge(q.ln_silu, g * KT + k + 1)
                    then(dve.tensor_copy(c_hi[:, k, :], conv_src(g)[:, k, :]))
                    dve.tensor_tensor(c_lo[:, k, :], conv_src(g)[:, k, :], Fv(c_hi[:, k, :]), ALU.subtract).then_inc(q.c_lo_ok, 1)
            r_lo_part(0)
            for g in range(NTG):
                for m in range(KT):
                    e = 16 * g + m
                    dve.wait_ge(q.mr_ps, e + 1)
                    dve.wait_ge(gt_in[(e // 2) % 2], 16 * (e // 4 + 1))
                    if g:
                        dve.wait_ge(q.m_lo_ok, KT * (g - 1) + m + 1)
                    dve.tensor_tensor(m_part[:, m, :], ps[:, e % 2, 0:TG], gate_t[:, e % 4, :], ALU.mult).then_inc(q.mr_evac, 1)
                    if g == 0:
                        if m == 0:
                            ln_sum(g)
                        if m == 2:
                            ln_center(g)
                            square_sum(g)
                        if m == 4:
                            ln_variance(g)
                        if m == 5:
                            ln_scale(g)
                            c_part(g)
                    elif m < 6:
                        tail_step(g - 1, m)
                for m in range(KT):
                    e = 16 * g + 8 + m
                    dve.wait_ge(q.mr_ps, e + 1)
                    dve.wait_ge(gt_in[(e // 2) % 2], 16 * (e // 4 + 1))
                    then(dve.tensor_tensor(gate_t[:, e % 4, :], ps[:, e % 2, 0:TG], gate_t[:, e % 4, :], ALU.mult))
                    dve.tensor_tensor(m_part[:, m, :], m_part[:, m, :], gate_t[:, e % 4, :], ALU.add).then_inc(q.mr_evac, 1)
                    if m == 5 and g + 1 < NTG:
                        r_lo_part(g + 1)
                if g + 1 < NTG:
                    ln_sum(g + 1)
                    ln_center(g + 1)
                    square_sum(g + 1)
                    ln_variance(g + 1)
                    ln_scale(g + 1)
                    c_part(g + 1)
            def B_part(ks):
                dve.wait_ge(q.rc_in, 32 * NTG)
                for k in ks:
                    dve.wait_ge(q.B_hi_ok, k + 1)
                    dve.tensor_tensor(B_lo[:, k, 0:2 * TG], h2_in[:, k, :], Fv(B_hi[:, k, 0:2 * TG]), ALU.subtract).then_inc(q.B_lo_ok, 1)
            for m in range(3):
                tail_step(NTG - 1, m)
            dve.wait_ge(q.mo_ps, 6 * NTG)
            B_part(range(KT))
            for m in range(3, 6):
                tail_step(NTG - 1, m)
            for t in range(3):
                tok = slice((3 * (NTG - 1) + t) * P, (3 * (NTG - 1) + t + 1) * P)
                dve.wait_ge(q.B_hi_ok, KT + t + 1)
                dve.tensor_tensor(B_lo[:, :, tok], h2o[:, :, :], Fv(B_hi[:, :, tok]), ALU.subtract).then_inc(q.B_lo_ok, 1)

            dve.wait_ge(q.fpad, 2)
            def taps(i, p, kind, which=(0, 1)):
                c0, cv = ((q.fa_c0, q.fa_c), (q.fg_c0, q.fg_c))[kind]
                if 0 in which:
                    dve.wait_ge(c0, i * 2 + p + 1)
                for n in which:
                    w = 2 * n
                    if n:
                        dve.wait_ge(cv, i * 4 + (2 * p + 1))
                    dve.scalar_tensor_tensor(out=f_cv[:, kind, :], in0=f_in[:, kind, w:w + F_OUT],
                                             scalar=VF[:, bass.ds(i * 2 + (w * 2 * FKT + kind * FKT + p), 1)],
                                             in1=f_cv[:, kind, :], op0=ALU.mult, op1=ALU.add).then_inc(cv, 1)
            def add_down(i, ns):
                for n in ns:
                    t, half = n // 2, n % 2
                    dve.wait_ge(q.fd_ps, i * 2 * NT + (n + 1))
                    y = y_acc[:, t, half * 512:(half + 1) * 512]
                    dve.tensor_tensor(y, ps[:, 6 + half, :], y, ALU.add).then_inc(q.y_add, 1)
            taps(0, 0, 0)
            taps(0, 0, 1)
            taps(0, 1, 0)
            taps(0, 1, 1)
            with dve.Fori(1, FKT // 2) as i:
                taps(i, 0, 0)
                add_down(i - 1, range(0, 3))
                taps(i, 0, 1, (0,))
                add_down(i - 1, range(3, 6))
                taps(i, 0, 1, (1,))
                add_down(i - 1, range(6, 2 * NT))
                taps(i, 1, 0)
                taps(i, 1, 1)

            def e_mean(t):
                dve.wait_ge(q.e_s, t + 1)
                dve.tensor_scalar(est[:, t, 1:2], est[:, t, 0:1], 1.0 / D, EPS, ALU.mult, ALU.add).then_inc(q.e_v, 1)
            def e_apply(t):
                cond = 0 if t < NL else 1
                dve.wait_ge(q.e_q, t + 1)
                then(dve.reciprocal(est[:, t, 3:4], est[:, t, 2:3]))
                if t == 0:
                    dve.wait_ge(q.g1_in, 64)
                then(dve.scalar_tensor_tensor(out=y_acc[:, t, :], in0=y_acc[:, t, :], scalar=est[:, t, 3:4], in1=g2_row[:, cond, :],
                                              op0=ALU.mult, op1=ALU.mult))
                dve.wait_ge(x2_in[t % 2], 16 * (t // 2 + 1))
                dve.tensor_tensor(x2t[:, t, :], x2t[:, t, :], y_acc[:, t, :], ALU.add).then_inc(q.e_o, 1)
            for t in range(NT):
                add_down(FKT // 2 - 1, (2 * t, 2 * t + 1))
                if t >= 1:
                    e_mean(t - 1)
                if t >= 2:
                    e_apply(t - 2)
            e_mean(NT - 1)
            e_apply(NT - 2)
            e_apply(NT - 1)


_INS = ["x_prompt", "x_sample", "state_ret_fwd", "state_ret_bwd", "c", "c_ctx", "norm1_pre", "norm1_post", "norm2_pre",
        "norm2_post", "ada_w", "ada_b", "w_in", "ret_decay_fwd", "ret_decay_bwd", "ret_gn_w", "ret_w_out", "conv_dw_w",
        "conv_dw_b", "conv_ln_w", "conv_ln_b", "conv_w_out", "w_mix_out", "ffn_w_up", "ffn_dw_w", "ffn_dw_b", "ffn_w_down"]
_OUTS = [(1, CTX, D), (1, LAT, D), (1, 1, HEADS, DK, DV), (1, 1, HEADS, DK, DV)]


def kernel(**inputs):
    import concourse.bacc as bacc
    from concourse.bass_utils import run_bass_kernel_spmd

    nc = bacc.Bacc("TRN2", target_bir_lowering=False, num_devices=1)
    arrays, aps = {}, {}
    rope_table, shape_table = shape_tables()
    for name, v in [(n, inputs[n]) for n in _INS] + [("rope_table", rope_table), ("shape_table", shape_table)]:
        v = np.ascontiguousarray(v)
        arrays[f"in_{name}"] = v
        aps[name] = nc.dram_tensor(f"in_{name}", v.shape, mybir.dt.from_np(v.dtype), kind="ExternalInput").ap()
    outs = [nc.dram_tensor(f"out_{i}", s, F32, kind="ExternalOutput").ap() for i, s in enumerate(_OUTS)]
    build(nc, aps, *outs)
    r = run_bass_kernel_spmd(nc, [arrays], core_ids=[0])
    return tuple(r.results[0][f"out_{i}"] for i in range(len(_OUTS)))
```
